# Optimizing a Trainium2 kernel written in Bass

```python
import jax, jax.numpy as jnp
from jax import lax
import numpy as np

D_MODEL = 1024
BATCH = 1
SEQ = 128
DEPTH = 1
DEC_BATCH = 1
DEC_SEQ = 1024
PAST_LEN = 128

GRID_W = 64
RWKV_HEADS = 8
RWKV_HEAD_DIM = 64
RWKV_WIDTH = RWKV_HEADS * RWKV_HEAD_DIM
DECAY_LORA = 64
ICLR_LORA = 64
GATE_LORA = 128
N_DIRS = 2
FOURIER_GROUPS = 4
FOURIER_GROUP_DIM = 128
FOURIER_WIDTH = FOURIER_GROUPS * FOURIER_GROUP_DIM
N_BRANCHES = 2
D_FF = 2816
N_MOD = 9
NORM_EPS = 1e-6
GN_EPS = 64e-5

OFF_WD = 3 * RWKV_WIDTH
OFF_AD = OFF_WD + N_DIRS * DECAY_LORA
OFF_GD = OFF_AD + N_DIRS * ICLR_LORA
OFF_F = OFF_GD + GATE_LORA
OFF_GATE = OFF_F + FOURIER_WIDTH
PROJ_W = OFF_GATE + N_BRANCHES * D_MODEL

kernel_name = "hybrid_rwkv7_fnet_macaron_diffusion_step"

def rmsnorm(x, w):
    xf = x.astype(jnp.float32)
    y = xf * lax.rsqrt(jnp.mean(xf * xf, axis=-1, keepdims=True) + NORM_EPS)
    return (y * w.astype(jnp.float32)).astype(x.dtype)

def swiglu(h, w13, w2):
    a, b = jnp.split(h @ w13, 2, axis=-1)
    return (jax.nn.silu(a) * b) @ w2

def short_conv(x, k):
    xp = jnp.pad(x, ((0, 0), (1, 1), (0, 0)))
    return xp[:, :-2] * k[0] + xp[:, 1:-1] * k[1] + xp[:, 2:] * k[2]

def heads(t):
    return t.reshape(t.shape[:-1] + (RWKV_HEADS, RWKV_HEAD_DIM))

def wkv_scan(r, w, k, v, kk, a, s0, reverse):
    xs = tuple(jnp.moveaxis(t, 1, 0) for t in (r, w, k, v, kk, a))

    def step(S, inp):
        r_t, w_t, k_t, v_t, kk_t, a_t = inp
        sa = jnp.einsum('bhij,bhj->bhi', S, kk_t)
        S = (S * w_t[:, :, None, :]
             - sa[..., None] * (kk_t * a_t)[:, :, None, :]
             + v_t[..., None] * k_t[:, :, None, :])
        o = jnp.einsum('bhij,bhj->bhi', S, r_t)
        return S, o

    s_final, o = lax.scan(step, s0, xs, reverse=reverse)
    return jnp.moveaxis(o, 0, 1), s_final

def fourier_mix(f, grid):
    B, T, _ = f.shape
    ff = f.astype(jnp.float32).reshape(B, T, FOURIER_GROUPS, FOURIER_GROUP_DIM)
    if grid:
        rows = T // GRID_W
        ff = ff.reshape(B, rows, GRID_W, FOURIER_GROUPS, FOURIER_GROUP_DIM)
        out = jnp.fft.fftn(ff, axes=(1, 2, 4), norm="ortho").real
    else:
        out = jnp.fft.fftn(ff, axes=(1, 3), norm="ortho").real
    return out.reshape(B, T, FOURIER_WIDTH).astype(f.dtype)

def token_mixer(h, s_fwd0, s_bwd0, grid, w_in, gate_b, conv_rkv, w0, w_up, a0, a_up, g_up,
                k_k, k_a, r_k, lnx_w, lnx_b, w_o_rwkv, w_fourier, w_out):
    B, T, _ = h.shape
    f32 = jnp.float32
    u = h @ w_in
    rkv = short_conv(u[..., :OFF_WD], conv_rkv).astype(f32)
    r, k, v = jnp.split(rkv, 3, axis=-1)
    wd = u[..., OFF_WD:OFF_AD].astype(f32).reshape(B, T, N_DIRS, DECAY_LORA)
    ad = u[..., OFF_AD:OFF_GD].astype(f32).reshape(B, T, N_DIRS, ICLR_LORA)
    gd = u[..., OFF_GD:OFF_F].astype(f32)
    f = u[..., OFF_F:OFF_GATE]
    gates = jax.nn.sigmoid(u[..., OFF_GATE:].astype(f32).reshape(B, T, N_BRANCHES, D_MODEL)
                           + gate_b.astype(f32))
    w_log = -jax.nn.softplus(-(w0.astype(f32) + jnp.einsum('btdr,drc->btdc', jnp.tanh(wd), w_up.astype(f32)))) - 0.5
    decay = heads(jnp.exp(-jnp.exp(w_log)))
    a = jax.nn.sigmoid(a0.astype(f32) + jnp.einsum('btdr,drc->btdc', ad, a_up.astype(f32)))
    g = jax.nn.sigmoid(gd) @ g_up.astype(f32)
    kk = heads(k * k_k.astype(f32))
    kk = kk / jnp.maximum(jnp.sqrt(jnp.sum(kk * kk, axis=-1, keepdims=True)), 1e-12)
    k_dir = heads(k[:, :, None] * (1.0 + (a - 1.0) * k_a.astype(f32)))
    a_h = heads(a)
    r_h, v_h = heads(r), heads(v)
    o_f, s_f = wkv_scan(r_h, decay[:, :, 0], k_dir[:, :, 0], v_h, kk, a_h[:, :, 0],
                        s_fwd0.astype(f32), False)
    o_b, s_b = wkv_scan(r_h, decay[:, :, 1], k_dir[:, :, 1], v_h, kk, a_h[:, :, 1],
                        s_bwd0.astype(f32), True)
    o = o_f + o_b
    mu = jnp.mean(o, axis=-1, keepdims=True)
    var = jnp.mean(jnp.square(o - mu), axis=-1, keepdims=True)
    o = (o - mu) * lax.rsqrt(var + GN_EPS) * heads(lnx_w.astype(f32)) + heads(lnx_b.astype(f32))
    bonus = jnp.sum(jnp.sum(r_h[:, :, None] * k_dir * r_k.astype(f32), axis=-1, keepdims=True)
                    * v_h[:, :, None], axis=2)
    o = (o + bonus).reshape(B, T, RWKV_WIDTH) * g
    y_rwkv = o.astype(h.dtype) @ w_o_rwkv
    y_four = fourier_mix(f, grid) @ w_fourier
    merged = (gates[:, :, 0] * y_rwkv + gates[:, :, 1] * y_four).astype(h.dtype)
    return merged @ w_out, s_f, s_b

def trunk_layer(x, mod, s_fwd0, s_bwd0, grid, norm_w, ffn1_w13, ffn1_w2, ffn2_w13, ffn2_w2, mixer_params):
    m = mod[:, None].astype(x.dtype)
    h = rmsnorm(x, norm_w[0]) * (1.0 + m[:, :, 1]) + m[:, :, 0]
    x = x + 0.5 * m[:, :, 2] * swiglu(h, ffn1_w13, ffn1_w2)
    h = rmsnorm(x, norm_w[1]) * (1.0 + m[:, :, 4]) + m[:, :, 3]
    y, s_f, s_b = token_mixer(h, s_fwd0, s_bwd0, grid, *mixer_params)
    x = x + m[:, :, 5] * y
    h = rmsnorm(x, norm_w[2]) * (1.0 + m[:, :, 7]) + m[:, :, 6]
    x = x + 0.5 * m[:, :, 8] * swiglu(h, ffn2_w13, ffn2_w2)
    return x, s_f, s_b

def setup_inputs(seed: int = 0) -> dict:
    key = jax.random.key(seed)
    ks = iter(jax.random.split(key, 40))
    nrm = lambda shape, s: jax.random.normal(next(ks), shape, jnp.float32) * s
    L, D = DEPTH, D_MODEL
    st_shape = (DEC_BATCH, DEPTH, RWKV_HEADS, RWKV_HEAD_DIM, RWKV_HEAD_DIM)
    conv = nrm((L, 3, 3 * RWKV_WIDTH), 0.2)
    conv = conv.at[:, 1].add(1.0)
    return {
        "x_prompt": nrm((BATCH, SEQ, D), 1.0),
        "x_sample": nrm((DEC_BATCH, DEC_SEQ, D), 1.0),
        "state_rwkv_fwd": nrm(st_shape, 0.5),
        "state_rwkv_bwd": nrm(st_shape, 0.5),
        "c": nrm((DEC_BATCH, D), 1.0),
        "c_ctx": nrm((D,), 1.0),
        "ada_w": nrm((L, D, N_MOD * D), 0.5 * D ** -0.5),
        "ada_b": nrm((L, N_MOD * D), 0.01),
        "norm_w": 1.0 + nrm((L, 3, D), 0.02),
        "ffn1_w13": nrm((L, D, 2 * D_FF), D ** -0.5),
        "ffn1_w2": nrm((L, D_FF, D), D_FF ** -0.5),
        "ffn2_w13": nrm((L, D, 2 * D_FF), D ** -0.5),
        "ffn2_w2": nrm((L, D_FF, D), D_FF ** -0.5),
        "w_in": nrm((L, D, PROJ_W), D ** -0.5),
        "gate_b": nrm((L, N_BRANCHES, D), 0.1),
        "conv_rkv": conv,
        "w0": nrm((L, N_DIRS, RWKV_WIDTH), 2.0) - 2.0,
        "w_up": nrm((L, N_DIRS, DECAY_LORA, RWKV_WIDTH), 0.5 * DECAY_LORA ** -0.5),
        "a0": nrm((L, N_DIRS, RWKV_WIDTH), 0.5),
        "a_up": nrm((L, N_DIRS, ICLR_LORA, RWKV_WIDTH), 0.5 * ICLR_LORA ** -0.5),
        "g_up": nrm((L, GATE_LORA, RWKV_WIDTH), GATE_LORA ** -0.5),
        "k_k": 0.85 + nrm((L, RWKV_WIDTH), 0.1),
        "k_a": 1.0 + nrm((L, RWKV_WIDTH), 0.1),
        "r_k": nrm((L, RWKV_HEADS, RWKV_HEAD_DIM), 0.1),
        "lnx_w": 1.0 + nrm((L, RWKV_WIDTH), 0.02),
        "lnx_b": nrm((L, RWKV_WIDTH), 0.02),
        "w_o_rwkv": nrm((L, RWKV_WIDTH, D), RWKV_WIDTH ** -0.5),
        "w_fourier": nrm((L, FOURIER_WIDTH, D), FOURIER_WIDTH ** -0.5),
        "w_out": nrm((L, D, D), D ** -0.5),
        "final_norm": 1.0 + nrm((D,), 0.02),
    }

def reference(x_prompt, x_sample, state_rwkv_fwd, state_rwkv_bwd, c, c_ctx, ada_w, ada_b, norm_w,
              ffn1_w13, ffn1_w2, ffn2_w13, ffn2_w2, w_in, gate_b, conv_rkv, w0, w_up, a0, a_up, g_up,
              k_k, k_a, r_k, lnx_w, lnx_b, w_o_rwkv, w_fourier, w_out, final_norm):
    x_p, x_s = x_prompt, x_sample
    b_p, b_s = x_prompt.shape[0], x_sample.shape[0]
    zero_state = jnp.zeros((b_p, RWKV_HEADS, RWKV_HEAD_DIM, RWKV_HEAD_DIM), jnp.float32)
    new_f, new_b = [], []
    for l in range(DEPTH):
        mixer_params = (w_in[l], gate_b[l], conv_rkv[l], w0[l], w_up[l], a0[l], a_up[l], g_up[l],
                        k_k[l], k_a[l], r_k[l], lnx_w[l], lnx_b[l], w_o_rwkv[l], w_fourier[l], w_out[l])
        ffn = (norm_w[l], ffn1_w13[l], ffn1_w2[l], ffn2_w13[l], ffn2_w2[l])
        mod_ctx = (jax.nn.silu(c_ctx) @ ada_w[l] + ada_b[l]).reshape(1, N_MOD, D_MODEL)
        x_p, s_f, s_b = trunk_layer(x_p, mod_ctx, zero_state, zero_state, False, *ffn, mixer_params)
        new_f.append(s_f)
        new_b.append(s_b)
        mod_lat = (jax.nn.silu(c) @ ada_w[l] + ada_b[l]).reshape(b_s, N_MOD, D_MODEL)
        x_s, _, _ = trunk_layer(x_s, mod_lat, state_rwkv_fwd[:, l], state_rwkv_bwd[:, l], True,
                                *ffn, mixer_params)
    y_prompt = rmsnorm(x_p, final_norm)
    y_sample = rmsnorm(x_s, final_norm)
    new_state_fwd = jnp.stack(new_f, axis=1)
    new_state_bwd = jnp.stack(new_b, axis=1)
    return (y_prompt, y_sample, new_state_fwd, new_state_bwd)


_drawn_inputs = setup_inputs


def setup_inputs(seed=0):
    import zlib

    import numpy as np

    out = dict(_drawn_inputs(seed))
    spreads = {}
    factors = {'state_rwkv_fwd': 8.0,
     'state_rwkv_bwd': 8.0,
     'gate_b': 7.455,
     'lnx_w': 8.0,
     'lnx_b': 8.0,
     'final_norm': 2.932}
    for name, (base, spread) in spreads.items():
        noise = np.random.default_rng([zlib.crc32(name.encode()), seed]).standard_normal(out[name].shape)
        drawn = base * np.exp(spread * noise) if base else spread * noise
        out[name] = __import__('jax').numpy.asarray(drawn.astype(out[name].dtype))
    for name, factor in factors.items():
        out[name] = (out[name] * factor).astype(out[name].dtype)
    return out
```

```python
from contextlib import ExitStack, contextmanager

import numpy as np

import concourse.bass as bass
from concourse import mybir

ALU = mybir.AluOpType
ACT = mybir.ActivationFunctionType
F32 = mybir.dt.float32
F32R = mybir.dt.float32r

P = 128
D = 1024
KT = D // P
T_CTX = 128
T_LAT = 1024
T = T_CTX + T_LAT
CH = 384
NC = T // CH
F_TILES = 2816 // P
HEADS, HD = 8, 64
W = HEADS * HD
CT = W // P
CK = 64
FG, FD = 4, 128
LORA = 64
NTT = T // P
NORM_EPS = 1e-6
GN_EPS = 64e-5
DECAY_SCALE = float(np.exp(-0.5))
J_WD, J_AD, J_GD, J_F, J_GATE = 12, 13, 14, 15, 19
J_END = 35

PACK = {}
_at = 0
for _name, _n in (("ada_b", 72), ("norm_w", 24), ("final_norm", 8), ("gate_b", 16), ("conv", 36),
                  ("w0", 8), ("a0", 8), ("k_k", 4), ("k_a", 4), ("r_k", 4), ("lnx_w", 4),
                  ("lnx_b", 4), ("c", 16)):
    PACK[_name] = (_at, _n)
    _at += _n
PACK_W = _at


def segments(c):
    return [(0, 0, T_CTX), (1, T_CTX, CH)] if c == 0 else [(1, 0, CH)]


class Kit:

    def __init__(self, nc, ctx, dram):
        self.nc, self.ctx, self.dram = nc, ctx, dram
        self.banks = [ctx.enter_context(nc.psum_tensor(f"bank{b}", [P, 512], F32)) for b in range(8)]
        self.x = None
        self.vec = self.resident("vec", [P, PACK_W])
        self.mod = self.resident("mod", [P, 9, KT, 2])
        self.scale = self.resident("scale", [P, 3, KT, 2])
        self.gate = self.resident("gate", [P, 3, KT, 2])
        self.ones = self.resident("ones", [P, P])
        self.eps = self.resident("eps", [P, 2])
        self.passed = nc.alloc_semaphore("passed")

    def resident(self, name, shape, dt=F32):
        return self.ctx.enter_context(self.nc.sbuf_tensor(name, shape, dt))

    def sem(self, name):
        s = self.nc.alloc_semaphore(name)
        self.stage_sems.append(s)
        return s

    @contextmanager
    def stage(self):
        self.stage_sems = []
        yield
        self.nc.clear_and_free_semaphores(self.stage_sems)
        self.nc.all_engine_barrier()

    def col(self, name, i=0, n=1):
        a = PACK[name][0]
        return self.vec[:, a + i:a + i + n]

    def hold(self, eng, sem, value):
        eng.wait_ge(sem, value)
        eng.sem_inc(self.passed, 1)


def modulation(kit):
    nc = kit.nc
    loaded_vec, loaded_x = kit.sem("vec_loaded"), kit.sem("x_loaded")
    loaded = [kit.sem(f"ada_loaded{s}") for s in range(4)]
    silu_ready, ones_ready = kit.sem("silu_ready"), kit.sem("ones_ready")
    section_done, section_added = kit.sem("section_done"), kit.sem("section_added")
    slot_free = kit.sem("ada_slot_free")
    with ExitStack() as ctx:
        raw = ctx.enter_context(nc.sbuf_tensor("ada_raw", [P, 4, 2, KT, P], F32))
        cs = ctx.enter_context(nc.sbuf_tensor("cond_silu", [P, KT, 2], F32))
        block = ctx.enter_context(nc.Block())

        @block.sync
        def _(sp):
            sp.dma_start(kit.vec[:], kit.dram["vec"]).then_inc(loaded_vec, 16)
            for s in range(4):
                sp.dma_start(raw[:, s], kit.dram["ada_w"][s]).then_inc(loaded[s], 16)
            with sp.Fori(1, 9) as i:
                for s in range(4):
                    kit.hold(sp, slot_free, i * 4 - 3 + s)
                    sp.dma_start(raw[:, s], kit.dram["ada_w"][i * 4 + s]).then_inc(loaded[s], 16)

        @block.gpsimd
        def _(pool):
            pool.memset(kit.ones[:], 1.0).then_inc(ones_ready, 1)
            pool.memset(kit.eps[:, 0:1], NORM_EPS).then_inc(ones_ready, 1)
            pool.memset(kit.eps[:, 1:2], GN_EPS).then_inc(ones_ready, 1)

        @block.scalar
        def _(act):
            act.wait_ge(loaded_vec, 16)
            a = PACK["c"][0]
            for cond in range(2):
                nc.scalar.activation(cs[:, :, cond], kit.vec[:, a + 8 * cond:a + 8 * cond + 8],
                                     ACT.Silu).then_inc(silu_ready, 1)
            for k in range(KT):
                act.dma_start(kit.x[:, k, :], kit.dram["xT"][k]).then_inc(loaded_x, 16)
            act.wait_ge(loaded_x, 16 * KT)

        @block.tensor
        def _(pe):
            pe.wait_ge(silu_ready, 2)

            def section(i, first=False):
                for s in range(4):
                    pe.wait_ge(loaded[s], (i + 1) * 16)
                    if s == 0 and not first:
                        pe.wait_ge(section_added, i)
                    for half in range(2):
                        mt = 2 * s + half
                        for k in range(KT):
                            mm = nc.tensor.matmul(kit.banks[mt % 8][:, 0:2], raw[:, s, half, k], cs[:, k, :],
                                                  start=(k == 0), stop=(k == KT - 1))
                    mm.then_inc(slot_free, 1)
            section(0, True)
            with pe.Fori(1, 9) as i:
                section(i)

        @block.vector
        def _(dve):
            dve.wait_ge(loaded_vec, 16)

            a = PACK["ada_b"][0]

            def section(i):
                dve.wait_ge(slot_free, i * 4 + 4)
                for mt in range(8):
                    ins = nc.vector.tensor_scalar(kit.mod[:, i, mt, :], kit.banks[mt][:, 0:2],
                                                  kit.vec[:, a + i * 8 + mt:a + i * 8 + mt + 1], None, ALU.add)
                ins.then_inc(section_added, 1)
            for i in range(9):
                section(i)
            dve.wait_ge(section_added, 9)
            a = PACK["norm_w"][0]
            for n in range(3):
                for cond in range(2):
                    ins = nc.vector.scalar_tensor_tensor(
                        kit.scale[:, n, :, cond], kit.mod[:, 3 * n + 1, :, cond], 1.0,
                        kit.vec[:, a + 8 * n:a + 8 * n + 8], ALU.add, ALU.mult)
                ins = nc.vector.tensor_scalar(kit.gate[:, n], kit.mod[:, 3 * n + 2],
                                              1.0 if n == 1 else 0.5, None, ALU.mult)
            ins.then_inc(section_done, 1)
            dve.wait_ge(section_done, 1)


class Norm:

    def __init__(self, kit, ctx, n, h_hi, h_lo):
        self.kit, self.n, self.h_hi, self.h_lo = kit, n, h_hi, h_lo
        buf = lambda name, shape: ctx.enter_context(kit.nc.sbuf_tensor(f"{name}_n{n}", shape, F32))
        self.sq = buf("square", [P, 2, CH])
        self.rms = buf("rms", [P, CH])
        self.inv = buf("inv_rms", [P, NC, CH])
        self.xn = buf("x_normed", [P, 2, CH])
        self.h32 = buf("h_full", [P, 2, CH])
        (self.sq_ready, self.stat_done, self.rms_ready, self.inv_ready, self.xn_ready, self.h32_ready,
         self.h_ready) = (kit.sem(f"{s}_n{n}") for s in (
             "sq_ready", "stat_done", "rms_ready", "inv_ready", "xn_ready", "h32_ready", "h_ready"))

    def at(self, buf, k, c):
        return buf[:, k, c * CH:(c + 1) * CH]

    def tensor(self, pe):
        nc, kit = self.kit.nc, self.kit
        for c in range(NC):
            for k in range(KT):
                m = c * KT + k
                pe.wait_ge(self.sq_ready, m + 1)
                nc.tensor.matmul(kit.banks[4 + c][:, 0:CH], kit.ones[:], self.sq[:, m % 2],
                                 start=(k == 0), stop=(k == KT - 1)).then_inc(self.stat_done, 1)

    def scalar(self, act):
        nc, kit = self.kit.nc, self.kit
        for c in range(NC):
            for k in range(KT):
                m = c * KT + k
                if m >= 2:
                    act.wait_ge(self.stat_done, m - 1)
                nc.scalar.activation(self.sq[:, m % 2], self.at(kit.x, k, c), ACT.Square).then_inc(self.sq_ready, 1)
        for c in range(NC):
            act.wait_ge(self.stat_done, KT * (c + 1))
            if c:
                act.wait_ge(self.inv_ready, c)
            nc.scalar.activation(self.rms[:], kit.banks[4 + c][:, 0:CH], ACT.Sqrt, scale=1.0 / D,
                                 bias=kit.eps[:, 0:1]).then_inc(self.rms_ready, 1)
        for m in range(NC * KT):
            c, k = divmod(m, KT)
            act.wait_ge(self.xn_ready, m + 1)
            if m >= 2:
                act.wait_ge(self.h_ready, m - 1)
            for full in (False, True):
                for cond, a, b in segments(c):
                    out = self.h32[:, m % 2, a:b] if full else self.at(self.h_hi, k, c)[:, a:b]
                    ins = nc.scalar.activation(out, self.xn[:, m % 2, a:b], ACT.Identity,
                                               bias=kit.mod[:, 3 * self.n, k, cond:cond + 1],
                                               scale=kit.scale[:, self.n, k, cond:cond + 1])
            ins.then_inc(self.h32_ready, 1)

    def vector(self, dve):
        nc, kit = self.kit.nc, self.kit
        for c in range(NC):
            dve.wait_ge(self.rms_ready, c + 1)
            nc.vector.reciprocal(self.inv[:, c], self.rms[:]).then_inc(self.inv_ready, 1)

        def low(m):
            c, k = divmod(m, KT)
            dve.wait_ge(self.h32_ready, m + 1)
            nc.vector.tensor_tensor(self.at(self.h_lo, k, c), self.h32[:, m % 2],
                                    self.at(self.h_hi, k, c).bitcast(F32), ALU.subtract).then_inc(self.h_ready, 1)
        dve.wait_ge(self.inv_ready, NC)
        for m in range(NC * KT):
            c, k = divmod(m, KT)
            if m >= 2:
                dve.wait_ge(self.h32_ready, m - 1)
            nc.vector.tensor_tensor(self.xn[:, m % 2], self.at(kit.x, k, c), self.inv[:, c],
                                    ALU.mult).then_inc(self.xn_ready, 1)
            if m:
                low(m - 1)
        low(NC * KT - 1)


def hidden_stage(kit, tag, tiles, ku, w_up, w_down, norm, moving, combine, gate):
    nc = kit.nc
    kinds = ("a", "b", "d")
    loaded = {q: kit.sem(f"w{q}_loaded_{tag}") for q in kinds}
    w_hi_ready = {q: kit.sem(f"w{q}_hi_ready_{tag}") for q in kinds}
    w_ready = {q: kit.sem(f"w{q}_ready_{tag}") for q in kinds}
    up_done, act_ready = kit.sem(f"up_done_{tag}"), kit.sem(f"act_ready_{tag}")
    g32_ready, g_hi_ready, g_ready = (kit.sem(f"{s}_{tag}") for s in ("g32_ready", "g_hi_ready", "g_ready"))
    down_done, x_added = kit.sem(f"down_done_{tag}"), kit.sem(f"x_added_{tag}")
    with ExitStack() as ctx:
        buf = lambda name, shape, dt=F32: ctx.enter_context(nc.sbuf_tensor(f"{name}_{tag}", shape, dt))
        width = {"a": ku * P, "b": ku * P, "d": D}
        raw = {q: buf(f"raw_{q}", [P, width[q]]) for q in kinds}
        whi = {q: buf(f"whi_{q}", [P, 2, width[q]], F32R) for q in kinds}
        wlo = {q: buf(f"wlo_{q}", [P, 2, width[q]], F32R) for q in kinds}
        g_hi, g_lo = buf("g_hi", [P, NC, CH], F32R), buf("g_lo", [P, NC, CH], F32R)
        act_out, g32 = buf("act_out", [P, 2, CH]), buf("g32", [P, 2, CH])
        norm_part, moving = (norm(ctx), None) if norm else (None, moving)
        if norm_part:
            moving = [(norm_part.h_hi, norm_part.h_lo)] * 2
        combine.setup(ctx)
        block = ctx.enter_context(nc.Block())
        source = {"a": w_up[0], "b": w_up[1], "d": w_down}

        @block.sync
        def _(sp):
            def load(q, f, first=False):
                if not first:
                    kit.hold(sp, w_ready[q], f)
                if q == "d":
                    combine.load(sp, f, first)
                sp.dma_start(raw[q][:], source[q][f]).then_inc(loaded[q], 16)
            for q in kinds:
                load(q, 0, True)
            with sp.Fori(1, tiles) as f:
                for q in kinds:
                    load(q, f)

        @block.scalar
        def _(act):
            def high(q, f, slot, first=False):
                act.wait_ge(loaded[q], (f + 1) * 16)
                if not first:
                    act.wait_ge(*((down_done, (f - 1) * 24) if q == "d" else (up_done, (f - 1) * 3)))
                nc.scalar.activation(whi[q][:, slot], raw[q][:], ACT.Copy).then_inc(w_hi_ready[q], 1)

            def step(f, c, par, early, last):
                n = f * 3 + c
                act.wait_ge(up_done, n + 1)
                if not (early and par == 0 and c < 2):
                    act.wait_ge(g32_ready, n - 1)
                slot = (3 * par + c) % 2
                combine.scalar(act, kit.banks[2 * slot][:, 0:CH], act_out[:, slot]).then_inc(act_ready, 1)
                act.wait_ge(g32_ready, n + 1)
                if not (early and par == 0):
                    act.wait_ge(down_done, (n - 2) * 8)
                nc.scalar.activation(g_hi[:, c], g32[:, slot], ACT.Copy).then_inc(g_hi_ready, 1)
                if not last:
                    high(kinds[c], f + 1, 1 - par, early and par == 0)

            for q in kinds:
                high(q, 0, 0, True)
            if norm_part:
                norm_part.scalar(act)

            def pair(i, early=False, last=False):
                for par in range(2):
                    for c in range(NC):
                        step(i * 2 + par, c, par, early, last and par == 1)
            pair(0, early=True)
            with act.Fori(1, tiles // 2 - 1) as i:
                pair(i)
            pair(tiles // 2 - 1, last=True)

        @block.vector
        def _(dve):
            def low(q, f, slot):
                dve.wait_ge(w_hi_ready[q], f + 1)
                nc.vector.tensor_tensor(wlo[q][:, slot], raw[q][:], whi[q][:, slot].bitcast(F32),
                                        ALU.subtract).then_inc(w_ready[q], 1)

            def add_to_x(n, c):
                for d in range(KT):
                    m = n * 8 + d
                    dve.wait_ge(down_done, m + 1)
                    for cond, a, b in segments(c):
                        xs = kit.x[:, d, c * CH + a:c * CH + b]
                        ins = nc.vector.scalar_tensor_tensor(xs, kit.banks[4 + d % 4][:, a:b],
                                                             kit.gate[:, gate, d, cond:cond + 1], xs,
                                                             ALU.mult, ALU.add)
                    ins.then_inc(x_added, 1)

            def step(f, c, par, early, last):
                n = f * 3 + c
                slot = (3 * par + c) % 2
                dve.wait_ge(act_ready, n + 1)
                if not (early and par == 0 and c < 2):
                    dve.wait_ge(g_ready, n - 1)
                combine.vector(dve, f, n, c, kit.banks[2 * slot][:, 0:CH], kit.banks[2 * slot + 1][:, 0:CH],
                               act_out[:, slot], g32[:, slot]).then_inc(g32_ready, 1)
                if not (early and par == 0 and c == 0):
                    add_to_x(n - 1, (c - 1) % NC)
                dve.wait_ge(g_hi_ready, n + 1)
                nc.vector.tensor_tensor(g_lo[:, c], g32[:, slot], g_hi[:, c].bitcast(F32),
                                        ALU.subtract).then_inc(g_ready, 1)
                if not last:
                    low(kinds[c], f + 1, 1 - par)

            for q in kinds:
                low(q, 0, 0)
            if norm_part:
                norm_part.vector(dve)

            def pair(i, early=False, last=False):
                for par in range(2):
                    for c in range(NC):
                        step(i * 2 + par, c, par, early, last and par == 1)
            pair(0, early=True)
            with dve.Fori(1, tiles // 2 - 1) as i:
                pair(i)
            pair(tiles // 2 - 1, last=True)
            add_to_x(tiles * 3 - 1, NC - 1)
            dve.wait_ge(x_added, tiles * 24)

        @block.tensor
        def _(pe):
            if norm_part:
                norm_part.tensor(pe)

            def up(f, c, par, early):
                n = f * 3 + c
                slot = (3 * par + c) % 2
                if norm_part and early and par == 0:
                    pe.wait_ge(norm_part.h_ready, KT * (c + 1))
                if c == 0:
                    pe.wait_ge(w_ready["a"], f + 1)
                    pe.wait_ge(w_ready["b"], f + 1)
                if not (early and par == 0 and c < 2):
                    pe.wait_ge(g32_ready, n - 1)
                for j, q in enumerate("ab"):
                    hi, lo = moving[j]
                    for k in range(ku):
                        cols, toks = slice(k * P, (k + 1) * P), slice(c * CH, (c + 1) * CH)
                        for m, (w, v) in enumerate(((wlo, hi), (whi, lo), (whi, hi))):
                            mm = nc.tensor.matmul(kit.banks[2 * slot + j][:, 0:CH], w[q][:, par, cols],
                                                  v[:, k, toks], start=(k == 0 and m == 0),
                                                  stop=(k == ku - 1 and m == 2))
                mm.then_inc(up_done, 1)


            def step(f, c, par, early):
                up(f, c, par, early)
                if early and par == 0 and c == 0:
                    return
                if c == 1:
                    pe.wait_ge(w_ready["d"], f + 1)
                prev_c = (c - 1) % NC
                down_of(f * 3 + c - 1, prev_c, par if c else 1 - par, early and par == 0 and c == 1)

            def down_of(n, c, par, first):
                pe.wait_ge(g_ready, n + 1)
                for d in range(KT):
                    if not (first and d < 4):
                        pe.wait_ge(x_added, n * 8 + d - 3)
                    cols = slice(d * P, (d + 1) * P)
                    for m, (w, v) in enumerate(((wlo, g_hi), (whi, g_lo), (whi, g_hi))):
                        mm = nc.tensor.matmul(kit.banks[4 + d % 4][:, 0:CH], w["d"][:, par, cols], v[:, c],
                                              start=(m == 0), stop=(m == 2))
                    mm.then_inc(down_done, 1)

            for par in range(2):
                for c in range(NC):
                    step(par, c, par, True)
            with pe.Fori(1, tiles // 2) as i:
                for par in range(2):
                    for c in range(NC):
                        step(i * 2 + par, c, par, False)
            down_of(tiles * 3 - 1, NC - 1, 1, False)


class SwiGLU:

    def __init__(self, nc):
        self.nc = nc

    def setup(self, ctx):
        pass

    def load(self, sp, f, first):
        pass

    def scalar(self, act, a, out):
        return self.nc.scalar.activation(out, a, ACT.Silu)

    def vector(self, dve, f, n, c, a, b, act_out, g32):
        return self.nc.vector.tensor_tensor(g32, act_out, b, ALU.mult)


def ffn(kit, tag, n, w13, w2):
    def norm(ctx):
        h_hi = ctx.enter_context(kit.nc.sbuf_tensor(f"h_hi_{tag}", [P, KT, T], F32R))
        h_lo = ctx.enter_context(kit.nc.sbuf_tensor(f"h_lo_{tag}", [P, KT, T], F32R))
        return Norm(kit, ctx, n, h_hi, h_lo)
    hidden_stage(kit, tag, F_TILES, KT, (kit.dram[w13][0], kit.dram[w13][1]), kit.dram[w2], norm, None,
                 SwiGLU(kit.nc), n)


def with_x(kit, ctx):
    kit.x = ctx.enter_context(kit.nc.sbuf_tensor(f"x{kit.nc.next_id()}", [P, KT, T], F32))


def projection(kit, mix, x_saved):
    nc = kit.nc
    saved = kit.sem("x_saved")
    loaded, w_hi_ready, w_ready = kit.sem("win_loaded"), kit.sem("win_hi_ready"), kit.sem("win_ready")
    proj_done, evicted = kit.sem("proj_done"), kit.sem("proj_evicted")
    pads_ready, tap_done, row_ready = (kit.sem(s) for s in ("pads_ready", "tap_done", "row_ready"))
    stored = [kit.sem(f"row_stored{p}") for p in range(2)]
    with ExitStack() as ctx:
        buf = lambda name, shape, dt=F32: ctx.enter_context(nc.sbuf_tensor(name, shape, dt))
        h_hi, h_lo = buf("h_hi_mix", [P, KT, T], F32R), buf("h_lo_mix", [P, KT, T], F32R)
        norm = Norm(kit, ctx, 1, h_hi, h_lo)
        raw = buf("raw_in", [P, D])
        whi, wlo = buf("whi_in", [P, 2, D], F32R), buf("wlo_in", [P, 2, D], F32R)
        padded = buf("u_padded", [P, 2, T + 4])
        taps = buf("taps", [P, 3])
        row = buf("row_out", [P, 2, T + 4])
        taps_ready = kit.sem("taps_ready")
        block = ctx.enter_context(nc.Block())
        CONV, LORA_, PLAIN, GATE = range(4)

        def kind_of(j):
            return CONV if j < J_WD else LORA_ if j < J_F else PLAIN if j < J_GATE else GATE

        def stored_before(rank):
            if isinstance(rank, int):
                return 32 * min(rank, J_WD // 2) + 16 * max(0, rank - J_WD // 2)
            return rank * 16 + 16 * (J_WD // 2)

        def schedule(eng, step):
            for j in range(2):
                step(j, j, kind_of(j), 0)
            with eng.Fori(1, J_WD // 2) as i:
                for par in range(2):
                    step(i * 2 + par, par, CONV, i)
            for j in range(J_WD, J_GATE + 2):
                step(j, j % 2, kind_of(j), j // 2)
            first = J_GATE + 2
            with eng.Fori(0, (J_END - first) // 2 - 1) as i:
                for o in range(2):
                    step(i * 2 + first + o, (first + o) % 2, GATE, i + (first + o) // 2)
            for j in range(J_END - 2, J_END):
                step(j, j % 2, GATE, j // 2)

        @block.sync
        def _(sp):
            sp.dma_start(raw[:], kit.dram["w_in"][0]).then_inc(loaded, 16)
            for k in range(KT):
                sp.dma_start(x_saved[k], kit.x[:, k]).then_inc(saved, 16)

            def step(j, par, kind, rank):
                if not (isinstance(j, int) and j == J_END - 1):
                    kit.hold(sp, w_ready, j + 1)
                    sp.dma_start(raw[:], kit.dram["w_in"][j + 1]).then_inc(loaded, 16)
                kit.hold(sp, row_ready, j + 1)
                if kind == CONV:
                    sp.dma_start(mix[j][:, 0:T_CTX], row[:, par, 1:T_CTX + 1]).then_inc(stored[par], 16)
                    sp.dma_start(mix[j][:, T_CTX:T], row[:, par, T_CTX + 3:T + 3]).then_inc(stored[par], 16)
                else:
                    sp.dma_start(mix[j], row[:, par, 0:T]).then_inc(stored[par], 16)
            schedule(sp, step)
            for par in range(2):
                sp.wait_ge(stored[par], stored_before((J_END + 1 - par) // 2))
            sp.wait_ge(saved, 16 * KT)

        @block.scalar
        def _(act):
            def high(j, slot, first=False):
                act.wait_ge(loaded, (j + 1) * 16)
                if not first:
                    act.wait_ge(proj_done, (j - 1) * 3)
                nc.scalar.activation(whi[:, slot], raw[:], ACT.Copy).then_inc(w_hi_ready, 1)
            high(0, 0, True)
            norm.scalar(act)

            def step(j, par, kind, rank):
                if kind == CONV and not (isinstance(j, int) and j < 2):
                    act.wait_ge(row_ready, j - 1)
                if kind != CONV:
                    act.wait_ge(stored[par], stored_before(rank))
                for c in range(NC):
                    n = j * 3 + c
                    kit.hold(act, proj_done, n + 1)
                    src = kit.banks[3 * par + c]
                    if kind == CONV:
                        for cond, a, b in segments(c):
                            at = c * CH + a + 1 + 2 * cond
                            ins = nc.scalar.activation(padded[:, par, at:at + b - a], src[:, a:b], ACT.Copy)
                    elif kind == LORA_:
                        func = {J_WD: ACT.Tanh, J_AD: ACT.Copy, J_GD: ACT.Sigmoid}[j]
                        ins = nc.scalar.activation(row[:, par, c * CH:(c + 1) * CH], src[:, 0:CH], func)
                    elif kind == PLAIN:
                        ins = nc.scalar.activation(row[:, par, c * CH:(c + 1) * CH], src[:, 0:CH], ACT.Copy)
                    else:
                        g = PACK["gate_b"][0] - J_GATE
                        ins = nc.scalar.activation(row[:, par, c * CH:(c + 1) * CH], src[:, 0:CH], ACT.Sigmoid,
                                                   bias=kit.vec[:, bass.ds(j + g, 1)])
                    ins.then_inc(evicted, 1)
                    if c == 0 and not (isinstance(j, int) and j == J_END - 1):
                        high(j + 1, 1 - par, isinstance(j, int) and j == 0)
            schedule(act, step)

        @block.vector
        def _(dve):
            def low(j, slot):
                dve.wait_ge(w_hi_ready, j + 1)
                nc.vector.tensor_tensor(wlo[:, slot], raw[:], whi[:, slot].bitcast(F32),
                                        ALU.subtract).then_inc(w_ready, 1)
            for par in range(2):
                for a, b in ((0, 1), (T_CTX + 1, T_CTX + 3), (T + 3, T + 4)):
                    nc.vector.memset(padded[:, par, a:b], 0.0).then_inc(pads_ready, 1)
            dve.wait_ge(pads_ready, 6)
            low(0, 0)
            norm.vector(dve)
            conv = PACK["conv"][0]

            def step(j, par, kind, rank):
                if not (isinstance(j, int) and j == J_END - 1):
                    low(j + 1, 1 - par)
                if kind != CONV:
                    dve.wait_ge(evicted, j * 3 + 3)
                    dve.sem_inc(row_ready, 1)
                    return
                for t in range(3):
                    ins = nc.vector.tensor_copy(taps[:, t:t + 1], kit.vec[:, bass.ds(j + (conv + 12 * t), 1)])
                ins.then_inc(taps_ready, 1)
                dve.wait_ge(taps_ready, j + 1)
                dve.wait_ge(evicted, j * 3 + 3)
                if not (isinstance(j, int) and j < 2):
                    dve.wait_ge(stored[par], rank * 32)
                out = row[:, par, 1:T + 3]
                nc.vector.tensor_scalar(out, padded[:, par, 0:T + 2], taps[:, 0:1], None, ALU.mult).then_inc(tap_done, 1)
                for t in (1, 2):
                    dve.wait_ge(tap_done, j * 2 + t)
                    ins = nc.vector.scalar_tensor_tensor(out, padded[:, par, t:T + 2 + t], taps[:, t:t + 1], out,
                                                         ALU.mult, ALU.add)
                    ins.then_inc(tap_done if t == 1 else row_ready, 1)
            schedule(dve, step)

        @block.tensor
        def _(pe):
            norm.tensor(pe)

            def step(j, par, early=False):
                for c in range(NC):
                    if early and par == 0:
                        pe.wait_ge(norm.h_ready, KT * (c + 1))
                    if c == 0:
                        pe.wait_ge(w_ready, j + 1)
                    if not early:
                        pe.wait_ge(evicted, j * 3 + c - 5)
                    for k in range(KT):
                        cols, toks = slice(k * P, (k + 1) * P), slice(c * CH, (c + 1) * CH)
                        for m, (w, v) in enumerate(((wlo, h_hi), (whi, h_lo), (whi, h_hi))):
                            mm = nc.tensor.matmul(kit.banks[3 * par + c][:, 0:CH], w[:, par, cols], v[:, k, toks],
                                                  start=(k == 0 and m == 0), stop=(k == KT - 1 and m == 2))
                    mm.then_inc(proj_done, 1)
            for j in range(2):
                step(j, j, True)
            with pe.Fori(1, J_END // 2) as i:
                for par in range(2):
                    step(i * 2 + par, par)
            step(J_END - 1, (J_END - 1) % 2)


def unit_keys(kit, mix, keys, cst):
    nc = kit.nc
    s = {q: kit.sem("uk_" + q) for q in ("scaled", "squared", "summed", "rooted", "guarded",
                                         "inverted", "ready", "stored")}
    loaded = [kit.sem(f"uk_loaded{ct}") for ct in range(CT)]
    with ExitStack() as ctx:
        buf = lambda name, shape, dt=F32: ctx.enter_context(nc.sbuf_tensor(name, shape, dt))
        k_raw, kk, sq = (buf(n, [P, CT, T]) for n in ("uk_raw", "uk_scaled", "uk_square"))
        block = ctx.enter_context(nc.Block())

        @block.sync
        def _(sp):
            for ct in range(CT):
                sp.dma_start(k_raw[:, ct], mix[CT + ct]).then_inc(loaded[ct], 16)
            for ct in range(CT):
                sp.wait_ge(s["ready"], NC * (ct + 1))
                sp.dma_start(keys[ct], kk[:, ct]).then_inc(s["stored"], 16)
            sp.wait_ge(s["stored"], 16 * CT)

        @block.scalar
        def _(act):
            for ct in range(CT):
                act.wait_ge(s["scaled"], ct + 1)
                nc.scalar.activation(sq[:, ct], kk[:, ct], ACT.Square).then_inc(s["squared"], 1)
            for m in range(CT * NC):
                ct, c = divmod(m, NC)
                act.wait_ge(s["summed"], m + 1)
                nc.scalar.activation(k_raw[:, ct, c * CH:(c + 1) * CH], kit.banks[m % 8][:, 0:CH],
                                     ACT.Sqrt).then_inc(s["rooted"], 1)

        @block.tensor
        def _(pe):
            for m in range(CT * NC):
                ct, c = divmod(m, NC)
                pe.wait_ge(s["squared"], ct + 1)
                if m >= 8:
                    pe.wait_ge(s["rooted"], m - 7)
                nc.tensor.matmul(kit.banks[m % 8][:, 0:CH], cst.pair_ones, sq[:, ct, c * CH:(c + 1) * CH],
                                 start=True, stop=True).then_inc(s["summed"], 1)

        @block.vector
        def _(dve):
            for ct in range(CT):
                dve.wait_ge(loaded[ct], 16)
                nc.vector.tensor_scalar(kk[:, ct], k_raw[:, ct], kit.col("k_k", ct), None, ALU.mult).then_inc(s["scaled"], 1)
            for m in range(CT * NC):
                ct, c = divmod(m, NC)
                part = slice(c * CH, (c + 1) * CH)
                dve.wait_ge(s["rooted"], m + 1)
                nc.vector.tensor_scalar(k_raw[:, ct, part], k_raw[:, ct, part], 1e-12, None, ALU.max).then_inc(s["guarded"], 1)
                dve.wait_ge(s["guarded"], m + 1)
                nc.vector.reciprocal(sq[:, ct, part], k_raw[:, ct, part]).then_inc(s["inverted"], 1)
                dve.wait_ge(s["inverted"], m + 1)
                nc.vector.tensor_tensor(kk[:, ct, part], kk[:, ct, part], sq[:, ct, part], ALU.mult).then_inc(s["ready"], 1)


class Constants:

    def __init__(self, kit, ctx):
        nc = kit.nc
        self.squares = ctx.enter_context(nc.sbuf_tensor("squares", [P, 2, P], F32))
        self.ident, self.pair_ones = self.squares[:, 0], self.squares[:, 1]
        self.one_minus_ka = ctx.enter_context(nc.sbuf_tensor("one_minus_ka", [P, CT], F32))
        loaded, ready = kit.sem("const_loaded"), kit.sem("const_ready")
        with nc.Block() as block:
            @block.sync
            def _(sp):
                sp.dma_start(self.squares[:], kit.dram["squares"]).then_inc(loaded, 16)
                sp.wait_ge(loaded, 16)

            @block.vector
            def _(dve):
                nc.vector.tensor_scalar(self.one_minus_ka[:], kit.col("k_a", 0, CT), -1.0, 1.0,
                                        ALU.mult, ALU.add).then_inc(ready, 1)
                dve.wait_ge(ready, 1)


def scans(kit, cst, mix, keys, o, kd_sum, states_in, states_out):
    nc = kit.nc
    sem_names = ("lora_done", "lam_ready", "a_ready", "cum_ready", "state_loaded", "state_stored",
                 "pads", "loaded", "g_ready", "ig_ready", "t_ready", "kka_ready", "kd_ready", "sum_ready",
                 "wide_ready", "turned", "tall_ready", "am_done", "am_ready", "y_done", "y_ready",
                 "wy_done", "wy_ready", "wa_done", "wa_ready", "u_done", "u_ready", "z_done", "z_summed",
                 "z_ready", "o_done", "o_ready", "const_in")
    S = {q: kit.sem("sc_" + q) for q in sem_names}
    G2 = {q: [kit.sem(f"sc_{q}{g}") for g in range(2)]
          for q in ("level_ready", "v_ready", "w_done", "w_ready", "p_done", "p_ready", "v_done")}
    LEVELS = 6
    with ExitStack() as ctx:
        buf = lambda name, shape, dt=F32: ctx.enter_context(nc.sbuf_tensor(name, shape, dt))
        masks = buf("masks", [P, 2, 10, P])
        lora_w = buf("lora_w", [P, 2, W])
        lora = buf("lora", [P, 2, T])
        reset = buf("reset", [P, 2, T])
        cum, a_all = buf("cum_decay", [P, CT, T]), buf("a_all", [P, CT, T])
        lam = buf("decay_rate", [P, T])
        rt, kt, vt, kkt = (buf(f"{n}_tile", [P, CT, P]) for n in ("r", "k", "v", "kk"))
        g_pad, inv_g = buf("g_pad", [P, CT, 2, CK + 1]), buf("inv_g", [P, CT, P])
        t_ka, kka, kd = buf("t_ka", [P, CT, P]), buf("kka", [P, CT, P]), buf("kd", [P, CT, P])
        ar = buf("a_r_wide", [P, CT, 2, P])
        b_wide, k_wide = buf("b_wide", [P, CT, P]), buf("k_wide", [P, CT, P])
        a_tall, k_tall, b_tall, v_tall = (buf(f"{n}_tall", [P, W]) for n in ("a", "k", "b", "v"))
        am = buf("am", [P, HEADS, 4, P])
        level = buf("n_level", [P, 2, 2, 4, P])
        v_inv, w_inv, prod = (buf(n, [P, 2, 4, P]) for n in ("inv_t", "inv", "prod"))
        y_tall, wy_tall, u_tall = (buf(n, [P, W]) for n in ("y_tall", "wy_tall", "u_tall"))
        wa = buf("wa_wide", [P, CT, P])
        z, z_sum = buf("z", [P, CT, HD]), buf("z_sum", [P, CT, HD])
        block = ctx.enter_context(nc.Block())
        bank = kit.banks

        def tile_schedule(eng, head, tile, between):
            for d in range(2):
                head(d)
                tile(d, d * NTT, 0)
                between(d)
                with eng.Fori(1, NTT) as i:
                    tile(d, i + d * NTT, i * P if d == 0 else i * (-P) + NTT * P)

        def tokens(buf4, tau):
            return buf4[:, :, tau:tau + P]

        def cum_step(d, ct, c):
            return (d * CT + ct) * NC + c

        @block.sync
        def _(sp):
            sp.dma_start(lora_w[:], kit.dram["lora_up"]).then_inc(S["const_in"], 16)
            sp.dma_start(reset[:], kit.dram["reset"]).then_inc(S["const_in"], 16)
            sp.dma_start(masks[:], kit.dram["masks"]).then_inc(S["const_in"], 16)
            sp.dma_start(lora[:], mix[J_WD:J_GD].rearrange("c p t -> p c t")).then_inc(S["const_in"], 16)

            def tile(d, s, tau):
                if not (isinstance(s, int) and s == 0):
                    kit.hold(sp, S["wide_ready"], s * 4)
                    kit.hold(sp, S["turned"], s * 4)
                for dst, src in ((rt, mix[0:CT]), (kt, mix[CT:2 * CT]), (vt, mix[2 * CT:3 * CT]), (kkt, keys)):
                    sp.dma_start(dst[:], src[:, :, bass.ds(tau, P)].rearrange("c p t -> p c t")).then_inc(S["loaded"], 16)

            def between(d):
                sp.wait_ge(S["z_ready"], (d * NTT + 1) * 2)
                sp.dma_start(states_out[d], z[:]).then_inc(S["state_stored"], 16)
                sp.wait_ge(S["state_stored"], 16 * (d + 1))
                sp.wait_ge(S["o_done"], d * NTT + 1)
                sp.dma_start(z[:], states_in[d]).then_inc(S["state_loaded"], 16)
            tile_schedule(sp, lambda d: None, tile, between)
            sp.wait_ge(S["state_stored"], 32)

        @block.gpsimd
        def _(pool):
            pool.wait_ge(S["const_in"], 64)

            def head(d):
                pool.wait_ge(S["a_ready"], CT * NC * (d + 1))

            def tile(d, s, tau):
                at = bass.ds(tau, P)
                kit.hold(pool, S["loaded"], (s + 1) * 64)
                nc.gpsimd.tensor_tensor(kka[:], kkt[:], a_all[:, :, at], ALU.mult).then_inc(S["kka_ready"], 1)
                pool.wait_ge(S["t_ready"], (s + 1) * CT)
                nc.gpsimd.tensor_tensor(kd[:], kt[:], t_ka[:], ALU.mult).then_inc(S["kd_ready"], 1)
                kit.hold(pool, S["kd_ready"], s + 1)
                if d == 0:
                    nc.gpsimd.tensor_copy(kd_sum[:, :, at], kd[:]).then_inc(S["sum_ready"], 1)
                else:
                    nc.gpsimd.tensor_tensor(kd_sum[:, :, at], kd_sum[:, :, at], kd[:], ALU.add).then_inc(S["sum_ready"], 1)
                for l in range(LEVELS):
                    for g in range(2):
                        if l == 0:
                            pool.wait_ge(S["am_ready"], s * 8 + 4 * g + 4)
                        if l == 2:
                            pool.wait_ge(G2["v_ready"][g], s * 6 + 1)
                        if l >= 3:
                            pool.wait_ge(G2["p_done"][g], s * 5 + l - 2)
                        nc.gpsimd.tensor_tensor(level[:, g, l % 2], am[:, 4 * g:4 * g + 4, 0],
                                                masks[:, d, 4 + l:5 + l].broadcast_to([P, 4, P]),
                                                ALU.mult).then_inc(G2["level_ready"][g], 1)
            tile_schedule(pool, head, tile, lambda d: None)

        @block.scalar
        def _(act):
            act.wait_ge(S["const_in"], 64)

            def head(d):
                for ct in range(CT):
                    for c in range(NC):
                        n = cum_step(d, ct, c)
                        part = slice(c * CH, (c + 1) * CH)
                        act.wait_ge(S["lora_done"], 2 * n + 1)
                        if c == 0 and d * CT + ct:
                            act.wait_ge(S["cum_ready"], d * CT + ct)
                        nc.scalar.activation(lam[:, part], bank[n % 4][:, 0:CH], ACT.Sigmoid,
                                             bias=kit.col("w0", d * CT + ct)).then_inc(S["lam_ready"], 1)
                        act.wait_ge(S["lora_done"], 2 * n + 2)
                        nc.scalar.activation(a_all[:, ct, part], bank[4 + n % 4][:, 0:CH], ACT.Sigmoid,
                                             bias=kit.col("a0", d * CT + ct)).then_inc(S["a_ready"], 1)
                act.wait_ge(S["cum_ready"], CT * (d + 1))
                act.wait_ge(S["a_ready"], CT * NC * (d + 1))

            def tile(d, s, tau):
                at = bass.ds(tau, P)
                body = slice(1, CK + 1) if d == 0 else slice(0, CK)
                if not (isinstance(s, int) and s == 0):
                    kit.hold(act, S["z_ready"], s * 2)
                for ct in range(CT):
                    ins = nc.scalar.activation(g_pad[:, ct, :, body],
                                               cum[:, ct, at].rearrange("p (k t) -> p k t", k=2),
                                               ACT.Exp, scale=-DECAY_SCALE)
                ins.then_inc(S["g_ready"], 1)
                nc.scalar.activation(inv_g[:], cum[:, :, at], ACT.Exp, scale=DECAY_SCALE).then_inc(S["ig_ready"], 1)
                for ct in range(CT):
                    nc.scalar.activation(t_ka[:, ct], a_all[:, ct, at], ACT.Identity, scale=kit.col("k_a", ct),
                                         bias=cst.one_minus_ka[:, ct:ct + 1]).then_inc(S["t_ready"], 1)
                for m, dst in enumerate((a_tall, k_tall, b_tall, v_tall)):
                    act.wait_ge(S["turned"], s * 4 + m + 1)
                    nc.scalar.activation(dst[:], bank[4 + m][:], ACT.Copy).then_inc(S["tall_ready"], 1)
                act.wait_ge(S["y_done"], s + 1)
                nc.scalar.activation(y_tall[:], bank[4][:], ACT.Copy).then_inc(S["y_ready"], 1)
                for l in range(1, LEVELS):
                    for g in range(2):
                        act.wait_ge(G2["w_done"][g], s * 5 + l)
                        nc.scalar.activation(w_inv[:, g], bank[2 * g][:], ACT.Copy).then_inc(G2["w_ready"][g], 1)
                    for g in range(2):
                        act.wait_ge(G2["p_done"][g], s * 5 + l)
                        nc.scalar.activation(prod[:, g], bank[2 * g][:], ACT.Copy).then_inc(G2["p_ready"][g], 1)
                act.wait_ge(S["wy_done"], s + 1)
                nc.scalar.activation(wy_tall[:], bank[5][:], ACT.Copy).then_inc(S["wy_ready"], 1)
                act.wait_ge(S["wa_done"], s + 1)
                nc.scalar.activation(wa[:], bank[6][:], ACT.Copy).then_inc(S["wa_ready"], 1)
            tile_schedule(act, head, tile, lambda d: None)

        @block.vector
        def _(dve):
            dve.wait_ge(S["const_in"], 64)

            def head(d):
                for ct in range(CT):
                    dve.wait_ge(S["lam_ready"], cum_step(d, ct, NC))
                    way = slice(None, None, 1 if d == 0 else -1)
                    nc.vector.tensor_tensor_scan(cum[:, ct, way], reset[:, d, way], lam[:, way], 0.0,
                                                 ALU.mult, ALU.add).then_inc(S["cum_ready"], 1)
                edge = 0 if d == 0 else CK
                nc.vector.memset(g_pad[:, :, :, edge:edge + 1], 1.0).then_inc(S["pads"], 1)
                nc.vector.memset(z[:], 0.0).then_inc(S["pads"], 1)
                dve.wait_ge(S["pads"], 2 * d + 2)

            def between(d):
                dve.wait_ge(S["state_loaded"], 16 * (d + 1))

            def tile(d, s, tau):
                at = bass.ds(tau, P)
                before, upto = (slice(0, CK), slice(1, CK + 1)) if d == 0 else (slice(1, CK + 1), slice(0, CK))
                last = slice(CK, CK + 1) if d == 0 else slice(0, 1)
                by_chunk = lambda v: v.rearrange("p c (k t) -> p c k t", k=2)
                dve.wait_ge(S["loaded"], (s + 1) * 64)
                dve.wait_ge(S["g_ready"], s + 1)
                if not (isinstance(s, int) and s == 0):
                    dve.wait_ge(S["o_done"], s)
                nc.vector.tensor_tensor(by_chunk(ar[:, :, 0]), by_chunk(kkt[:]), g_pad[:, :, :, before],
                                        ALU.mult).then_inc(S["wide_ready"], 1)
                nc.vector.tensor_tensor(by_chunk(ar[:, :, 1]), by_chunk(rt[:]), g_pad[:, :, :, upto],
                                        ALU.mult).then_inc(S["wide_ready"], 1)
                dve.wait_ge(S["ig_ready"], s + 1)
                dve.wait_ge(S["kka_ready"], s + 1)
                nc.vector.scalar_tensor_tensor(b_wide[:], kka[:], -1.0, inv_g[:], ALU.mult, ALU.mult)\
                    .then_inc(S["wide_ready"], 1)
                dve.wait_ge(S["kd_ready"], s + 1)
                nc.vector.tensor_tensor(k_wide[:], kd[:], inv_g[:], ALU.mult).then_inc(S["wide_ready"], 1)
                for h in range(HEADS):
                    dve.wait_ge(S["am_done"], s * 8 + h + 1)
                    nc.vector.tensor_tensor(am[:, h], bank[h % 4][:].rearrange("p (m t) -> p m t", m=4),
                                            masks[:, d, 0:4], ALU.mult).then_inc(S["am_ready"], 1)
                for g in range(2):
                    dve.wait_ge(G2["level_ready"][g], s * 6 + 1)
                    nc.vector.tensor_tensor(v_inv[:, g], level[:, g, 0],
                                            cst.squares[:, 0:1].broadcast_to([P, 4, P]), ALU.add)\
                        .then_inc(G2["v_ready"][g], 1)
                for l in range(1, LEVELS):
                    for g in range(2):
                        dve.wait_ge(G2["v_done"][g], s * 5 + l)
                        nc.vector.tensor_tensor(v_inv[:, g], bank[2 * g + 1][:].rearrange("p (h t) -> p h t", h=4),
                                                v_inv[:, g], ALU.add).then_inc(G2["v_ready"][g], 1)
                for c in ((0, 1) if d == 0 else (1, 0)):
                    first = c == (0 if d == 0 else 1)
                    n = s * 2 + (0 if first else 1)
                    rows = slice(CK * c, CK * c + CK)
                    by_head = lambda v: v[rows].rearrange("p (c e i) -> p c e i", e=2, i=HD)
                    dve.wait_ge(S["u_done"], n + 1)
                    if first:
                        dve.wait_ge(S["wy_ready"], s + 1)
                    for e in range(2):
                        nc.vector.tensor_tensor(by_head(u_tall[:])[:, :, e],
                                                bank[4 + e][rows, 0:CT * HD].rearrange("p (c i) -> p c i", c=CT),
                                                by_head(wy_tall[:])[:, :, e], ALU.add).then_inc(S["u_ready"], 1)
                    dve.wait_ge(S["z_done"], n + 1)
                    nc.vector.tensor_tensor(z_sum[:], bank[6][:, 0:CT * HD].rearrange("p (c i) -> p c i", c=CT), z[:],
                                            ALU.add).then_inc(S["z_summed"], 1)
                    dve.wait_ge(S["z_summed"], n + 1)
                    nc.vector.tensor_tensor(z[:], z_sum[:], g_pad[:, :, c, last].broadcast_to([P, CT, HD]),
                                            ALU.mult).then_inc(S["z_ready"], 1)
                kit.hold(dve, S["o_done"], s + 1)
                for e in range(2):
                    half = slice(64 * e, 64 * e + 64)
                    src = bank[e][half].rearrange("p (c t) -> p c t", c=CT)
                    dst = o[half, :, at]
                    if d == 0:
                        nc.vector.tensor_copy(dst, src).then_inc(S["o_ready"], 1)
                    else:
                        nc.vector.tensor_tensor(dst, src, dst, ALU.add).then_inc(S["o_ready"], 1)
            tile_schedule(dve, head, tile, between)

        @block.tensor
        def _(pe):
            pe.wait_ge(S["const_in"], 64)

            def head(d):
                rows = slice(LORA * d, LORA * d + LORA)
                if d:
                    pe.wait_ge(S["o_ready"], 2 * NTT)
                for ct in range(CT):
                    for c in range(NC):
                        n = cum_step(d, ct, c)
                        part = slice(c * CH, (c + 1) * CH)
                        for m, ready in ((0, "lam_ready"), (1, "a_ready")):
                            if n >= 4:
                                pe.wait_ge(S[ready], n - 3)
                            nc.tensor.matmul(bank[4 * m + n % 4][:, 0:CH], lora_w[rows, m, ct * P:(ct + 1) * P],
                                             lora[rows, m, part], start=True, stop=True).then_inc(S["lora_done"], 1)
                pe.wait_ge(S["a_ready"], CT * NC * (d + 1))
                pe.wait_ge(S["pads"], 2 * d + 2)

            def between(d):
                kit.hold(pe, S["state_loaded"], 16 * (d + 1))

            def tile(d, s, tau):
                mm = nc.tensor.matmul
                hold = lambda q, v: kit.hold(pe, S[q], v)
                if not (isinstance(s, int) and s == 0):
                    hold("o_ready", s * 2)
                hold("loaded", (s + 1) * 64)
                for m, (src, n) in enumerate(((lambda ct: ar[:, ct, 0], 1), (lambda ct: k_wide[:, ct], 4),
                                              (lambda ct: b_wide[:, ct], 4), (lambda ct: vt[:, ct], 4))):
                    hold("wide_ready", s * 4 + n)
                    for ct in range(CT):
                        ins = nc.tensor.transpose(bank[4 + m][:, ct * P:(ct + 1) * P], src(ct), cst.ident)
                    ins.then_inc(S["turned"], 1)
                for h in range(HEADS):
                    ct, e = divmod(h, 2)
                    half = slice(64 * e, 64 * e + 64)
                    if h >= 4:
                        hold("am_ready", s * 8 + h - 3)
                    both = ar[half, ct].rearrange("p m t -> p (m t)")
                    mm(bank[h % 4][:, 0:2 * P], b_wide[half, ct], both, start=True, stop=True)
                    mm(bank[h % 4][:, 2 * P:4 * P], k_wide[half, ct], both, start=True, stop=True)\
                        .then_inc(S["am_done"], 1)
                hold("am_ready", s * 8 + 8)
                hold("tall_ready", s * 4 + 4)
                for h in range(HEADS):
                    ins = mm(bank[4][:, h * HD:(h + 1) * HD], am[:, h, 2], v_tall[:, h * HD:(h + 1) * HD],
                             start=True, stop=True)
                ins.then_inc(S["y_done"], 1)
                for l in range(1, LEVELS):
                    for g in range(2):
                        kit.hold(pe, G2["v_ready"][g], s * 6 + l)
                        for q in range(4):
                            ins = nc.tensor.transpose(bank[2 * g][:, q * P:(q + 1) * P], v_inv[:, g, q], cst.ident)
                        ins.then_inc(G2["w_done"][g], 1)
                    for g in range(2):
                        kit.hold(pe, G2["level_ready"][g], s * 6 + l + 1)
                        kit.hold(pe, G2["w_ready"][g], s * 5 + l)
                        for q in range(4):
                            ins = mm(bank[2 * g][:, q * P:(q + 1) * P], level[:, g, l % 2, q], w_inv[:, g, q],
                                     start=True, stop=True)
                        ins.then_inc(G2["p_done"][g], 1)
                    for g in range(2):
                        kit.hold(pe, G2["p_ready"][g], s * 5 + l)
                        for q in range(4):
                            ins = mm(bank[2 * g + 1][:, q * P:(q + 1) * P], prod[:, g, q], v_inv[:, g, q],
                                     start=True, stop=True)
                        ins.then_inc(G2["v_done"][g], 1)
                hold("y_ready", s + 1)
                for g in range(2):
                    kit.hold(pe, G2["v_ready"][g], s * 6 + 6)
                for h in range(HEADS):
                    ins = mm(bank[5][:, h * HD:(h + 1) * HD], v_inv[:, h // 4, h % 4], y_tall[:, h * HD:(h + 1) * HD],
                             start=True, stop=True)
                ins.then_inc(S["wy_done"], 1)
                for h in range(HEADS):
                    ct, e = divmod(h, 2)
                    ins = mm(bank[6][64 * e:64 * e + 64, ct * P:(ct + 1) * P], a_tall[:, h * HD:(h + 1) * HD],
                             v_inv[:, h // 4, h % 4], start=True, stop=True)
                ins.then_inc(S["wa_done"], 1)
                for h in range(HEADS):
                    ct, e = divmod(h, 2)
                    mm(bank[e][64 * e:64 * e + 64, ct * P:(ct + 1) * P], v_tall[:, h * HD:(h + 1) * HD], am[:, h, 3],
                       start=(ct == 0), stop=False, skip_group_check=True)
                hold("wy_ready", s + 1)
                hold("wa_ready", s + 1)
                for c in ((0, 1) if d == 0 else (1, 0)):
                    first = c == (0 if d == 0 else 1)
                    n = s * 2 + (0 if first else 1)
                    rows = slice(CK * c, CK * c + CK)
                    if not (isinstance(n, int) and n == 0):
                        hold("z_ready", n)
                    for h in range(HEADS):
                        ct, e = divmod(h, 2)
                        half = slice(64 * e, 64 * e + 64)
                        ins = mm(bank[4 + e][rows, ct * HD:(ct + 1) * HD], wa[half, ct, rows], z[half, ct],
                                 start=True, stop=True)
                    ins.then_inc(S["u_done"], 1)
                    for h in range(HEADS):
                        ct, e = divmod(h, 2)
                        half = slice(64 * e, 64 * e + 64)
                        mm(bank[e][half, ct * P + CK * c:ct * P + CK * c + CK], z[half, ct], ar[half, ct, 1, rows],
                           start=False, stop=False, skip_group_check=True)
                    for h in range(HEADS):
                        ct, e = divmod(h, 2)
                        mm(bank[6][64 * e:64 * e + 64, ct * HD:(ct + 1) * HD], k_tall[rows, h * HD:(h + 1) * HD],
                           v_tall[rows, h * HD:(h + 1) * HD], start=(ct == 0), stop=False, skip_group_check=True)
                    hold("u_ready", (n + 1) * 2)
                    for h in range(HEADS):
                        ct, e = divmod(h, 2)
                        ins = mm(bank[6][64 * e:64 * e + 64, ct * HD:(ct + 1) * HD], b_tall[rows, h * HD:(h + 1) * HD],
                                 u_tall[rows, h * HD:(h + 1) * HD], start=False, stop=True, skip_group_check=True)
                    ins.then_inc(S["z_done"], 1)
                for h in range(HEADS):
                    ct, e = divmod(h, 2)
                    ins = mm(bank[e][64 * e:64 * e + 64, ct * P:(ct + 1) * P], u_tall[:, h * HD:(h + 1) * HD], am[:, h, 1],
                             start=False, stop=True, skip_group_check=True)
                ins.then_inc(S["o_done"], 1)
            tile_schedule(pe, head, tile, between)


def head_norm(kit, cst, mix, o, kd_sum, branch):
    nc = kit.nc
    s = {q: kit.sem("hn_" + q) for q in (
        "loaded", "mean_done", "centered", "rk_ready", "squared", "var_done", "rooted", "inverted", "scaled",
        "affine", "bonus_done", "bonus_v", "with_bonus", "gate_done", "gated", "hi_ready", "lo_ready", "stored")}
    with ExitStack() as ctx:
        buf = lambda name, shape, dt=F32: ctx.enter_context(nc.sbuf_tensor(name, shape, dt))
        r, v = buf("hn_r", [P, CT, T]), buf("hn_v", [P, CT, T])
        gd, g_up = buf("hn_gd", [P, T]), buf("hn_g_up", [P, W])
        o_hi, o_lo = buf("hn_hi", [P, CT, T], F32R), buf("hn_lo", [P, CT, T], F32R)
        block = ctx.enter_context(nc.Block())
        steps = CT * NC
        ct_of, part = (lambda m: m // NC), (lambda m: slice(m % NC * CH, m % NC * CH + CH))
        at = lambda a, m: a[:, ct_of(m), part(m)]
        bank = lambda m, q: kit.banks[4 * (m % 2) + q][:, 0:CH]

        def skewed(stages):
            for t in range(steps + max(lag for lag, _ in stages)):
                for lag, piece in stages:
                    if 0 <= t - lag < steps:
                        piece(t - lag)

        @block.sync
        def _(sp):
            sp.dma_start(g_up[:], kit.dram["g_up"]).then_inc(s["loaded"], 16)
            sp.dma_start(gd[:], mix[J_GD]).then_inc(s["loaded"], 16)
            sp.dma_start(r[:], mix[0:CT].rearrange("c p t -> p c t")).then_inc(s["loaded"], 16)
            sp.dma_start(v[:], mix[2 * CT:3 * CT].rearrange("c p t -> p c t")).then_inc(s["loaded"], 16)
            for ct in range(CT):
                sp.wait_ge(s["lo_ready"], NC * (ct + 1))
                sp.dma_start(branch[0, ct], o_hi[:, ct].bitcast(F32)).then_inc(s["stored"], 16)
                sp.dma_start(branch[1, ct], o_lo[:, ct].bitcast(F32)).then_inc(s["stored"], 16)
            sp.wait_ge(s["stored"], 32 * CT)

        @block.tensor
        def _(pe):
            pe.wait_ge(s["loaded"], 64)

            def sums(m):
                if m >= 2:
                    pe.wait_ge(s["centered"], m - 1)
                nc.tensor.matmul(bank(m, 0), cst.pair_ones, at(o, m), start=True, stop=True).then_inc(s["mean_done"], 1)
                if m >= 2:
                    pe.wait_ge(s["gated"], m - 1)
                nc.tensor.matmul(bank(m, 3), g_up[:, ct_of(m) * P:(ct_of(m) + 1) * P], gd[:, part(m)],
                                 start=True, stop=True).then_inc(s["gate_done"], 1)

            def bonus(m):
                pe.wait_ge(s["rk_ready"], m + 1)
                if m >= 2:
                    pe.wait_ge(s["bonus_v"], m - 1)
                nc.tensor.matmul(bank(m, 2), cst.pair_ones, at(kd_sum, m), start=True, stop=True)\
                    .then_inc(s["bonus_done"], 1)

            def variance(m):
                pe.wait_ge(s["squared"], m + 1)
                if m >= 2:
                    pe.wait_ge(s["rooted"], m - 1)
                nc.tensor.matmul(bank(m, 1), cst.pair_ones, at(r, m), start=True, stop=True).then_inc(s["var_done"], 1)
            skewed([(0, sums), (0, bonus), (0, variance)])

        @block.scalar
        def _(act):
            def square(m):
                act.wait_ge(s["centered"], m + 1)
                act.wait_ge(s["rk_ready"], m + 1)
                nc.scalar.activation(at(r, m), at(o, m), ACT.Square).then_inc(s["squared"], 1)

            def root(m):
                act.wait_ge(s["var_done"], m + 1)
                nc.scalar.activation(at(r, m), bank(m, 1), ACT.Sqrt, scale=1.0 / HD, bias=kit.eps[:, 1:2])\
                    .then_inc(s["rooted"], 1)

            def affine(m):
                act.wait_ge(s["scaled"], m + 1)
                nc.scalar.activation(at(r, m), at(o, m), ACT.Identity, scale=kit.col("lnx_w", ct_of(m)),
                                     bias=kit.col("lnx_b", ct_of(m))).then_inc(s["affine"], 1)

            def high(m):
                act.wait_ge(s["gated"], m + 1)
                nc.scalar.activation(at(o_hi, m), at(o, m), ACT.Copy).then_inc(s["hi_ready"], 1)
            skewed([(0, square), (0, root), (1, affine), (2, high)])

        @block.vector
        def _(dve):
            dve.wait_ge(s["loaded"], 64)

            def center(m):
                dve.wait_ge(s["mean_done"], m + 1)
                nc.vector.scalar_tensor_tensor(at(o, m), bank(m, 0), -1.0 / HD, at(o, m), ALU.mult, ALU.add)\
                    .then_inc(s["centered"], 1)
                nc.vector.scalar_tensor_tensor(at(kd_sum, m), at(r, m), kit.col("r_k", ct_of(m)), at(kd_sum, m),
                                               ALU.mult, ALU.mult).then_inc(s["rk_ready"], 1)

            def normed(m):
                dve.wait_ge(s["rooted"], m + 1)
                nc.vector.reciprocal(at(kd_sum, m), at(r, m)).then_inc(s["inverted"], 1)
                dve.wait_ge(s["inverted"], m + 1)
                nc.vector.tensor_tensor(at(o, m), at(o, m), at(kd_sum, m), ALU.mult).then_inc(s["scaled"], 1)

            def bonus(m):
                dve.wait_ge(s["bonus_done"], m + 1)
                nc.vector.tensor_tensor(at(v, m), bank(m, 2), at(v, m), ALU.mult).then_inc(s["bonus_v"], 1)

            def gated(m):
                dve.wait_ge(s["affine"], m + 1)
                dve.wait_ge(s["bonus_v"], m + 1)
                nc.vector.tensor_tensor(at(v, m), at(v, m), at(r, m), ALU.add).then_inc(s["with_bonus"], 1)
                dve.wait_ge(s["with_bonus"], m + 1)
                dve.wait_ge(s["gate_done"], m + 1)
                nc.vector.tensor_tensor(at(o, m), bank(m, 3), at(v, m), ALU.mult).then_inc(s["gated"], 1)

            def low(m):
                dve.wait_ge(s["hi_ready"], m + 1)
                nc.vector.tensor_tensor(at(o_lo, m), at(o, m), at(o_hi, m).bitcast(F32), ALU.subtract)\
                    .then_inc(s["lo_ready"], 1)
            skewed([(0, center), (0, bonus), (1, normed), (1, gated), (2, low)])


def fourier(kit, mix, branch):
    nc = kit.nc
    s = {q: kit.sem("fo_" + q) for q in (
        "f_loaded", "c_loaded", "g_done", "g_ready", "ctx_done", "ctx_hi", "ctx_lo", "g_hi_ready", "g_lo_ready",
        "dft_hi_ready", "dft_ready", "unit_done", "hi_ready", "lo_ready", "stored")}
    dft_loaded = [kit.sem(f"fo_dft_loaded{p}") for p in range(2)]
    LT = NTT - 1
    with ExitStack() as ctx:
        buf = lambda name, shape, dt=F32: ctx.enter_context(nc.sbuf_tensor(name, shape, dt))
        f = buf("fo_f", [P, FG, T])
        cs = buf("fo_cs", [P, 2 * FD])
        dft_ctx = buf("fo_dft_ctx", [P, 2, T_CTX])
        g = buf("fo_g", [P, NTT, 2, FG, FD])
        raw = buf("fo_raw", [P, 2, T_LAT])
        dft_hi, dft_lo = buf("fo_dft_hi", [P, 2, T_LAT], F32R), buf("fo_dft_lo", [P, 2, T_LAT], F32R)
        g_hi, g_lo = buf("fo_g_hi", [P, 2, FG, FD], F32R), buf("fo_g_lo", [P, 2, FG, FD], F32R)
        f_hi, f_lo = buf("fo_hi", [P, FG, T], F32R), buf("fo_lo", [P, FG, T], F32R)
        block = ctx.enter_context(nc.Block())
        bank = kit.banks

        @block.sync
        def _(sp):
            sp.dma_start(cs[:], kit.dram["dft_features"]).then_inc(s["c_loaded"], 16)
            sp.dma_start(dft_ctx[:], kit.dram["dft_context"]).then_inc(s["c_loaded"], 16)
            sp.dma_start(f[:], mix[J_F:J_GATE].rearrange("c p t -> p c t")).then_inc(s["f_loaded"], 16)

            def load(tt, first=False):
                for p in range(2):
                    if not first:
                        kit.hold(sp, s["dft_ready"], tt * 2 + (p - 1))
                    sp.dma_start(raw[:, p], kit.dram["dft_latents"][tt, p]).then_inc(dft_loaded[p], 16)
            load(0, True)
            with sp.Fori(1, LT) as tt:
                load(tt)
            for g_ in range(FG):
                sp.wait_ge(s["lo_ready"], 2 * (g_ + 1))
                sp.wait_ge(s["ctx_lo"], 1)
                sp.dma_start(branch[0, g_], f_hi[:, g_].bitcast(F32)).then_inc(s["stored"], 16)
                sp.dma_start(branch[1, g_], f_lo[:, g_].bitcast(F32)).then_inc(s["stored"], 16)
            sp.wait_ge(s["stored"], 32 * FG)

        @block.tensor
        def _(pe):
            pe.wait_ge(s["c_loaded"], 32)
            pe.wait_ge(s["f_loaded"], 16)
            for m in range(2 * NTT):
                tt, pair = divmod(m, 2)
                if m >= 8:
                    pe.wait_ge(s["g_ready"], m - 7)
                for q in range(2):
                    ins = nc.tensor.matmul(bank[m % 8][:, q * 2 * FD:(q + 1) * 2 * FD],
                                           f[:, 2 * pair + q, tt * P:(tt + 1) * P], cs[:], start=True, stop=True)
                ins.then_inc(s["g_done"], 1)
            pe.wait_ge(s["g_ready"], 2 * NTT)
            for q in range(FG):
                for p in range(2):
                    ins = nc.tensor.matmul(bank[0][:, q * P:(q + 1) * P], g[:, 0, p, q], dft_ctx[:, p],
                                           start=(p == 0), stop=(p == 1))
            ins.then_inc(s["ctx_done"], 1)
            pe.wait_ge(s["ctx_lo"], 1)

            def units(tt, early=False, late=False):
                for p in range(2):
                    pe.wait_ge(s["g_lo_ready"], tt * 2 + (p + 1))
                    pe.wait_ge(s["dft_ready"], tt * 2 + (p + 1))
                    for q in range(FG):
                        for half in range(2):
                            cols = slice(half * 512, half * 512 + 512)
                            for m, (w, v) in enumerate(((g_lo, dft_hi), (g_hi, dft_lo), (g_hi, dft_hi))):
                                ins = nc.tensor.matmul(bank[2 * q + half][:], w[:, p, q], v[:, p, cols],
                                                       start=(early and p == 0 and m == 0),
                                                       stop=(late and p == 1 and m == 2), skip_group_check=True)
                    ins.then_inc(s["unit_done"], 1)
            units(0, early=True)
            with pe.Fori(1, LT - 1) as tt:
                units(tt)
            units(LT - 1, late=True)

        @block.scalar
        def _(act):
            for m in range(2 * NTT):
                tt, pair = divmod(m, 2)
                act.wait_ge(s["g_done"], m + 1)
                for q in range(2):
                    ins = nc.scalar.activation(g[:, tt, :, 2 * pair + q], bank[m % 8][:, q * 2 * FD:(q + 1) * 2 * FD]
                                               .rearrange("p (a t) -> p a t", a=2), ACT.Copy)
                ins.then_inc(s["g_ready"], 1)
            act.wait_ge(s["ctx_done"], 1)
            nc.scalar.activation(f_hi[:, :, 0:T_CTX], bank[0][:].rearrange("p (g t) -> p g t", g=FG), ACT.Copy)\
                .then_inc(s["ctx_hi"], 1)
            act.wait_ge(s["g_ready"], 2 * NTT)

            def split(tt, first=False):
                for p in range(2):
                    if not first:
                        kit.hold(act, s["unit_done"], tt * 2 + (p - 1))
                    tile = g[:, bass.ds(tt + 1, 1), p]
                    nc.scalar.activation(g_hi[:, p:p + 1], tile, ACT.Copy).then_inc(s["g_hi_ready"], 1)
                    act.wait_ge(dft_loaded[p], (tt + 1) * 16)
                    nc.scalar.activation(dft_hi[:, p], raw[:, p], ACT.Copy).then_inc(s["dft_hi_ready"], 1)
            split(0, True)
            with act.Fori(1, LT) as tt:
                split(tt)
            act.wait_ge(s["unit_done"], 2 * LT)
            for q in range(FG):
                for half in range(2):
                    cols = slice(T_CTX + half * 512, T_CTX + half * 512 + 512)
                    nc.scalar.activation(f_hi[:, q, cols], bank[2 * q + half][:], ACT.Copy).then_inc(s["hi_ready"], 1)

        @block.vector
        def _(dve):
            dve.wait_ge(s["ctx_hi"], 1)
            nc.vector.tensor_tensor(f_lo[:, :, 0:T_CTX], bank[0][:].rearrange("p (g t) -> p g t", g=FG),
                                    f_hi[:, :, 0:T_CTX].bitcast(F32), ALU.subtract).then_inc(s["ctx_lo"], 1)

            def split(tt):
                for p in range(2):
                    dve.wait_ge(s["g_hi_ready"], tt * 2 + (p + 1))
                    nc.vector.tensor_tensor(g_lo[:, p:p + 1], g[:, bass.ds(tt + 1, 1), p], g_hi[:, p:p + 1].bitcast(F32),
                                            ALU.subtract).then_inc(s["g_lo_ready"], 1)
                    dve.wait_ge(s["dft_hi_ready"], tt * 2 + (p + 1))
                    nc.vector.tensor_tensor(dft_lo[:, p], raw[:, p], dft_hi[:, p].bitcast(F32),
                                            ALU.subtract).then_inc(s["dft_ready"], 1)
            split(0)
            with dve.Fori(1, LT) as tt:
                split(tt)
            for m in range(2 * FG):
                q, half = divmod(m, 2)
                cols = slice(T_CTX + half * 512, T_CTX + half * 512 + 512)
                dve.wait_ge(s["hi_ready"], m + 1)
                nc.vector.tensor_tensor(f_lo[:, q, cols], bank[m][:], f_hi[:, q, cols].bitcast(F32),
                                        ALU.subtract).then_inc(s["lo_ready"], 1)


class Merge:

    def __init__(self, kit, mix):
        self.kit, self.nc, self.mix = kit, kit.nc, mix
        self.loaded, self.left, self.right = kit.sem("gates_loaded"), kit.sem("gated_a"), kit.sem("gated_b")
        self.used = kit.sem("gates_used")

    def setup(self, ctx):
        self.gates = ctx.enter_context(self.nc.sbuf_tensor("gates", [P, 2, T], F32))
        self.parts = ctx.enter_context(self.nc.sbuf_tensor("gated_parts", [P, 2, CH], F32))

    def load(self, sp, f, first):
        if not first:
            self.kit.hold(sp, self.right, f * 3)
        for b in range(2):
            sp.dma_start(self.gates[:, b], self.mix[f + (J_GATE + KT * b)]).then_inc(self.loaded, 16)

    def scalar(self, act, a, out):
        return self.nc.scalar.activation(out, a, ACT.Copy)

    def vector(self, dve, f, n, c, a, b, act_out, g32):
        toks = slice(c * CH, (c + 1) * CH)
        if c == 0:
            dve.wait_ge(self.loaded, (f + 1) * 32)
        self.nc.vector.tensor_tensor(self.parts[:, 0], act_out, self.gates[:, 0, toks], ALU.mult).then_inc(self.left, 1)
        self.nc.vector.tensor_tensor(self.parts[:, 1], b, self.gates[:, 1, toks], ALU.mult).then_inc(self.right, 1)
        dve.wait_ge(self.left, n + 1)
        dve.wait_ge(self.right, n + 1)
        return self.nc.vector.tensor_tensor(g32, self.parts[:, 0], self.parts[:, 1], ALU.add)


def merge(kit, mix, branches, x_saved):
    nc = kit.nc
    loaded = kit.sem("branches_loaded")
    with ExitStack() as ctx:
        halves = [[ctx.enter_context(nc.sbuf_tensor(f"branch{b}_{q}", [P, CT, T], F32R)) for q in range(2)]
                  for b in range(2)]
        with nc.Block() as block:
            @block.sync
            def _(sp):
                for k in range(KT):
                    sp.dma_start(kit.x[:, k], x_saved[k]).then_inc(loaded, 16)
                for b in range(2):
                    for q in range(2):
                        sp.dma_start(halves[b][q][:].bitcast(F32), branches[b][q].rearrange("c p t -> p c t")).then_inc(loaded, 16)
                sp.wait_ge(loaded, 16 * (KT + 4))
        hidden_stage(kit, "merge", KT, CT, (kit.dram["w_rwkv"], kit.dram["w_fourier"]), kit.dram["w_out"],
                     None, halves, Merge(kit, mix), 1)


def final_norm(kit, out):
    nc = kit.nc
    s = {q: kit.sem("fn_" + q) for q in ("squared", "summed", "rooted", "inverted", "normed", "scaled", "stored")}
    with ExitStack() as ctx:
        buf = lambda name, shape: ctx.enter_context(nc.sbuf_tensor(name, shape, F32))
        sq, inv, y = buf("fn_square", [P, 2, CH]), buf("fn_inv", [P, 2, NC, CH]), buf("fn_y", [P, KT, T])
        block = ctx.enter_context(nc.Block())
        at = lambda a, k, c: a[:, k, c * CH:(c + 1) * CH]

        @block.scalar
        def _(act):
            for m in range(NC * KT):
                c, k = divmod(m, KT)
                if m >= 2:
                    act.wait_ge(s["summed"], m - 1)
                nc.scalar.activation(sq[:, m % 2], at(kit.x, k, c), ACT.Square).then_inc(s["squared"], 1)
                if k == KT - 1:
                    act.wait_ge(s["summed"], m + 1)
                    nc.scalar.activation(inv[:, 0, c], kit.banks[c][:, 0:CH], ACT.Sqrt, scale=1.0 / D,
                                         bias=kit.eps[:, 0:1]).then_inc(s["rooted"], 1)
            for m in range(NC * KT):
                c, k = divmod(m, KT)
                act.wait_ge(s["normed"], m + 1)
                nc.scalar.activation(at(y, k, c), at(y, k, c), ACT.Copy,
                                     scale=kit.col("final_norm", k)).then_inc(s["scaled"], 1)

        @block.tensor
        def _(pe):
            for m in range(NC * KT):
                c, k = divmod(m, KT)
                pe.wait_ge(s["squared"], m + 1)
                nc.tensor.matmul(kit.banks[c][:, 0:CH], kit.ones[:], sq[:, m % 2], start=(k == 0),
                                 stop=(k == KT - 1)).then_inc(s["summed"], 1)

        @block.vector
        def _(dve):
            for c in range(NC):
                dve.wait_ge(s["rooted"], c + 1)
                nc.vector.reciprocal(inv[:, 1, c], inv[:, 0, c]).then_inc(s["inverted"], 1)
                dve.wait_ge(s["inverted"], c + 1)
                for k in range(KT):
                    nc.vector.tensor_tensor(at(y, k, c), at(kit.x, k, c), inv[:, 1, c], ALU.mult).then_inc(s["normed"], 1)

        @block.sync
        def _(sp):
            for m in range(NC * KT):
                c, k = divmod(m, KT)
                sp.wait_ge(s["scaled"], m + 1)
                sp.dma_start(out[k][:, c * CH:(c + 1) * CH], at(y, k, c)).then_inc(s["stored"], 16)
            sp.wait_ge(s["stored"], 16 * NC * KT)


def program(nc, dram, y_out, states_out):
    scratch = lambda name, shape, dt=F32: nc.dram_tensor(name, shape, dt).ap()
    mix, keys = scratch("mix", (J_END, P, T)), scratch("keys", (CT, P, T))
    x_saved = scratch("x_saved", (KT, P, T))
    branches = [scratch(f"branch_{b}", (2, CT, P, T)) for b in ("rwkv", "fourier")]
    with ExitStack() as ctx:
        kit = Kit(nc, ctx, dram)
        with ExitStack() as first:
            with_x(kit, first)
            with kit.stage():
                modulation(kit)
            with kit.stage():
                ffn(kit, "ffn1", 0, "ffn1_w13", "ffn1_w2")
            with kit.stage():
                projection(kit, mix, x_saved)
        with ExitStack() as mixer:
            with kit.stage():
                cst = Constants(kit, mixer)
            with kit.stage():
                unit_keys(kit, mix, keys, cst)
            with ExitStack() as rwkv:
                o = rwkv.enter_context(nc.sbuf_tensor("o", [P, CT, T], F32))
                kd_sum = rwkv.enter_context(nc.sbuf_tensor("kd_sum", [P, CT, T], F32))
                with kit.stage():
                    scans(kit, cst, mix, keys, o, kd_sum, dram["states"], states_out)
                with kit.stage():
                    head_norm(kit, cst, mix, o, kd_sum, branches[0])
            with kit.stage():
                fourier(kit, mix, branches[1])
        with ExitStack() as last:
            with_x(kit, last)
            with kit.stage():
                merge(kit, mix, branches, x_saved)
            with kit.stage():
                ffn(kit, "ffn2", 2, "ffn2_w13", "ffn2_w2")
            with kit.stage():
                final_norm(kit, y_out)


def mask_array():
    s, t = np.arange(P)[:, None], np.arange(P)[None, :]
    out = np.zeros((P, 2, 10, P), np.float32)
    for d in range(2):
        strict = (s // CK == t // CK) & ((s < t) if d == 0 else (s > t))
        incl = strict | (s == t)
        out[:, d, 0] = out[:, d, 2] = strict
        out[:, d, 1] = out[:, d, 3] = incl
        for l in range(6):
            m = 1 << l
            out[:, d, 4 + l] = strict & (s // (2 * m) == t // (2 * m)) & (s // m != t // m)
    return out


def reset_array():
    t = np.arange(T)
    return np.broadcast_to(np.stack([t % CK != 0, t % CK != CK - 1]), (P, 2, T)).astype(np.float32)


def dft_arrays():
    def parts(angle, n, sign):
        return np.stack([np.cos(angle), sign * np.sin(angle)], 1).astype(np.float64) / np.sqrt(n)
    j = np.arange(FD)
    features = parts(2 * np.pi * (np.outer(j, j) % FD) / FD, FD, 1).reshape(FD, 2 * FD)
    t = np.arange(T_CTX)
    context = parts(2 * np.pi * (np.outer(t, t) % T_CTX) / T_CTX, T_CTX, -1)
    wide, rows = 64, T_LAT // 64
    r, c = np.divmod(np.arange(T_LAT), wide)
    turns = (np.outer(r, r) % rows) / rows + (np.outer(c, c) % wide) / wide
    latents = parts(2 * np.pi * turns, T_LAT, -1).reshape(T_LAT // P, P, 2, T_LAT).transpose(0, 2, 1, 3)
    return [a.astype(np.float32) for a in (features, context, latents)]


def up_tiles(w, n):
    k = w.shape[0] // P
    return w.reshape(k, P, n, P).transpose(2, 1, 0, 3).reshape(n, P, k * P)


def kernel(x_prompt, x_sample, state_rwkv_fwd, state_rwkv_bwd, c, c_ctx, ada_w, ada_b, norm_w, ffn1_w13, ffn1_w2,
           ffn2_w13, ffn2_w2, w_in, gate_b, conv_rkv, w0, w_up, a0, a_up, g_up, k_k, k_a, r_k, lnx_w, lnx_b,
           w_o_rwkv, w_fourier, w_out, final_norm):
    import concourse.bacc as bacc
    from concourse.bass_utils import run_bass_kernel_spmd

    a = np.asarray
    vectors = dict(ada_b=ada_b, norm_w=norm_w, final_norm=final_norm, gate_b=gate_b, conv=conv_rkv, w0=w0, a0=a0,
                   k_k=k_k, k_a=k_a, r_k=r_k, lnx_w=lnx_w, lnx_b=lnx_b)
    rows = [a(vectors[n]).reshape(-1, P) for n in PACK if n != "c"] + [a(c_ctx).reshape(-1, P), a(c).reshape(-1, P)]
    features, context, latents = dft_arrays()
    pair_ones = np.kron(np.eye(2, dtype=np.float32), np.ones((HD, HD), np.float32))

    def w13(w):
        w = a(w)[0]
        return np.stack([up_tiles(w[:, :F_TILES * P], F_TILES), up_tiles(w[:, F_TILES * P:], F_TILES)])

    def states(s):
        return a(s).reshape(CT, 2, HD, HD).transpose(1, 3, 0, 2).reshape(P, CT, HD)
    arrays = {
        "vec": np.concatenate(rows, 0).T,
        "xT": np.concatenate([a(x_prompt)[0], a(x_sample)[0]], 0).T.reshape(KT, P, T),
        "ada_w": a(ada_w)[0].reshape(KT, P, 36, 2, P).transpose(2, 1, 3, 0, 4),
        "ffn1_w13": w13(ffn1_w13), "ffn1_w2": a(ffn1_w2)[0].reshape(F_TILES, P, D),
        "ffn2_w13": w13(ffn2_w13), "ffn2_w2": a(ffn2_w2)[0].reshape(F_TILES, P, D),
        "w_in": up_tiles(a(w_in)[0], J_END),
        "lora_up": np.stack([a(w_up)[0].reshape(P, W), a(a_up)[0].reshape(P, W)], 1),
        "g_up": a(g_up)[0], "states": np.stack([states(state_rwkv_fwd), states(state_rwkv_bwd)]),
        "w_rwkv": up_tiles(a(w_o_rwkv)[0], KT), "w_fourier": up_tiles(a(w_fourier)[0], KT),
        "w_out": a(w_out)[0].reshape(KT, P, D),
        "masks": mask_array(), "reset": reset_array(), "squares": np.stack([np.eye(P, dtype=np.float32), pair_ones], 1),
        "dft_features": features, "dft_context": context, "dft_latents": latents,
    }
    arrays = {n: np.ascontiguousarray(v) for n, v in arrays.items()}
    nc = bacc.Bacc("TRN2", target_bir_lowering=False, num_devices=1)
    dram = {n: nc.dram_tensor("in_" + n, v.shape, F32, kind="ExternalInput").ap() for n, v in arrays.items()}
    y_out = nc.dram_tensor("out_y", (KT, P, T), F32, kind="ExternalOutput").ap()
    s_out = nc.dram_tensor("out_states", (2, P, CT, HD), F32, kind="ExternalOutput").ap()
    program(nc, dram, y_out, s_out)
    got = run_bass_kernel_spmd(nc, [{"in_" + n: v for n, v in arrays.items()}], core_ids=[0]).results[0]
    y = got["out_y"].reshape(D, T).T
    s = got["out_states"].reshape(2, 2, HD, CT, HD).transpose(0, 3, 1, 4, 2).reshape(2, 1, 1, HEADS, HD, HD)
    return (np.ascontiguousarray(y[None, :T_CTX]), np.ascontiguousarray(y[None, T_CTX:]),
            np.ascontiguousarray(s[0]), np.ascontiguousarray(s[1]))
```

```python
from contextlib import ExitStack, contextmanager

import numpy as np

import concourse.bass as bass
from concourse import mybir

ALU = mybir.AluOpType
ACT = mybir.ActivationFunctionType
F32 = mybir.dt.float32
F32R = mybir.dt.float32r

P = 128
D = 1024
KT = D // P
T_CTX = 128
T_LAT = 1024
T = T_CTX + T_LAT
CH = 384
NC = T // CH
F_TILES = 2816 // P
HEADS, HD = 8, 64
W = HEADS * HD
CT = W // P
CK = 64
FG, FD = 4, 128
LORA = 64
NTT = T // P
NORM_EPS = 1e-6
GN_EPS = 64e-5
DECAY_SCALE = float(np.exp(-0.5))
J_WD, J_AD, J_GD, J_F, J_GATE = 12, 13, 14, 15, 19
J_END = 35

PACK = {}
_at = 0
for _name, _n in (("ada_b", 72), ("norm_w", 24), ("final_norm", 8), ("gate_b", 16), ("conv", 36),
                  ("w0", 8), ("a0", 8), ("k_k", 4), ("k_a", 4), ("r_k", 4), ("lnx_w", 4),
                  ("lnx_b", 4), ("c", 16)):
    PACK[_name] = (_at, _n)
    _at += _n
PACK_W = _at


def segments(c):
    return [(0, 0, T_CTX), (1, T_CTX, CH)] if c == 0 else [(1, 0, CH)]


class Kit:

    def __init__(self, nc, ctx, dram):
        self.nc, self.ctx, self.dram = nc, ctx, dram
        self.banks = [ctx.enter_context(nc.psum_tensor(f"bank{b}", [P, 512], F32)) for b in range(8)]
        self.x = self.resident("x", [P, KT, T])
        self.vec = self.resident("vec", [P, PACK_W])
        self.mod = self.resident("mod", [P, 9, KT, 2])
        self.scale = self.resident("scale", [P, 3, KT, 2])
        self.gate = self.resident("gate", [P, 3, KT, 2])
        self.ones = self.resident("ones", [P, P])
        self.eps = self.resident("eps", [P, 2])
        self.passed = nc.alloc_semaphore("passed")

    def resident(self, name, shape, dt=F32):
        return self.ctx.enter_context(self.nc.sbuf_tensor(name, shape, dt))

    def sem(self, name):
        s = self.nc.alloc_semaphore(name)
        self.stage_sems.append(s)
        return s

    @contextmanager
    def stage(self):
        self.stage_sems = []
        yield
        self.nc.clear_and_free_semaphores(self.stage_sems)
        self.nc.all_engine_barrier()

    def col(self, name, i=0, n=1):
        a = PACK[name][0]
        return self.vec[:, a + i:a + i + n]

    def hold(self, eng, sem, value):
        eng.wait_ge(sem, value)
        eng.sem_inc(self.passed, 1)


def modulation(kit):
    nc = kit.nc
    loaded_vec, loaded_x, loaded_select = kit.sem("vec_loaded"), kit.sem("x_loaded"), kit.sem("select_loaded")
    loaded = [[kit.sem(f"ada_loaded{p}{g}") for g in range(4)] for p in range(2)]
    cleared, silu_ready, ones_ready = kit.sem("cond_cleared"), kit.sem("silu_ready"), kit.sem("ones_ready")
    rows_done, rows_ready, turned = kit.sem("mod_rows_done"), kit.sem("mod_rows_ready"), kit.sem("mod_turned")
    section_added, section_done = kit.sem("section_added"), kit.sem("section_done")
    HALF = D // 2
    with ExitStack() as ctx:
        raw = ctx.enter_context(nc.sbuf_tensor("ada_raw", [P, 2, 4, 2, D], F32))
        cs = ctx.enter_context(nc.sbuf_tensor("cond_silu", [P, KT, 32], F32))
        rows = ctx.enter_context(nc.sbuf_tensor("mod_rows", [P, 2, 2, HALF], F32))
        select = ctx.enter_context(nc.sbuf_tensor("select", [P, 2], F32))
        block = ctx.enter_context(nc.Block())

        @block.sync
        def _(sp):
            sp.dma_start(kit.vec[:], kit.dram["vec"]).then_inc(loaded_vec, 16)

            def section(i, par, first=False):
                if not first:
                    kit.hold(sp, rows_done, i * 2 - 2)
                for g in range(4):
                    sp.dma_start(raw[:, par, g], kit.dram["ada_w"][i, g]).then_inc(loaded[par][g], 16)
            section(0, 0, True)
            sp.dma_start(select[:], kit.dram["select"]).then_inc(loaded_select, 16)
            section(1, 1, True)
            for k in range(KT):
                sp.dma_start(kit.x[:, k, :], kit.dram["xT"][k]).then_inc(loaded_x, 16)
            section(2, 0)
            with sp.Fori(1, 4) as i:
                for par in range(2):
                    section(i * 2 + (1 + par), 1 - par)
            sp.wait_ge(loaded_x, 16 * KT)

        @block.gpsimd
        def _(pool):
            pool.memset(cs[:], 0.0).then_inc(cleared, 1)
            pool.memset(kit.ones[:], 1.0).then_inc(ones_ready, 1)
            pool.memset(kit.eps[:, 0:1], NORM_EPS).then_inc(ones_ready, 1)
            pool.memset(kit.eps[:, 1:2], GN_EPS).then_inc(ones_ready, 1)

        @block.scalar
        def _(act):
            act.wait_ge(loaded_vec, 16)
            act.wait_ge(cleared, 1)
            a = PACK["c"][0]
            for cond in range(2):
                nc.scalar.activation(cs[:, :, cond], kit.vec[:, a + 8 * cond:a + 8 * cond + 8],
                                     ACT.Silu).then_inc(silu_ready, 1)

            def section(i, par, first=False):
                for half in range(2):
                    act.wait_ge(rows_done, i * 2 + (half + 1))
                    if not first and half == 0:
                        act.wait_ge(turned, i - 1)
                    nc.scalar.activation(rows[:, par, half], kit.banks[2 * par + half][:], ACT.Copy)\
                        .then_inc(rows_ready, 1)
            section(0, 0, True)
            section(1, 1, True)
            section(2, 0)
            with act.Fori(1, 4) as i:
                for par in range(2):
                    section(i * 2 + (1 + par), 1 - par)

        @block.tensor
        def _(pe):
            pe.wait_ge(silu_ready, 2)

            def section(i, rank, par, first=False):
                for g in range(4):
                    pe.wait_ge(loaded[par][g], (rank + 1) * 16)
                if not first:
                    pe.wait_ge(rows_ready, i * 2 - 2)
                for half in range(2):
                    for kk in range(2):
                        for g in range(4):
                            mm = nc.tensor.matmul(kit.banks[2 * par + half][32 * g:32 * g + 32, :],
                                                  cs[:, 2 * g + kk, :],
                                                  raw[:, par, g, kk, half * HALF:(half + 1) * HALF],
                                                  start=(kk == 0), stop=(kk == 1))
                    mm.then_inc(rows_done, 1)

            def turn(i, par, early=False):
                pe.wait_ge(rows_ready, i * 2 + 2)
                if not early:
                    pe.wait_ge(section_added, i - 1)
                for mt in range(KT):
                    mm = nc.tensor.matmul(kit.banks[4 + par][:, 2 * mt:2 * mt + 2],
                                          rows[:, par, mt // 4, (mt % 4) * P:(mt % 4 + 1) * P], select[:],
                                          start=True, stop=True)
                mm.then_inc(turned, 1)
            section(0, 0, 0, True)
            pe.wait_ge(loaded_select, 16)
            section(1, 0, 1, True)
            turn(0, 0, True)
            section(2, 1, 0)
            turn(1, 1, True)
            with pe.Fori(1, 4) as i:
                section(i * 2 + 1, i, 1)
                turn(i * 2, 0)
                section(i * 2 + 2, i + 1, 0)
                turn(i * 2 + 1, 1)
            turn(8, 0)

        @block.vector
        def _(dve):
            dve.wait_ge(loaded_vec, 16)
            a = PACK["ada_b"][0]
            for i in range(9):
                dve.wait_ge(turned, i + 1)
                nc.vector.tensor_tensor(kit.mod[:, i], kit.banks[4 + i % 2][:, 0:2 * KT].rearrange("p (m c) -> p m c", c=2),
                                        kit.vec[:, a + i * KT:a + (i + 1) * KT].rearrange("p (m c) -> p m c", c=1)
                                        .broadcast_to([P, KT, 2]), ALU.add).then_inc(section_added, 1)
            dve.wait_ge(section_added, 9)
            a = PACK["norm_w"][0]
            for n in range(3):
                for cond in range(2):
                    ins = nc.vector.scalar_tensor_tensor(
                        kit.scale[:, n, :, cond], kit.mod[:, 3 * n + 1, :, cond], 1.0,
                        kit.vec[:, a + 8 * n:a + 8 * n + 8], ALU.add, ALU.mult)
                ins = nc.vector.tensor_scalar(kit.gate[:, n], kit.mod[:, 3 * n + 2],
                                              1.0 if n == 1 else 0.5, None, ALU.mult)
            ins.then_inc(section_done, 1)
            dve.wait_ge(section_done, 1)


class Norm:

    def __init__(self, kit, ctx, n, h_hi, h_lo):
        self.kit, self.n, self.h_hi, self.h_lo = kit, n, h_hi, h_lo
        buf = lambda name, shape: ctx.enter_context(kit.nc.sbuf_tensor(f"{name}_n{n}", shape, F32))
        self.sq = buf("square", [P, 3, 2, CH])
        self.rms = buf("rms", [P, CH])
        self.inv = buf("inv_rms", [P, 2, CH])
        self.xn = buf("x_normed", [P, 2, CH])
        self.full = buf("h_full", [P, 2, CH])
        self.sq_ready = [kit.sem(f"sq_ready_{o}_n{n}") for o in ("act", "dve", "pool")]
        (self.stat_done, self.rms_ready, self.inv_ready, self.xn_ready, self.hi_ready, self.full_ready,
         self.h_ready) = (kit.sem(f"{s}_n{n}") for s in (
             "stat_done", "rms_ready", "inv_ready", "xn_ready", "hi_ready", "full_ready", "h_ready"))
        self.order = [(0, k, k % 2) for k in range(KT)] + [(1, k, 2) for k in range(KT)] + [(2, k, 0) for k in range(KT)]

    def at(self, buf, k, c):
        return buf[:, k, c * CH:(c + 1) * CH]

    def squares(self, owner, eng, c, only=None):
        nc = self.kit.nc
        mine = [m for m, (_, _, o) in enumerate(self.order) if o == owner]
        for i, m in enumerate(mine):
            if self.order[m][0] != c or only not in (None, self.order[m][1]):
                continue
            k = self.order[m][1]
            if i >= 2:
                eng.wait_ge(self.stat_done, mine[i - 2] + 1)
            out, src = self.sq[:, owner, i % 2], self.at(self.kit.x, k, c)
            if owner == 0:
                ins = nc.scalar.activation(out, src, ACT.Square)
            elif owner == 1:
                ins = nc.vector.tensor_tensor(out, src, src, ALU.mult)
            else:
                ins = nc.gpsimd.tensor_tensor(out, src, src, ALU.mult)
            ins.then_inc(self.sq_ready[owner], 1)

    def tensor(self, pe):
        nc, kit = self.kit.nc, self.kit
        count = [0, 0, 0]
        for c, k, owner in self.order:
            pe.wait_ge(self.sq_ready[owner], count[owner] + 1)
            nc.tensor.matmul(kit.banks[4 + c][:, 0:CH], kit.ones[:], self.sq[:, owner, count[owner] % 2],
                             start=(k == 0), stop=(k == KT - 1)).then_inc(self.stat_done, 1)
            count[owner] += 1

    def scalar(self, act, split_weights):
        nc, kit = self.kit.nc, self.kit

        def root(c):
            act.wait_ge(self.stat_done, KT * (c + 1))
            if c:
                act.wait_ge(self.inv_ready, c)
            nc.scalar.activation(self.rms[:], kit.banks[4 + c][:, 0:CH], ACT.Sqrt, scale=1.0 / D,
                                 bias=kit.eps[:, 0:1]).then_inc(self.rms_ready, 1)
        self.squares(0, act, 0)
        split_weights()
        root(0)
        for m in range(NC * KT):
            c, k = divmod(m, KT)
            if k == 0 and c:
                root(c)
            act.wait_ge(self.xn_ready, m + 1)
            for cond, a, b in segments(c):
                ins = nc.scalar.activation(self.at(self.h_hi, k, c)[:, a:b], self.xn[:, m % 2, a:b], ACT.Identity,
                                           bias=kit.mod[:, 3 * self.n, k, cond:cond + 1],
                                           scale=kit.scale[:, self.n, k, cond:cond + 1])
            ins.then_inc(self.hi_ready, 1)
            if c == 0:
                self.squares(0, act, 2, k)

    def pool(self, pool):
        nc, kit = self.kit.nc, self.kit
        self.squares(2, pool, 1)
        for m in range(NC * KT):
            c, k = divmod(m, KT)
            pool.wait_ge(self.xn_ready, m + 1)
            if m >= 2:
                pool.wait_ge(self.h_ready, m - 1)
            for cond, a, b in segments(c):
                ins = nc.gpsimd.tensor_scalar(self.full[:, m % 2, a:b], self.xn[:, m % 2, a:b],
                                              kit.scale[:, self.n, k, cond:cond + 1],
                                              kit.mod[:, 3 * self.n, k, cond:cond + 1], ALU.mult, ALU.add)
            ins.then_inc(self.full_ready, 1)

    def vector(self, dve, split_weights):
        nc, kit = self.kit.nc, self.kit

        def low(m):
            c, k = divmod(m, KT)
            dve.wait_ge(self.hi_ready, m + 1)
            dve.wait_ge(self.full_ready, m + 1)
            nc.vector.tensor_tensor(self.at(self.h_lo, k, c), self.full[:, m % 2],
                                    self.at(self.h_hi, k, c).bitcast(F32), ALU.subtract).then_inc(self.h_ready, 1)
        self.squares(1, dve, 0)
        split_weights()
        for m in range(NC * KT):
            c, k = divmod(m, KT)
            if k == 0:
                if c:
                    low(m - 1)
                dve.wait_ge(self.rms_ready, c + 1)
                nc.vector.reciprocal(self.inv[:, c % 2], self.rms[:]).then_inc(self.inv_ready, 1)
                dve.wait_ge(self.inv_ready, c + 1)
            if m >= 2:
                dve.wait_ge(self.hi_ready, m - 1)
                dve.wait_ge(self.full_ready, m - 1)
            nc.vector.tensor_tensor(self.xn[:, m % 2], self.at(kit.x, k, c), self.inv[:, c % 2],
                                    ALU.mult).then_inc(self.xn_ready, 1)
            if k:
                low(m - 1)
        low(NC * KT - 1)


def hidden_stage(kit, tag, tiles, ku, w_up, w_down, norm, moving, combine, gate, load_x=None):
    nc = kit.nc
    kinds = ("a", "b", "d")
    loaded = {q: kit.sem(f"w{q}_loaded_{tag}") for q in kinds}
    w_hi_ready = {q: kit.sem(f"w{q}_hi_ready_{tag}") for q in kinds}
    w_ready = {q: kit.sem(f"w{q}_ready_{tag}") for q in kinds}
    up_done, act_ready = kit.sem(f"up_done_{tag}"), kit.sem(f"act_ready_{tag}")
    g32_ready, g_hi_ready, g_ready = (kit.sem(f"{s}_{tag}") for s in ("g32_ready", "g_hi_ready", "g_ready"))
    x_loaded = kit.sem(f"x_loaded_{tag}")
    down_done, x_added = kit.sem(f"down_done_{tag}"), kit.sem(f"x_added_{tag}")
    with ExitStack() as ctx:
        buf = lambda name, shape, dt=F32: ctx.enter_context(nc.sbuf_tensor(f"{name}_{tag}", shape, dt))
        width = {"a": ku * P, "b": ku * P, "d": D}
        raw = {q: buf(f"raw_{q}", [P, width[q]]) for q in kinds}
        whi = {q: buf(f"whi_{q}", [P, 2, width[q]], F32R) for q in kinds}
        wlo = {q: buf(f"wlo_{q}", [P, 2, width[q]], F32R) for q in kinds}
        g_hi, g_lo = buf("g_hi", [P, NC, CH], F32R), buf("g_lo", [P, NC, CH], F32R)
        act_out, g32 = buf("act_out", [P, 2, CH]), buf("g32", [P, 2, CH])
        norm_part, moving = (norm(ctx), None) if norm else (None, moving)
        if norm_part:
            moving = [(norm_part.h_hi, norm_part.h_lo)] * 2
        combine.setup(ctx)
        block = ctx.enter_context(nc.Block())
        source = {"a": w_up[0], "b": w_up[1], "d": w_down}

        @block.sync
        def _(sp):
            def load(q, f, first=False):
                if not first:
                    kit.hold(sp, w_ready[q], f)
                if q == "d":
                    combine.load(sp, f, first)
                sp.dma_start(raw[q][:], source[q][f]).then_inc(loaded[q], 16)
            for q in kinds:
                load(q, 0, True)
            if load_x:
                load_x(sp, x_loaded)
            with sp.Fori(1, tiles) as f:
                for q in kinds:
                    load(q, f)

        @block.scalar
        def _(act):
            def high(q, f, slot, first=False):
                act.wait_ge(loaded[q], (f + 1) * 16)
                if not first:
                    act.wait_ge(*((down_done, (f - 1) * 24) if q == "d" else (up_done, (f - 1) * 3)))
                nc.scalar.activation(whi[q][:, slot], raw[q][:], ACT.Copy).then_inc(w_hi_ready[q], 1)

            def step(f, c, par, early, last):
                n = f * 3 + c
                act.wait_ge(up_done, n + 1)
                if not (early and par == 0 and c < 2):
                    act.wait_ge(g32_ready, n - 1)
                slot = (3 * par + c) % 2
                combine.scalar(act, kit.banks[2 * slot][:, 0:CH], act_out[:, slot]).then_inc(act_ready, 1)
                act.wait_ge(g32_ready, n + 1)
                if not (early and par == 0):
                    act.wait_ge(down_done, (n - 2) * 8)
                nc.scalar.activation(g_hi[:, c], g32[:, slot], ACT.Copy).then_inc(g_hi_ready, 1)
                if not last:
                    high(kinds[c], f + 1, 1 - par, early and par == 0)

            def first_weights():
                for q in kinds:
                    high(q, 0, 0, True)
            if norm_part:
                norm_part.scalar(act, first_weights)
            else:
                first_weights()

            def pair(i, early=False, last=False):
                for par in range(2):
                    for c in range(NC):
                        step(i * 2 + par, c, par, early, last and par == 1)
            pair(0, early=True)
            with act.Fori(1, tiles // 2 - 1) as i:
                pair(i)
            pair(tiles // 2 - 1, last=True)

        @block.vector
        def _(dve):
            def low(q, f, slot):
                dve.wait_ge(w_hi_ready[q], f + 1)
                nc.vector.tensor_tensor(wlo[q][:, slot], raw[q][:], whi[q][:, slot].bitcast(F32),
                                        ALU.subtract).then_inc(w_ready[q], 1)

            def add_to_x(n, c):
                for d in range(KT):
                    m = n * 8 + d
                    dve.wait_ge(down_done, m + 1)
                    for cond, a, b in segments(c):
                        xs = kit.x[:, d, c * CH + a:c * CH + b]
                        ins = nc.vector.scalar_tensor_tensor(xs, kit.banks[4 + d % 4][:, a:b],
                                                             kit.gate[:, gate, d, cond:cond + 1], xs,
                                                             ALU.mult, ALU.add)
                    ins.then_inc(x_added, 1)

            def step(f, c, par, early, last):
                n = f * 3 + c
                slot = (3 * par + c) % 2
                dve.wait_ge(act_ready, n + 1)
                if not (early and par == 0 and c < 2):
                    dve.wait_ge(g_ready, n - 1)
                combine.vector(dve, f, n, c, kit.banks[2 * slot][:, 0:CH], kit.banks[2 * slot + 1][:, 0:CH],
                               act_out[:, slot], g32[:, slot]).then_inc(g32_ready, 1)
                if load_x and early and par == 0 and c == 1:
                    dve.wait_ge(x_loaded, 16 * KT)
                if not (early and par == 0 and c == 0):
                    add_to_x(n - 1, (c - 1) % NC)
                dve.wait_ge(g_hi_ready, n + 1)
                nc.vector.tensor_tensor(g_lo[:, c], g32[:, slot], g_hi[:, c].bitcast(F32),
                                        ALU.subtract).then_inc(g_ready, 1)
                if not last:
                    low(kinds[c], f + 1, 1 - par)

            def first_weights():
                for q in kinds:
                    low(q, 0, 0)
            if norm_part:
                norm_part.vector(dve, first_weights)
            else:
                first_weights()

            def pair(i, early=False, last=False):
                for par in range(2):
                    for c in range(NC):
                        step(i * 2 + par, c, par, early, last and par == 1)
            pair(0, early=True)
            with dve.Fori(1, tiles // 2 - 1) as i:
                pair(i)
            pair(tiles // 2 - 1, last=True)
            add_to_x(tiles * 3 - 1, NC - 1)
            dve.wait_ge(x_added, tiles * 24)

        if norm_part:
            @block.gpsimd
            def _(pool):
                norm_part.pool(pool)

        @block.tensor
        def _(pe):
            if norm_part:
                norm_part.tensor(pe)

            def up(f, c, par, early):
                n = f * 3 + c
                slot = (3 * par + c) % 2
                if norm_part and early and par == 0:
                    pe.wait_ge(norm_part.h_ready, KT * (c + 1))
                if c == 0:
                    pe.wait_ge(w_ready["a"], f + 1)
                    pe.wait_ge(w_ready["b"], f + 1)
                if not (early and par == 0 and c < 2):
                    pe.wait_ge(g32_ready, n - 1)
                for j, q in enumerate("ab"):
                    hi, lo = moving[j]
                    for k in range(ku):
                        cols, toks = slice(k * P, (k + 1) * P), slice(c * CH, (c + 1) * CH)
                        for m, (w, v) in enumerate(((wlo, hi), (whi, lo), (whi, hi))):
                            mm = nc.tensor.matmul(kit.banks[2 * slot + j][:, 0:CH], w[q][:, par, cols],
                                                  v[:, k, toks], start=(k == 0 and m == 0),
                                                  stop=(k == ku - 1 and m == 2))
                mm.then_inc(up_done, 1)


            def step(f, c, par, early):
                up(f, c, par, early)
                if early and par == 0 and c == 0:
                    return
                if c == 1:
                    pe.wait_ge(w_ready["d"], f + 1)
                prev_c = (c - 1) % NC
                down_of(f * 3 + c - 1, prev_c, par if c else 1 - par, early and par == 0 and c == 1)

            def down_of(n, c, par, first):
                pe.wait_ge(g_ready, n + 1)
                for d in range(KT):
                    if not (first and d < 4):
                        pe.wait_ge(x_added, n * 8 + d - 3)
                    cols = slice(d * P, (d + 1) * P)
                    for m, (w, v) in enumerate(((wlo, g_hi), (whi, g_lo), (whi, g_hi))):
                        mm = nc.tensor.matmul(kit.banks[4 + d % 4][:, 0:CH], w["d"][:, par, cols], v[:, c],
                                              start=(m == 0), stop=(m == 2))
                    mm.then_inc(down_done, 1)

            for par in range(2):
                for c in range(NC):
                    step(par, c, par, True)
            with pe.Fori(1, tiles // 2) as i:
                for par in range(2):
                    for c in range(NC):
                        step(i * 2 + par, c, par, False)
            down_of(tiles * 3 - 1, NC - 1, 1, False)


class SwiGLU:

    def __init__(self, nc):
        self.nc = nc

    def setup(self, ctx):
        pass

    def load(self, sp, f, first):
        pass

    def scalar(self, act, a, out):
        return self.nc.scalar.activation(out, a, ACT.Silu)

    def vector(self, dve, f, n, c, a, b, act_out, g32):
        return self.nc.vector.tensor_tensor(g32, act_out, b, ALU.mult)


def ffn(kit, tag, n, w13, w2):
    def norm(ctx):
        h_hi = ctx.enter_context(kit.nc.sbuf_tensor(f"h_hi_{tag}", [P, KT, T], F32R))
        h_lo = ctx.enter_context(kit.nc.sbuf_tensor(f"h_lo_{tag}", [P, KT, T], F32R))
        return Norm(kit, ctx, n, h_hi, h_lo)
    hidden_stage(kit, tag, F_TILES, KT, (kit.dram[w13][0], kit.dram[w13][1]), kit.dram[w2], norm, None,
                 SwiGLU(kit.nc), n)


def projection(kit, mix, x_saved):
    nc = kit.nc
    saved = kit.sem("x_saved")
    loaded, w_hi_ready, w_ready = kit.sem("win_loaded"), kit.sem("win_hi_ready"), kit.sem("win_ready")
    proj_done, evicted = kit.sem("proj_done"), kit.sem("proj_evicted")
    pads_ready, tap_done, row_ready = (kit.sem(s) for s in ("pads_ready", "tap_done", "row_ready"))
    stored = [kit.sem(f"row_stored{p}") for p in range(2)]
    with ExitStack() as ctx:
        buf = lambda name, shape, dt=F32: ctx.enter_context(nc.sbuf_tensor(name, shape, dt))
        h_hi, h_lo = buf("h_hi_mix", [P, KT, T], F32R), buf("h_lo_mix", [P, KT, T], F32R)
        norm = Norm(kit, ctx, 1, h_hi, h_lo)
        raw = buf("raw_in", [P, D])
        whi, wlo = buf("whi_in", [P, 2, D], F32R), buf("wlo_in", [P, 2, D], F32R)
        padded = buf("u_padded", [P, 2, T + 4])
        taps = buf("taps", [P, 3])
        row = buf("row_out", [P, 2, T + 4])
        taps_ready = kit.sem("taps_ready")
        block = ctx.enter_context(nc.Block())
        CONV, LORA_, PLAIN, GATE = range(4)

        def kind_of(j):
            return CONV if j < J_WD else LORA_ if j < J_F else PLAIN if j < J_GATE else GATE

        def stored_before(rank):
            if isinstance(rank, int):
                return 32 * min(rank, J_WD // 2) + 16 * max(0, rank - J_WD // 2)
            return rank * 16 + 16 * (J_WD // 2)

        def schedule(eng, step):
            for j in range(2):
                step(j, j, kind_of(j), 0)
            with eng.Fori(1, J_WD // 2) as i:
                for par in range(2):
                    step(i * 2 + par, par, CONV, i)
            for j in range(J_WD, J_GATE + 2):
                step(j, j % 2, kind_of(j), j // 2)
            first = J_GATE + 2
            with eng.Fori(0, (J_END - first) // 2 - 1) as i:
                for o in range(2):
                    step(i * 2 + first + o, (first + o) % 2, GATE, i + (first + o) // 2)
            for j in range(J_END - 2, J_END):
                step(j, j % 2, GATE, j // 2)

        @block.sync
        def _(sp):
            sp.dma_start(raw[:], kit.dram["w_in"][0]).then_inc(loaded, 16)
            for k in range(KT):
                sp.dma_start(x_saved[k], kit.x[:, k]).then_inc(saved, 16)

            def step(j, par, kind, rank):
                if not (isinstance(j, int) and j == J_END - 1):
                    kit.hold(sp, w_ready, j + 1)
                    sp.dma_start(raw[:], kit.dram["w_in"][j + 1]).then_inc(loaded, 16)
                kit.hold(sp, row_ready, j + 1)
                if kind == CONV:
                    sp.dma_start(mix[j][:, 0:T_CTX], row[:, par, 1:T_CTX + 1]).then_inc(stored[par], 16)
                    sp.dma_start(mix[j][:, T_CTX:T], row[:, par, T_CTX + 3:T + 3]).then_inc(stored[par], 16)
                else:
                    sp.dma_start(mix[j], row[:, par, 0:T]).then_inc(stored[par], 16)
            schedule(sp, step)
            for par in range(2):
                sp.wait_ge(stored[par], stored_before((J_END + 1 - par) // 2))
            sp.wait_ge(saved, 16 * KT)

        @block.scalar
        def _(act):
            def high(j, slot, first=False):
                act.wait_ge(loaded, (j + 1) * 16)
                if not first:
                    act.wait_ge(proj_done, (j - 1) * 3)
                nc.scalar.activation(whi[:, slot], raw[:], ACT.Copy).then_inc(w_hi_ready, 1)
            norm.scalar(act, lambda: high(0, 0, True))

            def step(j, par, kind, rank):
                if kind == CONV and not (isinstance(j, int) and j < 2):
                    act.wait_ge(row_ready, j - 1)
                if kind != CONV:
                    act.wait_ge(stored[par], stored_before(rank))
                for c in range(NC):
                    n = j * 3 + c
                    kit.hold(act, proj_done, n + 1)
                    src = kit.banks[3 * par + c]
                    if kind == CONV:
                        for cond, a, b in segments(c):
                            at = c * CH + a + 1 + 2 * cond
                            ins = nc.scalar.activation(padded[:, par, at:at + b - a], src[:, a:b], ACT.Copy)
                    elif kind == LORA_:
                        func = {J_WD: ACT.Tanh, J_AD: ACT.Copy, J_GD: ACT.Sigmoid}[j]
                        ins = nc.scalar.activation(row[:, par, c * CH:(c + 1) * CH], src[:, 0:CH], func)
                    elif kind == PLAIN:
                        ins = nc.scalar.activation(row[:, par, c * CH:(c + 1) * CH], src[:, 0:CH], ACT.Copy)
                    else:
                        g = PACK["gate_b"][0] - J_GATE
                        ins = nc.scalar.activation(row[:, par, c * CH:(c + 1) * CH], src[:, 0:CH], ACT.Sigmoid,
                                                   bias=kit.vec[:, bass.ds(j + g, 1)])
                    ins.then_inc(evicted, 1)
                    if c == 0 and not (isinstance(j, int) and j == J_END - 1):
                        high(j + 1, 1 - par, isinstance(j, int) and j == 0)
            schedule(act, step)

        @block.vector
        def _(dve):
            def low(j, slot):
                dve.wait_ge(w_hi_ready, j + 1)
                nc.vector.tensor_tensor(wlo[:, slot], raw[:], whi[:, slot].bitcast(F32),
                                        ALU.subtract).then_inc(w_ready, 1)
            for par in range(2):
                for a, b in ((0, 1), (T_CTX + 1, T_CTX + 3), (T + 3, T + 4)):
                    nc.vector.memset(padded[:, par, a:b], 0.0).then_inc(pads_ready, 1)
            dve.wait_ge(pads_ready, 6)
            norm.vector(dve, lambda: low(0, 0))
            conv = PACK["conv"][0]

            def step(j, par, kind, rank):
                if not (isinstance(j, int) and j == J_END - 1):
                    low(j + 1, 1 - par)
                if kind != CONV:
                    dve.wait_ge(evicted, j * 3 + 3)
                    dve.sem_inc(row_ready, 1)
                    return
                for t in range(3):
                    ins = nc.vector.tensor_copy(taps[:, t:t + 1], kit.vec[:, bass.ds(j + (conv + 12 * t), 1)])
                ins.then_inc(taps_ready, 1)
                dve.wait_ge(taps_ready, j + 1)
                dve.wait_ge(evicted, j * 3 + 3)
                if not (isinstance(j, int) and j < 2):
                    dve.wait_ge(stored[par], rank * 32)
                out = row[:, par, 1:T + 3]
                nc.vector.tensor_scalar(out, padded[:, par, 0:T + 2], taps[:, 0:1], None, ALU.mult).then_inc(tap_done, 1)
                for t in (1, 2):
                    dve.wait_ge(tap_done, j * 2 + t)
                    ins = nc.vector.scalar_tensor_tensor(out, padded[:, par, t:T + 2 + t], taps[:, t:t + 1], out,
                                                         ALU.mult, ALU.add)
                    ins.then_inc(tap_done if t == 1 else row_ready, 1)
            schedule(dve, step)

        @block.gpsimd
        def _(pool):
            norm.pool(pool)

        @block.tensor
        def _(pe):
            norm.tensor(pe)

            def step(j, par, early=False):
                for c in range(NC):
                    if early and par == 0:
                        pe.wait_ge(norm.h_ready, KT * (c + 1))
                    if c == 0:
                        pe.wait_ge(w_ready, j + 1)
                    if not early:
                        pe.wait_ge(evicted, j * 3 + c - 5)
                    for k in range(KT):
                        cols, toks = slice(k * P, (k + 1) * P), slice(c * CH, (c + 1) * CH)
                        for m, (w, v) in enumerate(((wlo, h_hi), (whi, h_lo), (whi, h_hi))):
                            mm = nc.tensor.matmul(kit.banks[3 * par + c][:, 0:CH], w[:, par, cols], v[:, k, toks],
                                                  start=(k == 0 and m == 0), stop=(k == KT - 1 and m == 2))
                    mm.then_inc(proj_done, 1)
            for j in range(2):
                step(j, j, True)
            with pe.Fori(1, J_END // 2) as i:
                for par in range(2):
                    step(i * 2 + par, par)
            step(J_END - 1, (J_END - 1) % 2)


def unit_keys(kit, mix, keys, cst):
    nc = kit.nc
    s = {q: kit.sem("uk_" + q) for q in ("scaled", "squared", "summed", "rooted", "guarded",
                                         "inverted", "ready", "stored")}
    loaded = [kit.sem(f"uk_loaded{ct}") for ct in range(CT)]
    with ExitStack() as ctx:
        buf = lambda name, shape, dt=F32: ctx.enter_context(nc.sbuf_tensor(name, shape, dt))
        k_raw, kk, sq = (buf(n, [P, CT, T]) for n in ("uk_raw", "uk_scaled", "uk_square"))
        block = ctx.enter_context(nc.Block())

        @block.sync
        def _(sp):
            for ct in range(CT):
                sp.dma_start(k_raw[:, ct], mix[CT + ct]).then_inc(loaded[ct], 16)
            for ct in range(CT):
                sp.wait_ge(s["ready"], NC * (ct + 1))
                sp.dma_start(keys[ct], kk[:, ct]).then_inc(s["stored"], 16)
            sp.wait_ge(s["stored"], 16 * CT)

        @block.scalar
        def _(act):
            for ct in range(CT):
                act.wait_ge(s["scaled"], ct + 1)
                nc.scalar.activation(sq[:, ct], kk[:, ct], ACT.Square).then_inc(s["squared"], 1)
            for m in range(CT * NC):
                ct, c = divmod(m, NC)
                act.wait_ge(s["summed"], m + 1)
                nc.scalar.activation(k_raw[:, ct, c * CH:(c + 1) * CH], kit.banks[m % 8][:, 0:CH],
                                     ACT.Sqrt).then_inc(s["rooted"], 1)

        @block.tensor
        def _(pe):
            for m in range(CT * NC):
                ct, c = divmod(m, NC)
                pe.wait_ge(s["squared"], ct + 1)
                if m >= 8:
                    pe.wait_ge(s["rooted"], m - 7)
                nc.tensor.matmul(kit.banks[m % 8][:, 0:CH], cst.pair_ones, sq[:, ct, c * CH:(c + 1) * CH],
                                 start=True, stop=True).then_inc(s["summed"], 1)

        @block.vector
        def _(dve):
            for ct in range(CT):
                dve.wait_ge(loaded[ct], 16)
                nc.vector.tensor_scalar(kk[:, ct], k_raw[:, ct], kit.col("k_k", ct), None, ALU.mult).then_inc(s["scaled"], 1)
            for m in range(CT * NC):
                ct, c = divmod(m, NC)
                part = slice(c * CH, (c + 1) * CH)
                dve.wait_ge(s["rooted"], m + 1)
                nc.vector.tensor_scalar(k_raw[:, ct, part], k_raw[:, ct, part], 1e-12, None, ALU.max).then_inc(s["guarded"], 1)
                dve.wait_ge(s["guarded"], m + 1)
                nc.vector.reciprocal(sq[:, ct, part], k_raw[:, ct, part]).then_inc(s["inverted"], 1)
                dve.wait_ge(s["inverted"], m + 1)
                nc.vector.tensor_tensor(kk[:, ct, part], kk[:, ct, part], sq[:, ct, part], ALU.mult).then_inc(s["ready"], 1)


class Constants:

    def __init__(self, kit, ctx):
        nc = kit.nc
        self.squares = ctx.enter_context(nc.sbuf_tensor("squares", [P, 2, P], F32))
        self.ident, self.pair_ones = self.squares[:, 0], self.squares[:, 1]
        self.one_minus_ka = ctx.enter_context(nc.sbuf_tensor("one_minus_ka", [P, CT], F32))
        loaded, ready = kit.sem("const_loaded"), kit.sem("const_ready")
        with nc.Block() as block:
            @block.sync
            def _(sp):
                sp.dma_start(self.squares[:], kit.dram["squares"]).then_inc(loaded, 16)
                sp.wait_ge(loaded, 16)

            @block.vector
            def _(dve):
                nc.vector.tensor_scalar(self.one_minus_ka[:], kit.col("k_a", 0, CT), -1.0, 1.0,
                                        ALU.mult, ALU.add).then_inc(ready, 1)
                dve.wait_ge(ready, 1)


def scans(kit, cst, mix, keys, o, kd_sum, states_in, states_out):
    nc = kit.nc
    sem_names = ("lora_done", "lam_ready", "a_ready", "cum_ready", "state_loaded", "state_stored",
                 "pads", "loaded", "g_ready", "ig_ready", "t_ready", "kka_ready", "kd_ready", "sum_ready",
                 "wide_ready", "turned", "tall_ready", "am_done", "am_ready", "y_done", "y_ready",
                 "wy_done", "wy_ready", "wa_done", "wa_ready", "u_done", "u_ready", "z_done", "z_summed",
                 "z_ready", "o_done", "o_ready", "const_in")
    S = {q: kit.sem("sc_" + q) for q in sem_names}
    G2 = {q: [kit.sem(f"sc_{q}{g}") for g in range(2)]
          for q in ("level_ready", "v_ready", "w_done", "w_ready", "p_done", "p_ready", "v_done")}
    LEVELS = 6
    with ExitStack() as ctx:
        buf = lambda name, shape, dt=F32: ctx.enter_context(nc.sbuf_tensor(name, shape, dt))
        masks = buf("masks", [P, 2, 10, P])
        lora_w = buf("lora_w", [P, 2, W])
        lora = buf("lora", [P, 2, T])
        reset = buf("reset", [P, 2, T])
        cum, a_all = buf("cum_decay", [P, CT, T]), buf("a_all", [P, CT, T])
        lam = buf("decay_rate", [P, T])
        rt, kt, vt, kkt = (buf(f"{n}_tile", [P, CT, P]) for n in ("r", "k", "v", "kk"))
        g_pad, inv_g = buf("g_pad", [P, CT, 2, CK + 1]), buf("inv_g", [P, CT, P])
        t_ka, kka, kd = buf("t_ka", [P, CT, P]), buf("kka", [P, CT, P]), buf("kd", [P, CT, P])
        ar = buf("a_r_wide", [P, CT, 2, P])
        b_wide, k_wide = buf("b_wide", [P, CT, P]), buf("k_wide", [P, CT, P])
        a_tall, k_tall, b_tall, v_tall = (buf(f"{n}_tall", [P, W]) for n in ("a", "k", "b", "v"))
        am = buf("am", [P, HEADS, 4, P])
        level = buf("n_level", [P, 2, 2, 4, P])
        v_inv, w_inv, prod = (buf(n, [P, 2, 4, P]) for n in ("inv_t", "inv", "prod"))
        y_tall, wy_tall, u_tall = (buf(n, [P, W]) for n in ("y_tall", "wy_tall", "u_tall"))
        wa = buf("wa_wide", [P, CT, P])
        z, z_sum = buf("z", [P, CT, HD]), buf("z_sum", [P, CT, HD])
        block = ctx.enter_context(nc.Block())
        bank = kit.banks

        def tile_schedule(eng, head, tile, between):
            for d in range(2):
                head(d)
                tile(d, d * NTT, 0)
                between(d)
                with eng.Fori(1, NTT) as i:
                    tile(d, i + d * NTT, i * P if d == 0 else i * (-P) + NTT * P)

        def tokens(buf4, tau):
            return buf4[:, :, tau:tau + P]

        def cum_step(d, ct, c):
            return (d * CT + ct) * NC + c

        @block.sync
        def _(sp):
            sp.dma_start(lora_w[:], kit.dram["lora_up"]).then_inc(S["const_in"], 16)
            sp.dma_start(reset[:], kit.dram["reset"]).then_inc(S["const_in"], 16)
            sp.dma_start(masks[:], kit.dram["masks"]).then_inc(S["const_in"], 16)
            sp.dma_start(lora[:], mix[J_WD:J_GD].rearrange("c p t -> p c t")).then_inc(S["const_in"], 16)

            def tile(d, s, tau):
                if not (isinstance(s, int) and s == 0):
                    kit.hold(sp, S["wide_ready"], s * 4)
                    kit.hold(sp, S["turned"], s * 4)
                for dst, src in ((rt, mix[0:CT]), (kt, mix[CT:2 * CT]), (vt, mix[2 * CT:3 * CT]), (kkt, keys)):
                    sp.dma_start(dst[:], src[:, :, bass.ds(tau, P)].rearrange("c p t -> p c t")).then_inc(S["loaded"], 16)

            def between(d):
                sp.wait_ge(S["z_ready"], (d * NTT + 1) * 2)
                sp.dma_start(states_out[d], z[:]).then_inc(S["state_stored"], 16)
                sp.wait_ge(S["state_stored"], 16 * (d + 1))
                sp.wait_ge(S["o_done"], d * NTT + 1)
                sp.dma_start(z[:], states_in[d]).then_inc(S["state_loaded"], 16)
            tile_schedule(sp, lambda d: None, tile, between)
            sp.wait_ge(S["state_stored"], 32)

        @block.gpsimd
        def _(pool):
            pool.wait_ge(S["const_in"], 64)

            def head(d):
                pool.wait_ge(S["a_ready"], CT * NC * (d + 1))

            def tile(d, s, tau):
                at = bass.ds(tau, P)
                kit.hold(pool, S["loaded"], (s + 1) * 64)
                nc.gpsimd.tensor_tensor(kka[:], kkt[:], a_all[:, :, at], ALU.mult).then_inc(S["kka_ready"], 1)
                pool.wait_ge(S["t_ready"], (s + 1) * CT)
                nc.gpsimd.tensor_tensor(kd[:], kt[:], t_ka[:], ALU.mult).then_inc(S["kd_ready"], 1)
                kit.hold(pool, S["kd_ready"], s + 1)
                if d == 0:
                    nc.gpsimd.tensor_copy(kd_sum[:, :, at], kd[:]).then_inc(S["sum_ready"], 1)
                else:
                    nc.gpsimd.tensor_tensor(kd_sum[:, :, at], kd_sum[:, :, at], kd[:], ALU.add).then_inc(S["sum_ready"], 1)
                for l in range(LEVELS):
                    for g in range(2):
                        if l == 0:
                            pool.wait_ge(S["am_ready"], s * 8 + 4 * g + 4)
                        if l == 2:
                            pool.wait_ge(G2["v_ready"][g], s * 6 + 1)
                        if l >= 3:
                            pool.wait_ge(G2["p_done"][g], s * 5 + l - 2)
                        nc.gpsimd.tensor_tensor(level[:, g, l % 2], am[:, 4 * g:4 * g + 4, 0],
                                                masks[:, d, 4 + l:5 + l].broadcast_to([P, 4, P]),
                                                ALU.mult).then_inc(G2["level_ready"][g], 1)
            tile_schedule(pool, head, tile, lambda d: None)

        @block.scalar
        def _(act):
            act.wait_ge(S["const_in"], 64)

            def head(d):
                for ct in range(CT):
                    for c in range(NC):
                        n = cum_step(d, ct, c)
                        part = slice(c * CH, (c + 1) * CH)
                        act.wait_ge(S["lora_done"], 2 * n + 1)
                        if c == 0 and d * CT + ct:
                            act.wait_ge(S["cum_ready"], d * CT + ct)
                        nc.scalar.activation(lam[:, part], bank[n % 4][:, 0:CH], ACT.Sigmoid,
                                             bias=kit.col("w0", d * CT + ct)).then_inc(S["lam_ready"], 1)
                        act.wait_ge(S["lora_done"], 2 * n + 2)
                        nc.scalar.activation(a_all[:, ct, part], bank[4 + n % 4][:, 0:CH], ACT.Sigmoid,
                                             bias=kit.col("a0", d * CT + ct)).then_inc(S["a_ready"], 1)
                act.wait_ge(S["cum_ready"], CT * (d + 1))
                act.wait_ge(S["a_ready"], CT * NC * (d + 1))

            def tile(d, s, tau):
                at = bass.ds(tau, P)
                body = slice(1, CK + 1) if d == 0 else slice(0, CK)
                if not (isinstance(s, int) and s == 0):
                    kit.hold(act, S["z_ready"], s * 2)
                for ct in range(CT):
                    ins = nc.scalar.activation(g_pad[:, ct, :, body],
                                               cum[:, ct, at].rearrange("p (k t) -> p k t", k=2),
                                               ACT.Exp, scale=-DECAY_SCALE)
                ins.then_inc(S["g_ready"], 1)
                nc.scalar.activation(inv_g[:], cum[:, :, at], ACT.Exp, scale=DECAY_SCALE).then_inc(S["ig_ready"], 1)
                for ct in range(CT):
                    nc.scalar.activation(t_ka[:, ct], a_all[:, ct, at], ACT.Identity, scale=kit.col("k_a", ct),
                                         bias=cst.one_minus_ka[:, ct:ct + 1]).then_inc(S["t_ready"], 1)
                for m, dst in enumerate((a_tall, k_tall, b_tall, v_tall)):
                    act.wait_ge(S["turned"], s * 4 + m + 1)
                    nc.scalar.activation(dst[:], bank[4 + m][:], ACT.Copy).then_inc(S["tall_ready"], 1)
                act.wait_ge(S["y_done"], s + 1)
                nc.scalar.activation(y_tall[:], bank[4][:], ACT.Copy).then_inc(S["y_ready"], 1)
                for l in range(1, LEVELS):
                    for g in range(2):
                        act.wait_ge(G2["w_done"][g], s * 5 + l)
                        nc.scalar.activation(w_inv[:, g], bank[2 * g][:], ACT.Copy).then_inc(G2["w_ready"][g], 1)
                    for g in range(2):
                        act.wait_ge(G2["p_done"][g], s * 5 + l)
                        nc.scalar.activation(prod[:, g], bank[2 * g][:], ACT.Copy).then_inc(G2["p_ready"][g], 1)
                act.wait_ge(S["wy_done"], s + 1)
                nc.scalar.activation(wy_tall[:], bank[5][:], ACT.Copy).then_inc(S["wy_ready"], 1)
                act.wait_ge(S["wa_done"], s + 1)
                nc.scalar.activation(wa[:], bank[6][:], ACT.Copy).then_inc(S["wa_ready"], 1)
            tile_schedule(act, head, tile, lambda d: None)

        @block.vector
        def _(dve):
            dve.wait_ge(S["const_in"], 64)

            def head(d):
                for ct in range(CT):
                    dve.wait_ge(S["lam_ready"], cum_step(d, ct, NC))
                    way = slice(None, None, 1 if d == 0 else -1)
                    nc.vector.tensor_tensor_scan(cum[:, ct, way], reset[:, d, way], lam[:, way], 0.0,
                                                 ALU.mult, ALU.add).then_inc(S["cum_ready"], 1)
                edge = 0 if d == 0 else CK
                nc.vector.memset(g_pad[:, :, :, edge:edge + 1], 1.0).then_inc(S["pads"], 1)
                nc.vector.memset(z[:], 0.0).then_inc(S["pads"], 1)
                dve.wait_ge(S["pads"], 2 * d + 2)

            def between(d):
                dve.wait_ge(S["state_loaded"], 16 * (d + 1))

            def tile(d, s, tau):
                at = bass.ds(tau, P)
                before, upto = (slice(0, CK), slice(1, CK + 1)) if d == 0 else (slice(1, CK + 1), slice(0, CK))
                last = slice(CK, CK + 1) if d == 0 else slice(0, 1)
                by_chunk = lambda v: v.rearrange("p c (k t) -> p c k t", k=2)
                dve.wait_ge(S["loaded"], (s + 1) * 64)
                dve.wait_ge(S["g_ready"], s + 1)
                if not (isinstance(s, int) and s == 0):
                    dve.wait_ge(S["o_done"], s)
                nc.vector.tensor_tensor(by_chunk(ar[:, :, 0]), by_chunk(kkt[:]), g_pad[:, :, :, before],
                                        ALU.mult).then_inc(S["wide_ready"], 1)
                nc.vector.tensor_tensor(by_chunk(ar[:, :, 1]), by_chunk(rt[:]), g_pad[:, :, :, upto],
                                        ALU.mult).then_inc(S["wide_ready"], 1)
                dve.wait_ge(S["ig_ready"], s + 1)
                dve.wait_ge(S["kka_ready"], s + 1)
                nc.vector.scalar_tensor_tensor(b_wide[:], kka[:], -1.0, inv_g[:], ALU.mult, ALU.mult)\
                    .then_inc(S["wide_ready"], 1)
                dve.wait_ge(S["kd_ready"], s + 1)
                nc.vector.tensor_tensor(k_wide[:], kd[:], inv_g[:], ALU.mult).then_inc(S["wide_ready"], 1)
                for h in range(HEADS):
                    dve.wait_ge(S["am_done"], s * 8 + h + 1)
                    nc.vector.tensor_tensor(am[:, h], bank[h % 4][:].rearrange("p (m t) -> p m t", m=4),
                                            masks[:, d, 0:4], ALU.mult).then_inc(S["am_ready"], 1)
                for g in range(2):
                    dve.wait_ge(G2["level_ready"][g], s * 6 + 1)
                    nc.vector.tensor_tensor(v_inv[:, g], level[:, g, 0],
                                            cst.squares[:, 0:1].broadcast_to([P, 4, P]), ALU.add)\
                        .then_inc(G2["v_ready"][g], 1)
                for l in range(1, LEVELS):
                    for g in range(2):
                        dve.wait_ge(G2["v_done"][g], s * 5 + l)
                        nc.vector.tensor_tensor(v_inv[:, g], bank[2 * g + 1][:].rearrange("p (h t) -> p h t", h=4),
                                                v_inv[:, g], ALU.add).then_inc(G2["v_ready"][g], 1)
                for c in ((0, 1) if d == 0 else (1, 0)):
                    first = c == (0 if d == 0 else 1)
                    n = s * 2 + (0 if first else 1)
                    rows = slice(CK * c, CK * c + CK)
                    by_head = lambda v: v[rows].rearrange("p (c e i) -> p c e i", e=2, i=HD)
                    dve.wait_ge(S["u_done"], n + 1)
                    if first:
                        dve.wait_ge(S["wy_ready"], s + 1)
                    for e in range(2):
                        nc.vector.tensor_tensor(by_head(u_tall[:])[:, :, e],
                                                bank[4 + e][rows, 0:CT * HD].rearrange("p (c i) -> p c i", c=CT),
                                                by_head(wy_tall[:])[:, :, e], ALU.add).then_inc(S["u_ready"], 1)
                    dve.wait_ge(S["z_done"], n + 1)
                    nc.vector.tensor_tensor(z_sum[:], bank[6][:, 0:CT * HD].rearrange("p (c i) -> p c i", c=CT), z[:],
                                            ALU.add).then_inc(S["z_summed"], 1)
                    dve.wait_ge(S["z_summed"], n + 1)
                    nc.vector.tensor_tensor(z[:], z_sum[:], g_pad[:, :, c, last].broadcast_to([P, CT, HD]),
                                            ALU.mult).then_inc(S["z_ready"], 1)
                kit.hold(dve, S["o_done"], s + 1)
                for e in range(2):
                    half = slice(64 * e, 64 * e + 64)
                    src = bank[e][half].rearrange("p (c t) -> p c t", c=CT)
                    dst = o[half, :, at]
                    if d == 0:
                        nc.vector.tensor_copy(dst, src).then_inc(S["o_ready"], 1)
                    else:
                        nc.vector.tensor_tensor(dst, src, dst, ALU.add).then_inc(S["o_ready"], 1)
            tile_schedule(dve, head, tile, between)

        @block.tensor
        def _(pe):
            pe.wait_ge(S["const_in"], 64)

            def head(d):
                rows = slice(LORA * d, LORA * d + LORA)
                if d:
                    pe.wait_ge(S["o_ready"], 2 * NTT)
                for ct in range(CT):
                    for c in range(NC):
                        n = cum_step(d, ct, c)
                        part = slice(c * CH, (c + 1) * CH)
                        for m, ready in ((0, "lam_ready"), (1, "a_ready")):
                            if n >= 4:
                                pe.wait_ge(S[ready], n - 3)
                            nc.tensor.matmul(bank[4 * m + n % 4][:, 0:CH], lora_w[rows, m, ct * P:(ct + 1) * P],
                                             lora[rows, m, part], start=True, stop=True).then_inc(S["lora_done"], 1)
                pe.wait_ge(S["a_ready"], CT * NC * (d + 1))
                pe.wait_ge(S["pads"], 2 * d + 2)

            def between(d):
                kit.hold(pe, S["state_loaded"], 16 * (d + 1))

            def tile(d, s, tau):
                mm = nc.tensor.matmul
                hold = lambda q, v: kit.hold(pe, S[q], v)
                if not (isinstance(s, int) and s == 0):
                    hold("o_ready", s * 2)
                hold("loaded", (s + 1) * 64)
                for m, (src, n) in enumerate(((lambda ct: ar[:, ct, 0], 1), (lambda ct: k_wide[:, ct], 4),
                                              (lambda ct: b_wide[:, ct], 4), (lambda ct: vt[:, ct], 4))):
                    hold("wide_ready", s * 4 + n)
                    for ct in range(CT):
                        ins = nc.tensor.transpose(bank[4 + m][:, ct * P:(ct + 1) * P], src(ct), cst.ident)
                    ins.then_inc(S["turned"], 1)
                for h in range(HEADS):
                    ct, e = divmod(h, 2)
                    half = slice(64 * e, 64 * e + 64)
                    if h >= 4:
                        hold("am_ready", s * 8 + h - 3)
                    both = ar[half, ct].rearrange("p m t -> p (m t)")
                    mm(bank[h % 4][:, 0:2 * P], b_wide[half, ct], both, start=True, stop=True)
                    mm(bank[h % 4][:, 2 * P:4 * P], k_wide[half, ct], both, start=True, stop=True)\
                        .then_inc(S["am_done"], 1)
                hold("am_ready", s * 8 + 8)
                hold("tall_ready", s * 4 + 4)
                for h in range(HEADS):
                    ins = mm(bank[4][:, h * HD:(h + 1) * HD], am[:, h, 2], v_tall[:, h * HD:(h + 1) * HD],
                             start=True, stop=True)
                ins.then_inc(S["y_done"], 1)
                for l in range(1, LEVELS):
                    for g in range(2):
                        kit.hold(pe, G2["v_ready"][g], s * 6 + l)
                        for q in range(4):
                            ins = nc.tensor.transpose(bank[2 * g][:, q * P:(q + 1) * P], v_inv[:, g, q], cst.ident)
                        ins.then_inc(G2["w_done"][g], 1)
                    for g in range(2):
                        kit.hold(pe, G2["level_ready"][g], s * 6 + l + 1)
                        kit.hold(pe, G2["w_ready"][g], s * 5 + l)
                        for q in range(4):
                            ins = mm(bank[2 * g][:, q * P:(q + 1) * P], level[:, g, l % 2, q], w_inv[:, g, q],
                                     start=True, stop=True)
                        ins.then_inc(G2["p_done"][g], 1)
                    for g in range(2):
                        kit.hold(pe, G2["p_ready"][g], s * 5 + l)
                        for q in range(4):
                            ins = mm(bank[2 * g + 1][:, q * P:(q + 1) * P], prod[:, g, q], v_inv[:, g, q],
                                     start=True, stop=True)
                        ins.then_inc(G2["v_done"][g], 1)
                hold("y_ready", s + 1)
                for g in range(2):
                    kit.hold(pe, G2["v_ready"][g], s * 6 + 6)
                for h in range(HEADS):
                    ins = mm(bank[5][:, h * HD:(h + 1) * HD], v_inv[:, h // 4, h % 4], y_tall[:, h * HD:(h + 1) * HD],
                             start=True, stop=True)
                ins.then_inc(S["wy_done"], 1)
                for h in range(HEADS):
                    ct, e = divmod(h, 2)
                    ins = mm(bank[6][64 * e:64 * e + 64, ct * P:(ct + 1) * P], a_tall[:, h * HD:(h + 1) * HD],
                             v_inv[:, h // 4, h % 4], start=True, stop=True)
                ins.then_inc(S["wa_done"], 1)
                for h in range(HEADS):
                    ct, e = divmod(h, 2)
                    mm(bank[e][64 * e:64 * e + 64, ct * P:(ct + 1) * P], v_tall[:, h * HD:(h + 1) * HD], am[:, h, 3],
                       start=(ct == 0), stop=False, skip_group_check=True)
                hold("wy_ready", s + 1)
                hold("wa_ready", s + 1)
                for c in ((0, 1) if d == 0 else (1, 0)):
                    first = c == (0 if d == 0 else 1)
                    n = s * 2 + (0 if first else 1)
                    rows = slice(CK * c, CK * c + CK)
                    if not (isinstance(n, int) and n == 0):
                        hold("z_ready", n)
                    for h in range(HEADS):
                        ct, e = divmod(h, 2)
                        half = slice(64 * e, 64 * e + 64)
                        ins = mm(bank[4 + e][rows, ct * HD:(ct + 1) * HD], wa[half, ct, rows], z[half, ct],
                                 start=True, stop=True)
                    ins.then_inc(S["u_done"], 1)
                    for h in range(HEADS):
                        ct, e = divmod(h, 2)
                        half = slice(64 * e, 64 * e + 64)
                        mm(bank[e][half, ct * P + CK * c:ct * P + CK * c + CK], z[half, ct], ar[half, ct, 1, rows],
                           start=False, stop=False, skip_group_check=True)
                    for h in range(HEADS):
                        ct, e = divmod(h, 2)
                        mm(bank[6][64 * e:64 * e + 64, ct * HD:(ct + 1) * HD], k_tall[rows, h * HD:(h + 1) * HD],
                           v_tall[rows, h * HD:(h + 1) * HD], start=(ct == 0), stop=False, skip_group_check=True)
                    hold("u_ready", (n + 1) * 2)
                    for h in range(HEADS):
                        ct, e = divmod(h, 2)
                        ins = mm(bank[6][64 * e:64 * e + 64, ct * HD:(ct + 1) * HD], b_tall[rows, h * HD:(h + 1) * HD],
                                 u_tall[rows, h * HD:(h + 1) * HD], start=False, stop=True, skip_group_check=True)
                    ins.then_inc(S["z_done"], 1)
                for h in range(HEADS):
                    ct, e = divmod(h, 2)
                    ins = mm(bank[e][64 * e:64 * e + 64, ct * P:(ct + 1) * P], u_tall[:, h * HD:(h + 1) * HD], am[:, h, 1],
                             start=False, stop=True, skip_group_check=True)
                ins.then_inc(S["o_done"], 1)
            tile_schedule(pe, head, tile, between)


def head_norm(kit, cst, mix, o, kd_sum, o_hi, o_lo):
    nc = kit.nc
    s = {q: kit.sem("hn_" + q) for q in (
        "loaded", "mean_done", "centered", "rk_ready", "squared", "var_done", "rooted", "inverted", "scaled",
        "affine", "bonus_done", "bonus_v", "with_bonus", "gate_done", "gated", "hi_ready", "lo_ready")}
    with ExitStack() as ctx:
        buf = lambda name, shape, dt=F32: ctx.enter_context(nc.sbuf_tensor(name, shape, dt))
        r, v = buf("hn_r", [P, CT, T]), buf("hn_v", [P, CT, T])
        gd, g_up = buf("hn_gd", [P, T]), buf("hn_g_up", [P, W])
        block = ctx.enter_context(nc.Block())
        steps = CT * NC
        ct_of, part = (lambda m: m // NC), (lambda m: slice(m % NC * CH, m % NC * CH + CH))
        at = lambda a, m: a[:, ct_of(m), part(m)]
        bank = lambda m, q: kit.banks[4 * (m % 2) + q][:, 0:CH]

        def skewed(stages):
            for t in range(steps + max(lag for lag, _ in stages)):
                for lag, piece in stages:
                    if 0 <= t - lag < steps:
                        piece(t - lag)

        @block.sync
        def _(sp):
            sp.dma_start(g_up[:], kit.dram["g_up"]).then_inc(s["loaded"], 16)
            sp.dma_start(gd[:], mix[J_GD]).then_inc(s["loaded"], 16)
            sp.dma_start(r[:], mix[0:CT].rearrange("c p t -> p c t")).then_inc(s["loaded"], 16)
            sp.dma_start(v[:], mix[2 * CT:3 * CT].rearrange("c p t -> p c t")).then_inc(s["loaded"], 16)

        @block.tensor
        def _(pe):
            pe.wait_ge(s["loaded"], 64)

            def sums(m):
                if m >= 2:
                    pe.wait_ge(s["centered"], m - 1)
                nc.tensor.matmul(bank(m, 0), cst.pair_ones, at(o, m), start=True, stop=True).then_inc(s["mean_done"], 1)
                if m >= 2:
                    pe.wait_ge(s["gated"], m - 1)
                nc.tensor.matmul(bank(m, 3), g_up[:, ct_of(m) * P:(ct_of(m) + 1) * P], gd[:, part(m)],
                                 start=True, stop=True).then_inc(s["gate_done"], 1)

            def bonus(m):
                pe.wait_ge(s["rk_ready"], m + 1)
                if m >= 2:
                    pe.wait_ge(s["bonus_v"], m - 1)
                nc.tensor.matmul(bank(m, 2), cst.pair_ones, at(kd_sum, m), start=True, stop=True)\
                    .then_inc(s["bonus_done"], 1)

            def variance(m):
                pe.wait_ge(s["squared"], m + 1)
                if m >= 2:
                    pe.wait_ge(s["rooted"], m - 1)
                nc.tensor.matmul(bank(m, 1), cst.pair_ones, at(r, m), start=True, stop=True).then_inc(s["var_done"], 1)
            skewed([(0, sums), (0, bonus), (0, variance)])

        @block.scalar
        def _(act):
            def square(m):
                act.wait_ge(s["centered"], m + 1)
                act.wait_ge(s["rk_ready"], m + 1)
                nc.scalar.activation(at(r, m), at(o, m), ACT.Square).then_inc(s["squared"], 1)

            def root(m):
                act.wait_ge(s["var_done"], m + 1)
                nc.scalar.activation(at(r, m), bank(m, 1), ACT.Sqrt, scale=1.0 / HD, bias=kit.eps[:, 1:2])\
                    .then_inc(s["rooted"], 1)

            def affine(m):
                act.wait_ge(s["scaled"], m + 1)
                nc.scalar.activation(at(r, m), at(o, m), ACT.Identity, scale=kit.col("lnx_w", ct_of(m)),
                                     bias=kit.col("lnx_b", ct_of(m))).then_inc(s["affine"], 1)

            def high(m):
                act.wait_ge(s["gated"], m + 1)
                nc.scalar.activation(at(o_hi, m), at(o, m), ACT.Copy).then_inc(s["hi_ready"], 1)
            skewed([(0, square), (0, root), (1, affine), (2, high)])

        @block.vector
        def _(dve):
            dve.wait_ge(s["loaded"], 64)

            def center(m):
                dve.wait_ge(s["mean_done"], m + 1)
                nc.vector.scalar_tensor_tensor(at(o, m), bank(m, 0), -1.0 / HD, at(o, m), ALU.mult, ALU.add)\
                    .then_inc(s["centered"], 1)
                nc.vector.scalar_tensor_tensor(at(kd_sum, m), at(r, m), kit.col("r_k", ct_of(m)), at(kd_sum, m),
                                               ALU.mult, ALU.mult).then_inc(s["rk_ready"], 1)

            def normed(m):
                dve.wait_ge(s["rooted"], m + 1)
                nc.vector.reciprocal(at(kd_sum, m), at(r, m)).then_inc(s["inverted"], 1)
                dve.wait_ge(s["inverted"], m + 1)
                nc.vector.tensor_tensor(at(o, m), at(o, m), at(kd_sum, m), ALU.mult).then_inc(s["scaled"], 1)

            def bonus(m):
                dve.wait_ge(s["bonus_done"], m + 1)
                nc.vector.tensor_tensor(at(v, m), bank(m, 2), at(v, m), ALU.mult).then_inc(s["bonus_v"], 1)

            def gated(m):
                dve.wait_ge(s["affine"], m + 1)
                dve.wait_ge(s["bonus_v"], m + 1)
                nc.vector.tensor_tensor(at(v, m), at(v, m), at(r, m), ALU.add).then_inc(s["with_bonus"], 1)
                dve.wait_ge(s["with_bonus"], m + 1)
                dve.wait_ge(s["gate_done"], m + 1)
                nc.vector.tensor_tensor(at(o, m), bank(m, 3), at(v, m), ALU.mult).then_inc(s["gated"], 1)

            def low(m):
                dve.wait_ge(s["hi_ready"], m + 1)
                nc.vector.tensor_tensor(at(o_lo, m), at(o, m), at(o_hi, m).bitcast(F32), ALU.subtract)\
                    .then_inc(s["lo_ready"], 1)
            skewed([(0, center), (0, bonus), (1, normed), (1, gated), (2, low)])
            dve.wait_ge(s["lo_ready"], steps)


def fourier(kit, mix, f_hi, f_lo):
    nc = kit.nc
    s = {q: kit.sem("fo_" + q) for q in (
        "f_loaded", "c_loaded", "g_done", "g_ready", "ctx_done", "ctx_hi", "ctx_lo", "g_hi_ready", "g_lo_ready",
        "dft_hi_ready", "dft_ready", "unit_done", "hi_ready", "lo_ready")}
    dft_loaded = [kit.sem(f"fo_dft_loaded{p}") for p in range(2)]
    LT = NTT - 1
    with ExitStack() as ctx:
        buf = lambda name, shape, dt=F32: ctx.enter_context(nc.sbuf_tensor(name, shape, dt))
        f = buf("fo_f", [P, FG, T])
        cs = buf("fo_cs", [P, 2 * FD])
        dft_ctx = buf("fo_dft_ctx", [P, 2, T_CTX])
        g = buf("fo_g", [P, NTT, 2, FG, FD])
        raw = buf("fo_raw", [P, 2, T_LAT])
        dft_hi, dft_lo = buf("fo_dft_hi", [P, 2, T_LAT], F32R), buf("fo_dft_lo", [P, 2, T_LAT], F32R)
        g_hi, g_lo = buf("fo_g_hi", [P, 2, FG, FD], F32R), buf("fo_g_lo", [P, 2, FG, FD], F32R)
        block = ctx.enter_context(nc.Block())
        bank = kit.banks

        @block.sync
        def _(sp):
            sp.dma_start(cs[:], kit.dram["dft_features"]).then_inc(s["c_loaded"], 16)
            sp.dma_start(dft_ctx[:], kit.dram["dft_context"]).then_inc(s["c_loaded"], 16)
            sp.dma_start(f[:], mix[J_F:J_GATE].rearrange("c p t -> p c t")).then_inc(s["f_loaded"], 16)

            def load(tt, first=False):
                for p in range(2):
                    if not first:
                        kit.hold(sp, s["dft_ready"], tt * 2 + (p - 1))
                    sp.dma_start(raw[:, p], kit.dram["dft_latents"][tt, p]).then_inc(dft_loaded[p], 16)
            load(0, True)
            with sp.Fori(1, LT) as tt:
                load(tt)

        @block.tensor
        def _(pe):
            pe.wait_ge(s["c_loaded"], 32)
            pe.wait_ge(s["f_loaded"], 16)
            for m in range(2 * NTT):
                tt, pair = divmod(m, 2)
                if m >= 8:
                    pe.wait_ge(s["g_ready"], m - 7)
                for q in range(2):
                    ins = nc.tensor.matmul(bank[m % 8][:, q * 2 * FD:(q + 1) * 2 * FD],
                                           f[:, 2 * pair + q, tt * P:(tt + 1) * P], cs[:], start=True, stop=True)
                ins.then_inc(s["g_done"], 1)
            pe.wait_ge(s["g_ready"], 2 * NTT)
            for q in range(FG):
                for p in range(2):
                    ins = nc.tensor.matmul(bank[0][:, q * P:(q + 1) * P], g[:, 0, p, q], dft_ctx[:, p],
                                           start=(p == 0), stop=(p == 1))
            ins.then_inc(s["ctx_done"], 1)
            pe.wait_ge(s["ctx_lo"], 1)

            def units(tt, early=False, late=False):
                for p in range(2):
                    pe.wait_ge(s["g_lo_ready"], tt * 2 + (p + 1))
                    pe.wait_ge(s["dft_ready"], tt * 2 + (p + 1))
                    for q in range(FG):
                        for half in range(2):
                            cols = slice(half * 512, half * 512 + 512)
                            for m, (w, v) in enumerate(((g_lo, dft_hi), (g_hi, dft_lo), (g_hi, dft_hi))):
                                ins = nc.tensor.matmul(bank[2 * q + half][:], w[:, p, q], v[:, p, cols],
                                                       start=(early and p == 0 and m == 0),
                                                       stop=(late and p == 1 and m == 2), skip_group_check=True)
                    ins.then_inc(s["unit_done"], 1)
            units(0, early=True)
            with pe.Fori(1, LT - 1) as tt:
                units(tt)
            units(LT - 1, late=True)

        @block.scalar
        def _(act):
            for m in range(2 * NTT):
                tt, pair = divmod(m, 2)
                act.wait_ge(s["g_done"], m + 1)
                for q in range(2):
                    ins = nc.scalar.activation(g[:, tt, :, 2 * pair + q], bank[m % 8][:, q * 2 * FD:(q + 1) * 2 * FD]
                                               .rearrange("p (a t) -> p a t", a=2), ACT.Copy)
                ins.then_inc(s["g_ready"], 1)
            act.wait_ge(s["ctx_done"], 1)
            nc.scalar.activation(f_hi[:, :, 0:T_CTX], bank[0][:].rearrange("p (g t) -> p g t", g=FG), ACT.Copy)\
                .then_inc(s["ctx_hi"], 1)
            act.wait_ge(s["g_ready"], 2 * NTT)

            def split(tt, first=False):
                for p in range(2):
                    if not first:
                        kit.hold(act, s["unit_done"], tt * 2 + (p - 1))
                    tile = g[:, bass.ds(tt + 1, 1), p]
                    nc.scalar.activation(g_hi[:, p:p + 1], tile, ACT.Copy).then_inc(s["g_hi_ready"], 1)
                    act.wait_ge(dft_loaded[p], (tt + 1) * 16)
                    nc.scalar.activation(dft_hi[:, p], raw[:, p], ACT.Copy).then_inc(s["dft_hi_ready"], 1)
            split(0, True)
            with act.Fori(1, LT) as tt:
                split(tt)
            act.wait_ge(s["unit_done"], 2 * LT)
            for q in range(FG):
                for half in range(2):
                    cols = slice(T_CTX + half * 512, T_CTX + half * 512 + 512)
                    nc.scalar.activation(f_hi[:, q, cols], bank[2 * q + half][:], ACT.Copy).then_inc(s["hi_ready"], 1)

        @block.vector
        def _(dve):
            dve.wait_ge(s["ctx_hi"], 1)
            nc.vector.tensor_tensor(f_lo[:, :, 0:T_CTX], bank[0][:].rearrange("p (g t) -> p g t", g=FG),
                                    f_hi[:, :, 0:T_CTX].bitcast(F32), ALU.subtract).then_inc(s["ctx_lo"], 1)

            def split(tt):
                for p in range(2):
                    dve.wait_ge(s["g_hi_ready"], tt * 2 + (p + 1))
                    nc.vector.tensor_tensor(g_lo[:, p:p + 1], g[:, bass.ds(tt + 1, 1), p], g_hi[:, p:p + 1].bitcast(F32),
                                            ALU.subtract).then_inc(s["g_lo_ready"], 1)
                    dve.wait_ge(s["dft_hi_ready"], tt * 2 + (p + 1))
                    nc.vector.tensor_tensor(dft_lo[:, p], raw[:, p], dft_hi[:, p].bitcast(F32),
                                            ALU.subtract).then_inc(s["dft_ready"], 1)
            split(0)
            with dve.Fori(1, LT) as tt:
                split(tt)
            for m in range(2 * FG):
                q, half = divmod(m, 2)
                cols = slice(T_CTX + half * 512, T_CTX + half * 512 + 512)
                dve.wait_ge(s["hi_ready"], m + 1)
                nc.vector.tensor_tensor(f_lo[:, q, cols], bank[m][:], f_hi[:, q, cols].bitcast(F32),
                                        ALU.subtract).then_inc(s["lo_ready"], 1)
            dve.wait_ge(s["lo_ready"], 2 * FG)


class Merge:

    def __init__(self, kit, mix):
        self.kit, self.nc, self.mix = kit, kit.nc, mix
        self.loaded, self.left, self.right = kit.sem("gates_loaded"), kit.sem("gated_a"), kit.sem("gated_b")
        self.used = kit.sem("gates_used")

    def setup(self, ctx):
        self.gates = ctx.enter_context(self.nc.sbuf_tensor("gates", [P, 2, T], F32))
        self.parts = ctx.enter_context(self.nc.sbuf_tensor("gated_parts", [P, 2, CH], F32))

    def load(self, sp, f, first):
        if not first:
            self.kit.hold(sp, self.right, f * 3)
        for b in range(2):
            sp.dma_start(self.gates[:, b], self.mix[f + (J_GATE + KT * b)]).then_inc(self.loaded, 16)

    def scalar(self, act, a, out):
        return self.nc.scalar.activation(out, a, ACT.Copy)

    def vector(self, dve, f, n, c, a, b, act_out, g32):
        toks = slice(c * CH, (c + 1) * CH)
        if c == 0:
            dve.wait_ge(self.loaded, (f + 1) * 32)
        self.nc.vector.tensor_tensor(self.parts[:, 0], act_out, self.gates[:, 0, toks], ALU.mult).then_inc(self.left, 1)
        self.nc.vector.tensor_tensor(self.parts[:, 1], b, self.gates[:, 1, toks], ALU.mult).then_inc(self.right, 1)
        dve.wait_ge(self.left, n + 1)
        dve.wait_ge(self.right, n + 1)
        return self.nc.vector.tensor_tensor(g32, self.parts[:, 0], self.parts[:, 1], ALU.add)


def merge(kit, mix, halves, x_saved):
    def load_x(sp, loaded):
        for k in range(KT):
            sp.dma_start(kit.x[:, k], x_saved[k]).then_inc(loaded, 16)
    hidden_stage(kit, "merge", KT, CT, (kit.dram["w_rwkv"], kit.dram["w_fourier"]), kit.dram["w_out"],
                 None, halves, Merge(kit, mix), 1, load_x)


def final_norm(kit, out):
    nc = kit.nc
    s = {q: kit.sem("fn_" + q) for q in ("squared", "summed", "rooted", "inverted", "normed", "scaled", "stored")}
    with ExitStack() as ctx:
        buf = lambda name, shape: ctx.enter_context(nc.sbuf_tensor(name, shape, F32))
        sq, inv, y = buf("fn_square", [P, 2, CH]), buf("fn_inv", [P, 2, NC, CH]), buf("fn_y", [P, KT, T])
        block = ctx.enter_context(nc.Block())
        at = lambda a, k, c: a[:, k, c * CH:(c + 1) * CH]

        @block.scalar
        def _(act):
            for m in range(NC * KT):
                c, k = divmod(m, KT)
                if m >= 2:
                    act.wait_ge(s["summed"], m - 1)
                nc.scalar.activation(sq[:, m % 2], at(kit.x, k, c), ACT.Square).then_inc(s["squared"], 1)
                if k == KT - 1:
                    act.wait_ge(s["summed"], m + 1)
                    nc.scalar.activation(inv[:, 0, c], kit.banks[c][:, 0:CH], ACT.Sqrt, scale=1.0 / D,
                                         bias=kit.eps[:, 0:1]).then_inc(s["rooted"], 1)
            for m in range(NC * KT):
                c, k = divmod(m, KT)
                act.wait_ge(s["normed"], m + 1)
                nc.scalar.activation(at(y, k, c), at(y, k, c), ACT.Copy,
                                     scale=kit.col("final_norm", k)).then_inc(s["scaled"], 1)

        @block.tensor
        def _(pe):
            for m in range(NC * KT):
                c, k = divmod(m, KT)
                pe.wait_ge(s["squared"], m + 1)
                nc.tensor.matmul(kit.banks[c][:, 0:CH], kit.ones[:], sq[:, m % 2], start=(k == 0),
                                 stop=(k == KT - 1)).then_inc(s["summed"], 1)

        @block.vector
        def _(dve):
            for c in range(NC):
                dve.wait_ge(s["rooted"], c + 1)
                nc.vector.reciprocal(inv[:, 1, c], inv[:, 0, c]).then_inc(s["inverted"], 1)
                dve.wait_ge(s["inverted"], c + 1)
                for k in range(KT):
                    nc.vector.tensor_tensor(at(y, k, c), at(kit.x, k, c), inv[:, 1, c], ALU.mult).then_inc(s["normed"], 1)

        @block.sync
        def _(sp):
            for m in range(NC * KT):
                c, k = divmod(m, KT)
                sp.wait_ge(s["scaled"], m + 1)
                sp.dma_start(out[k][:, c * CH:(c + 1) * CH], at(y, k, c)).then_inc(s["stored"], 16)
            sp.wait_ge(s["stored"], 16 * NC * KT)


def program(nc, dram, y_out, states_out):
    scratch = lambda name, shape, dt=F32: nc.dram_tensor(name, shape, dt).ap()
    mix, keys = scratch("mix", (J_END, P, T)), scratch("keys", (CT, P, T))
    x_saved = scratch("x_saved", (KT, P, T))
    with ExitStack() as ctx:
        kit = Kit(nc, ctx, dram)
        with kit.stage():
            modulation(kit)
        with kit.stage():
            ffn(kit, "ffn1", 0, "ffn1_w13", "ffn1_w2")
        with kit.stage():
            projection(kit, mix, x_saved)
        with ExitStack() as mixer:
            with kit.stage():
                cst = Constants(kit, mixer)
            with kit.stage():
                unit_keys(kit, mix, keys, cst)
            o, kd_sum = kit.x[:, 0:CT], kit.x[:, CT:KT]
            with kit.stage():
                scans(kit, cst, mix, keys, o, kd_sum, dram["states"], states_out)
            halves = [[mixer.enter_context(nc.sbuf_tensor(f"{branch}_{q}", [P, CT, T], F32R)) for q in ("hi", "lo")]
                      for branch in ("rwkv", "fourier")]
            with kit.stage():
                head_norm(kit, cst, mix, o, kd_sum, *halves[0])
            with kit.stage():
                fourier(kit, mix, *halves[1])
            with kit.stage():
                merge(kit, mix, halves, x_saved)
        with kit.stage():
            ffn(kit, "ffn2", 2, "ffn2_w13", "ffn2_w2")
        with kit.stage():
            final_norm(kit, y_out)


def mask_array():
    s, t = np.arange(P)[:, None], np.arange(P)[None, :]
    out = np.zeros((P, 2, 10, P), np.float32)
    for d in range(2):
        strict = (s // CK == t // CK) & ((s < t) if d == 0 else (s > t))
        incl = strict | (s == t)
        out[:, d, 0] = out[:, d, 2] = strict
        out[:, d, 1] = out[:, d, 3] = incl
        for l in range(6):
            m = 1 << l
            out[:, d, 4 + l] = strict & (s // (2 * m) == t // (2 * m)) & (s // m != t // m)
    return out


def reset_array():
    t = np.arange(T)
    return np.broadcast_to(np.stack([t % CK != 0, t % CK != CK - 1]), (P, 2, T)).astype(np.float32)


def dft_arrays():
    def parts(angle, n, sign):
        return np.stack([np.cos(angle), sign * np.sin(angle)], 1).astype(np.float64) / np.sqrt(n)
    j = np.arange(FD)
    features = parts(2 * np.pi * (np.outer(j, j) % FD) / FD, FD, 1).reshape(FD, 2 * FD)
    t = np.arange(T_CTX)
    context = parts(2 * np.pi * (np.outer(t, t) % T_CTX) / T_CTX, T_CTX, -1)
    wide, rows = 64, T_LAT // 64
    r, c = np.divmod(np.arange(T_LAT), wide)
    turns = (np.outer(r, r) % rows) / rows + (np.outer(c, c) % wide) / wide
    latents = parts(2 * np.pi * turns, T_LAT, -1).reshape(T_LAT // P, P, 2, T_LAT).transpose(0, 2, 1, 3)
    return [a.astype(np.float32) for a in (features, context, latents)]


def up_tiles(w, n):
    k = w.shape[0] // P
    return w.reshape(k, P, n, P).transpose(2, 1, 0, 3).reshape(n, P, k * P)


def kernel(x_prompt, x_sample, state_rwkv_fwd, state_rwkv_bwd, c, c_ctx, ada_w, ada_b, norm_w, ffn1_w13, ffn1_w2,
           ffn2_w13, ffn2_w2, w_in, gate_b, conv_rkv, w0, w_up, a0, a_up, g_up, k_k, k_a, r_k, lnx_w, lnx_b,
           w_o_rwkv, w_fourier, w_out, final_norm):
    import concourse.bacc as bacc
    from concourse.bass_utils import run_bass_kernel_spmd

    a = np.asarray
    vectors = dict(ada_b=ada_b, norm_w=norm_w, final_norm=final_norm, gate_b=gate_b, conv=conv_rkv, w0=w0, a0=a0,
                   k_k=k_k, k_a=k_a, r_k=r_k, lnx_w=lnx_w, lnx_b=lnx_b)
    rows = [a(vectors[n]).reshape(-1, P) for n in PACK if n != "c"] + [a(c_ctx).reshape(-1, P), a(c).reshape(-1, P)]
    features, context, latents = dft_arrays()
    pair_ones = np.kron(np.eye(2, dtype=np.float32), np.ones((HD, HD), np.float32))

    def w13(w):
        w = a(w)[0]
        return np.stack([up_tiles(w[:, :F_TILES * P], F_TILES), up_tiles(w[:, F_TILES * P:], F_TILES)])

    def states(s):
        return a(s).reshape(CT, 2, HD, HD).transpose(1, 3, 0, 2).reshape(P, CT, HD)
    arrays = {
        "vec": np.concatenate(rows, 0).T,
        "xT": np.concatenate([a(x_prompt)[0], a(x_sample)[0]], 0).T.reshape(KT, P, T),
        "ada_w": a(ada_w)[0].reshape(4, 2, P, 9, D).transpose(3, 0, 2, 1, 4),
        "select": np.equal(np.arange(P)[:, None] % 32, np.arange(2)).astype(np.float32),
        "ffn1_w13": w13(ffn1_w13), "ffn1_w2": a(ffn1_w2)[0].reshape(F_TILES, P, D),
        "ffn2_w13": w13(ffn2_w13), "ffn2_w2": a(ffn2_w2)[0].reshape(F_TILES, P, D),
        "w_in": up_tiles(a(w_in)[0], J_END),
        "lora_up": np.stack([a(w_up)[0].reshape(P, W), a(a_up)[0].reshape(P, W)], 1),
        "g_up": a(g_up)[0], "states": np.stack([states(state_rwkv_fwd), states(state_rwkv_bwd)]),
        "w_rwkv": up_tiles(a(w_o_rwkv)[0], KT), "w_fourier": up_tiles(a(w_fourier)[0], KT),
        "w_out": a(w_out)[0].reshape(KT, P, D),
        "masks": mask_array(), "reset": reset_array(), "squares": np.stack([np.eye(P, dtype=np.float32), pair_ones], 1),
        "dft_features": features, "dft_context": context, "dft_latents": latents,
    }
    arrays = {n: np.ascontiguousarray(v) for n, v in arrays.items()}
    nc = bacc.Bacc("TRN2", target_bir_lowering=False, num_devices=1)
    dram = {n: nc.dram_tensor("in_" + n, v.shape, F32, kind="ExternalInput").ap() for n, v in arrays.items()}
    y_out = nc.dram_tensor("out_y", (KT, P, T), F32, kind="ExternalOutput").ap()
    s_out = nc.dram_tensor("out_states", (2, P, CT, HD), F32, kind="ExternalOutput").ap()
    program(nc, dram, y_out, s_out)
    got = run_bass_kernel_spmd(nc, [{"in_" + n: v for n, v in arrays.items()}], core_ids=[0]).results[0]
    y = got["out_y"].reshape(D, T).T
    s = got["out_states"].reshape(2, 2, HD, CT, HD).transpose(0, 3, 1, 4, 2).reshape(2, 1, 1, HEADS, HD, HD)
    return (np.ascontiguousarray(y[None, :T_CTX]), np.ascontiguousarray(y[None, T_CTX:]),
            np.ascontiguousarray(s[0]), np.ascontiguousarray(s[1]))
```

```python
from contextlib import ExitStack, contextmanager

import numpy as np

import concourse.bass as bass
from concourse import mybir

ALU = mybir.AluOpType
ACT = mybir.ActivationFunctionType
F32 = mybir.dt.float32
F32R = mybir.dt.float32r

P = 128
D = 1024
KT = D // P
T_CTX = 128
T_LAT = 1024
T = T_CTX + T_LAT
CH = 384
NC = T // CH
F_TILES = 2816 // P
HEADS, HD = 8, 64
W = HEADS * HD
CT = W // P
CK = 64
FG, FD = 4, 128
LORA = 64
NTT = T // P
NORM_EPS = 1e-6
GN_EPS = 64e-5
DECAY_SCALE = float(np.exp(-0.5))
J_WD, J_AD, J_GD, J_F, J_GATE = 12, 13, 14, 15, 19
J_END = 35

PACK = {}
_at = 0
for _name, _n in (("ada_b", 72), ("norm_w", 24), ("final_norm", 8), ("gate_b", 16), ("conv", 36),
                  ("w0", 8), ("a0", 8), ("k_k", 4), ("k_a", 4), ("r_k", 4), ("lnx_w", 4),
                  ("lnx_b", 4), ("c", 16)):
    PACK[_name] = (_at, _n)
    _at += _n
PACK_W = _at


def segments(c):
    return [(0, 0, T_CTX), (1, T_CTX, CH)] if c == 0 else [(1, 0, CH)]


class Kit:

    def __init__(self, nc, ctx, dram):
        self.nc, self.ctx, self.dram = nc, ctx, dram
        self.banks = [ctx.enter_context(nc.psum_tensor(f"bank{b}", [P, 512], F32)) for b in range(8)]
        self.x = self.resident("x", [P, KT, T])
        self.vec = self.resident("vec", [P, PACK_W])
        self.mod = self.resident("mod", [P, 9, KT, 2])
        self.scale = self.resident("scale", [P, 3, KT, 2])
        self.gate = self.resident("gate", [P, 3, KT, 2])
        self.ones = self.resident("ones", [P, P])
        self.eps = self.resident("eps", [P, 2])
        self.passed = nc.alloc_semaphore("passed")

    def resident(self, name, shape, dt=F32):
        return self.ctx.enter_context(self.nc.sbuf_tensor(name, shape, dt))

    def sem(self, name):
        s = self.nc.alloc_semaphore(name)
        self.stage_sems.append(s)
        return s

    @contextmanager
    def stage(self):
        self.stage_sems = []
        yield
        self.nc.clear_and_free_semaphores(self.stage_sems)
        self.nc.all_engine_barrier()

    def col(self, name, i=0, n=1):
        a = PACK[name][0]
        return self.vec[:, a + i:a + i + n]

    def hold(self, eng, sem, value):
        eng.wait_ge(sem, value)
        eng.sem_inc(self.passed, 1)


def modulation(kit):
    nc = kit.nc
    loaded_vec, loaded_x, loaded_select = kit.sem("vec_loaded"), kit.sem("x_loaded"), kit.sem("select_loaded")
    loaded = [[kit.sem(f"ada_loaded{p}{g}") for g in range(4)] for p in range(2)]
    cleared, silu_ready, ones_ready = kit.sem("cond_cleared"), kit.sem("silu_ready"), kit.sem("ones_ready")
    rows_done, rows_ready, turned = kit.sem("mod_rows_done"), kit.sem("mod_rows_ready"), kit.sem("mod_turned")
    section_added, section_done = kit.sem("section_added"), kit.sem("section_done")
    HALF = D // 2
    with ExitStack() as ctx:
        raw = ctx.enter_context(nc.sbuf_tensor("ada_raw", [P, 2, 4, 2, D], F32))
        cs = ctx.enter_context(nc.sbuf_tensor("cond_silu", [P, KT, 32], F32))
        rows = ctx.enter_context(nc.sbuf_tensor("mod_rows", [P, 2, 2, HALF], F32))
        select = ctx.enter_context(nc.sbuf_tensor("select", [P, 2], F32))
        block = ctx.enter_context(nc.Block())

        @block.sync
        def _(sp):
            sp.dma_start(kit.vec[:], kit.dram["vec"]).then_inc(loaded_vec, 16)

            def section(i, par, first=False):
                if not first:
                    kit.hold(sp, rows_done, i * 2 - 2)
                for g in range(4):
                    sp.dma_start(raw[:, par, g], kit.dram["ada_w"][i, g]).then_inc(loaded[par][g], 16)
            section(0, 0, True)
            sp.dma_start(select[:], kit.dram["select"]).then_inc(loaded_select, 16)
            section(1, 1, True)
            for k in range(KT):
                sp.dma_start(kit.x[:, k, :], kit.dram["xT"][k]).then_inc(loaded_x, 16)
            section(2, 0)
            with sp.Fori(1, 4) as i:
                for par in range(2):
                    section(i * 2 + (1 + par), 1 - par)
            sp.wait_ge(loaded_x, 16 * KT)

        @block.gpsimd
        def _(pool):
            pool.memset(cs[:], 0.0).then_inc(cleared, 1)
            pool.memset(kit.ones[:], 1.0).then_inc(ones_ready, 1)
            pool.memset(kit.eps[:, 0:1], NORM_EPS).then_inc(ones_ready, 1)
            pool.memset(kit.eps[:, 1:2], GN_EPS).then_inc(ones_ready, 1)

        @block.scalar
        def _(act):
            act.wait_ge(loaded_vec, 16)
            act.wait_ge(cleared, 1)
            a = PACK["c"][0]
            for cond in range(2):
                nc.scalar.activation(cs[:, :, cond], kit.vec[:, a + 8 * cond:a + 8 * cond + 8],
                                     ACT.Silu).then_inc(silu_ready, 1)

            def section(i, par, first=False):
                for half in range(2):
                    act.wait_ge(rows_done, i * 2 + (half + 1))
                    if not first and half == 0:
                        act.wait_ge(turned, i - 1)
                    nc.scalar.activation(rows[:, par, half], kit.banks[2 * par + half][:], ACT.Copy)\
                        .then_inc(rows_ready, 1)
            section(0, 0, True)
            section(1, 1, True)
            section(2, 0)
            with act.Fori(1, 4) as i:
                for par in range(2):
                    section(i * 2 + (1 + par), 1 - par)

        @block.tensor
        def _(pe):
            pe.wait_ge(silu_ready, 2)

            def section(i, rank, par, first=False):
                for g in range(4):
                    pe.wait_ge(loaded[par][g], (rank + 1) * 16)
                if not first:
                    pe.wait_ge(rows_ready, i * 2 - 2)
                for half in range(2):
                    for kk in range(2):
                        for g in range(4):
                            mm = nc.tensor.matmul(kit.banks[2 * par + half][32 * g:32 * g + 32, :],
                                                  cs[:, 2 * g + kk, :],
                                                  raw[:, par, g, kk, half * HALF:(half + 1) * HALF],
                                                  start=(kk == 0), stop=(kk == 1))
                    mm.then_inc(rows_done, 1)

            def turn(i, par, early=False):
                pe.wait_ge(rows_ready, i * 2 + 2)
                if not early:
                    pe.wait_ge(section_added, i - 1)
                for mt in range(KT):
                    mm = nc.tensor.matmul(kit.banks[4 + par][:, 2 * mt:2 * mt + 2],
                                          rows[:, par, mt // 4, (mt % 4) * P:(mt % 4 + 1) * P], select[:],
                                          start=True, stop=True)
                mm.then_inc(turned, 1)
            section(0, 0, 0, True)
            pe.wait_ge(loaded_select, 16)
            section(1, 0, 1, True)
            turn(0, 0, True)
            section(2, 1, 0)
            turn(1, 1, True)
            with pe.Fori(1, 4) as i:
                section(i * 2 + 1, i, 1)
                turn(i * 2, 0)
                section(i * 2 + 2, i + 1, 0)
                turn(i * 2 + 1, 1)
            turn(8, 0)

        @block.vector
        def _(dve):
            dve.wait_ge(loaded_vec, 16)
            a = PACK["ada_b"][0]
            for i in range(9):
                dve.wait_ge(turned, i + 1)
                nc.vector.tensor_tensor(kit.mod[:, i], kit.banks[4 + i % 2][:, 0:2 * KT].rearrange("p (m c) -> p m c", c=2),
                                        kit.vec[:, a + i * KT:a + (i + 1) * KT].rearrange("p (m c) -> p m c", c=1)
                                        .broadcast_to([P, KT, 2]), ALU.add).then_inc(section_added, 1)
            dve.wait_ge(section_added, 9)
            a = PACK["norm_w"][0]
            for n in range(3):
                for cond in range(2):
                    ins = nc.vector.scalar_tensor_tensor(
                        kit.scale[:, n, :, cond], kit.mod[:, 3 * n + 1, :, cond], 1.0,
                        kit.vec[:, a + 8 * n:a + 8 * n + 8], ALU.add, ALU.mult)
                ins = nc.vector.tensor_scalar(kit.gate[:, n], kit.mod[:, 3 * n + 2],
                                              1.0 if n == 1 else 0.5, None, ALU.mult)
            ins.then_inc(section_done, 1)
            dve.wait_ge(section_done, 1)


class Norm:

    def __init__(self, kit, ctx, n, h_hi, h_lo):
        self.kit, self.n, self.h_hi, self.h_lo = kit, n, h_hi, h_lo
        buf = lambda name, shape: ctx.enter_context(kit.nc.sbuf_tensor(f"{name}_n{n}", shape, F32))
        self.sq = buf("square", [P, 3, 2, CH])
        self.rms = buf("rms", [P, CH])
        self.inv = buf("inv_rms", [P, 2, CH])
        self.xn = buf("x_normed", [P, 2, CH])
        self.full = buf("h_full", [P, 2, CH])
        self.sq_ready = [kit.sem(f"sq_ready_{o}_n{n}") for o in ("act", "dve", "pool")]
        (self.stat_done, self.rms_ready, self.inv_ready, self.xn_ready, self.hi_ready, self.full_ready,
         self.h_ready) = (kit.sem(f"{s}_n{n}") for s in (
             "stat_done", "rms_ready", "inv_ready", "xn_ready", "hi_ready", "full_ready", "h_ready"))
        self.order = [(0, k, k % 2) for k in range(KT)] + [(1, k, 2) for k in range(KT)] + [(2, k, 0) for k in range(KT)]

    def at(self, buf, k, c):
        return buf[:, k, c * CH:(c + 1) * CH]

    def squares(self, owner, eng, c, only=None):
        nc = self.kit.nc
        mine = [m for m, (_, _, o) in enumerate(self.order) if o == owner]
        for i, m in enumerate(mine):
            if self.order[m][0] != c or only not in (None, self.order[m][1]):
                continue
            k = self.order[m][1]
            if i >= 2:
                eng.wait_ge(self.stat_done, mine[i - 2] + 1)
            out, src = self.sq[:, owner, i % 2], self.at(self.kit.x, k, c)
            if owner == 0:
                ins = nc.scalar.activation(out, src, ACT.Square)
            elif owner == 1:
                ins = nc.vector.tensor_tensor(out, src, src, ALU.mult)
            else:
                ins = nc.gpsimd.tensor_tensor(out, src, src, ALU.mult)
            ins.then_inc(self.sq_ready[owner], 1)

    def tensor(self, pe):
        nc, kit = self.kit.nc, self.kit
        count = [0, 0, 0]
        for c, k, owner in self.order:
            pe.wait_ge(self.sq_ready[owner], count[owner] + 1)
            nc.tensor.matmul(kit.banks[4 + c][:, 0:CH], kit.ones[:], self.sq[:, owner, count[owner] % 2],
                             start=(k == 0), stop=(k == KT - 1)).then_inc(self.stat_done, 1)
            count[owner] += 1

    def scalar(self, act, split_weights):
        nc, kit = self.kit.nc, self.kit

        def root(c):
            act.wait_ge(self.stat_done, KT * (c + 1))
            if c:
                act.wait_ge(self.inv_ready, c)
            nc.scalar.activation(self.rms[:], kit.banks[4 + c][:, 0:CH], ACT.Sqrt, scale=1.0 / D,
                                 bias=kit.eps[:, 0:1]).then_inc(self.rms_ready, 1)
        self.squares(0, act, 0)
        split_weights()
        root(0)
        for m in range(NC * KT):
            c, k = divmod(m, KT)
            if k == 0 and c:
                root(c)
            act.wait_ge(self.xn_ready, m + 1)
            for cond, a, b in segments(c):
                ins = nc.scalar.activation(self.at(self.h_hi, k, c)[:, a:b], self.xn[:, m % 2, a:b], ACT.Identity,
                                           bias=kit.mod[:, 3 * self.n, k, cond:cond + 1],
                                           scale=kit.scale[:, self.n, k, cond:cond + 1])
            ins.then_inc(self.hi_ready, 1)
            if c == 0:
                self.squares(0, act, 2, k)

    def pool(self, pool):
        nc, kit = self.kit.nc, self.kit
        self.squares(2, pool, 1)
        for m in range(NC * KT):
            c, k = divmod(m, KT)
            pool.wait_ge(self.xn_ready, m + 1)
            if m >= 2:
                pool.wait_ge(self.h_ready, m - 1)
            for cond, a, b in segments(c):
                ins = nc.gpsimd.tensor_scalar(self.full[:, m % 2, a:b], self.xn[:, m % 2, a:b],
                                              kit.scale[:, self.n, k, cond:cond + 1],
                                              kit.mod[:, 3 * self.n, k, cond:cond + 1], ALU.mult, ALU.add)
            ins.then_inc(self.full_ready, 1)

    def vector(self, dve, split_weights):
        nc, kit = self.kit.nc, self.kit

        def low(m):
            c, k = divmod(m, KT)
            dve.wait_ge(self.hi_ready, m + 1)
            dve.wait_ge(self.full_ready, m + 1)
            nc.vector.tensor_tensor(self.at(self.h_lo, k, c), self.full[:, m % 2],
                                    self.at(self.h_hi, k, c).bitcast(F32), ALU.subtract).then_inc(self.h_ready, 1)
        self.squares(1, dve, 0)
        split_weights()
        for m in range(NC * KT):
            c, k = divmod(m, KT)
            if k == 0:
                if c:
                    low(m - 1)
                dve.wait_ge(self.rms_ready, c + 1)
                nc.vector.reciprocal(self.inv[:, c % 2], self.rms[:]).then_inc(self.inv_ready, 1)
                dve.wait_ge(self.inv_ready, c + 1)
            if m >= 2:
                dve.wait_ge(self.hi_ready, m - 1)
                dve.wait_ge(self.full_ready, m - 1)
            nc.vector.tensor_tensor(self.xn[:, m % 2], self.at(kit.x, k, c), self.inv[:, c % 2],
                                    ALU.mult).then_inc(self.xn_ready, 1)
            if k:
                low(m - 1)
        low(NC * KT - 1)


def hidden_stage(kit, tag, tiles, ku, w_up, w_down, norm, moving, combine, gate, load_x=None):
    nc = kit.nc
    kinds = ("a", "b", "d")
    loaded = {q: kit.sem(f"w{q}_loaded_{tag}") for q in kinds}
    w_hi_ready = {q: kit.sem(f"w{q}_hi_ready_{tag}") for q in kinds}
    w_ready = {q: kit.sem(f"w{q}_ready_{tag}") for q in kinds}
    up_done, act_ready = kit.sem(f"up_done_{tag}"), kit.sem(f"act_ready_{tag}")
    g32_ready, g_hi_ready, g_ready = (kit.sem(f"{s}_{tag}") for s in ("g32_ready", "g_hi_ready", "g_ready"))
    x_loaded = kit.sem(f"x_loaded_{tag}")
    down_done, x_added = kit.sem(f"down_done_{tag}"), kit.sem(f"x_added_{tag}")
    with ExitStack() as ctx:
        buf = lambda name, shape, dt=F32: ctx.enter_context(nc.sbuf_tensor(f"{name}_{tag}", shape, dt))
        width = {"a": ku * P, "b": ku * P, "d": D}
        raw = {q: buf(f"raw_{q}", [P, width[q]]) for q in kinds}
        whi = {q: buf(f"whi_{q}", [P, 2, width[q]], F32R) for q in kinds}
        wlo = {q: buf(f"wlo_{q}", [P, 2, width[q]], F32R) for q in kinds}
        g_hi, g_lo = buf("g_hi", [P, NC, CH], F32R), buf("g_lo", [P, NC, CH], F32R)
        act_out, g32 = buf("act_out", [P, 2, CH]), buf("g32", [P, 2, CH])
        norm_part, moving = (norm(ctx), None) if norm else (None, moving)
        if norm_part:
            moving = [(norm_part.h_hi, norm_part.h_lo)] * 2
        combine.setup(ctx)
        block = ctx.enter_context(nc.Block())
        source = {"a": w_up[0], "b": w_up[1], "d": w_down}

        @block.sync
        def _(sp):
            def load(q, f, first=False):
                if not first:
                    kit.hold(sp, w_ready[q], f)
                sp.dma_start(raw[q][:], source[q][f]).then_inc(loaded[q], 16)
                if q == "d":
                    combine.load(sp, f, first, g32_ready)
            for q in kinds:
                load(q, 0, True)
            if load_x:
                load_x(sp, x_loaded)
            with sp.Fori(1, tiles) as f:
                for q in kinds:
                    load(q, f)

        @block.scalar
        def _(act):
            def high(q, f, slot, first=False):
                act.wait_ge(loaded[q], (f + 1) * 16)
                if not first:
                    act.wait_ge(*((down_done, (f - 1) * 24) if q == "d" else (up_done, (f - 1) * 3)))
                nc.scalar.activation(whi[q][:, slot], raw[q][:], ACT.Copy).then_inc(w_hi_ready[q], 1)

            def step(f, c, par, early, last):
                n = f * 3 + c
                act.wait_ge(up_done, n + 1)
                if not (early and par == 0 and c < 2):
                    act.wait_ge(g32_ready, n - 1)
                slot = (3 * par + c) % 2
                combine.scalar(act, kit.banks[2 * slot][:, 0:CH], act_out[:, slot]).then_inc(act_ready, 1)
                act.wait_ge(g32_ready, n + 1)
                if not (early and par == 0):
                    act.wait_ge(down_done, (n - 2) * 8)
                nc.scalar.activation(g_hi[:, c], g32[:, slot], ACT.Copy).then_inc(g_hi_ready, 1)
                if not last:
                    high(kinds[c], f + 1, 1 - par, early and par == 0)

            def first_weights():
                for q in kinds:
                    high(q, 0, 0, True)
            if norm_part:
                norm_part.scalar(act, first_weights)
            else:
                first_weights()

            def pair(i, early=False, last=False):
                for par in range(2):
                    for c in range(NC):
                        step(i * 2 + par, c, par, early, last and par == 1)
            pair(0, early=True)
            with act.Fori(1, tiles // 2 - 1) as i:
                pair(i)
            pair(tiles // 2 - 1, last=True)

        @block.vector
        def _(dve):
            def low(q, f, slot):
                dve.wait_ge(w_hi_ready[q], f + 1)
                nc.vector.tensor_tensor(wlo[q][:, slot], raw[q][:], whi[q][:, slot].bitcast(F32),
                                        ALU.subtract).then_inc(w_ready[q], 1)

            def add_to_x(n, c):
                for d in range(KT):
                    m = n * 8 + d
                    dve.wait_ge(down_done, m + 1)
                    for cond, a, b in segments(c):
                        xs = kit.x[:, d, c * CH + a:c * CH + b]
                        ins = nc.vector.scalar_tensor_tensor(xs, kit.banks[4 + d % 4][:, a:b],
                                                             kit.gate[:, gate, d, cond:cond + 1], xs,
                                                             ALU.mult, ALU.add)
                    ins.then_inc(x_added, 1)

            def step(f, c, par, early, last):
                n = f * 3 + c
                slot = (3 * par + c) % 2
                dve.wait_ge(act_ready, n + 1)
                if not (early and par == 0 and c < 2):
                    dve.wait_ge(g_ready, n - 1)
                combine.vector(dve, f, n, c, kit.banks[2 * slot + 1][:, 0:CH], act_out[:, slot], g32[:, slot],
                               g32_ready)
                if load_x and early and par == 0 and c == 1:
                    dve.wait_ge(x_loaded, 16 * KT)
                if not (early and par == 0 and c == 0):
                    add_to_x(n - 1, (c - 1) % NC)
                dve.wait_ge(g_hi_ready, n + 1)
                nc.vector.tensor_tensor(g_lo[:, c], g32[:, slot], g_hi[:, c].bitcast(F32),
                                        ALU.subtract).then_inc(g_ready, 1)
                if not last:
                    low(kinds[c], f + 1, 1 - par)

            def first_weights():
                for q in kinds:
                    low(q, 0, 0)
            if norm_part:
                norm_part.vector(dve, first_weights)
            else:
                first_weights()

            def pair(i, early=False, last=False):
                for par in range(2):
                    for c in range(NC):
                        step(i * 2 + par, c, par, early, last and par == 1)
            pair(0, early=True)
            with dve.Fori(1, tiles // 2 - 1) as i:
                pair(i)
            pair(tiles // 2 - 1, last=True)
            add_to_x(tiles * 3 - 1, NC - 1)
            dve.wait_ge(x_added, tiles * 24)

        @block.gpsimd
        def _(pool):
            if norm_part:
                norm_part.pool(pool)
            if not combine.on_pool:
                return

            def pair(i, early=False):
                for par in range(2):
                    for c in range(NC):
                        n, slot = (i * 2 + par) * 3 + c, (3 * par + c) % 2
                        pool.wait_ge(act_ready, n + 1)
                        if not (early and par == 0 and c < 2):
                            pool.wait_ge(g_ready, n - 1)
                        combine.pool(pool, i * 2 + par, n, c, act_out[:, slot], g32[:, slot], g32_ready)
            pair(0, early=True)
            with pool.Fori(1, tiles // 2) as i:
                pair(i)

        @block.tensor
        def _(pe):
            if norm_part:
                norm_part.tensor(pe)

            def up(f, c, par, early):
                n = f * 3 + c
                slot = (3 * par + c) % 2
                if norm_part and early and par == 0:
                    pe.wait_ge(norm_part.h_ready, KT * (c + 1))
                if c == 0:
                    pe.wait_ge(w_ready["a"], f + 1)
                    pe.wait_ge(w_ready["b"], f + 1)
                if not (early and par == 0 and c < 2):
                    pe.wait_ge(g32_ready, n - 1)
                for j, q in enumerate("ab"):
                    hi, lo = moving[j]
                    for k in range(ku):
                        cols, toks = slice(k * P, (k + 1) * P), slice(c * CH, (c + 1) * CH)
                        for m, (w, v) in enumerate(((wlo, hi), (whi, lo), (whi, hi))):
                            mm = nc.tensor.matmul(kit.banks[2 * slot + j][:, 0:CH], w[q][:, par, cols],
                                                  v[:, k, toks], start=(k == 0 and m == 0),
                                                  stop=(k == ku - 1 and m == 2))
                mm.then_inc(up_done, 1)


            def step(f, c, par, early):
                up(f, c, par, early)
                if early and par == 0 and c == 0:
                    return
                if c == 1:
                    pe.wait_ge(w_ready["d"], f + 1)
                prev_c = (c - 1) % NC
                down_of(f * 3 + c - 1, prev_c, par if c else 1 - par, early and par == 0 and c == 1)

            def down_of(n, c, par, first):
                pe.wait_ge(g_ready, n + 1)
                for d in range(KT):
                    if not (first and d < 4):
                        pe.wait_ge(x_added, n * 8 + d - 3)
                    cols = slice(d * P, (d + 1) * P)
                    for m, (w, v) in enumerate(((wlo, g_hi), (whi, g_lo), (whi, g_hi))):
                        mm = nc.tensor.matmul(kit.banks[4 + d % 4][:, 0:CH], w["d"][:, par, cols], v[:, c],
                                              start=(m == 0), stop=(m == 2))
                    mm.then_inc(down_done, 1)

            for par in range(2):
                for c in range(NC):
                    step(par, c, par, True)
            with pe.Fori(1, tiles // 2) as i:
                for par in range(2):
                    for c in range(NC):
                        step(i * 2 + par, c, par, False)
            down_of(tiles * 3 - 1, NC - 1, 1, False)


class SwiGLU:

    on_pool = False

    def __init__(self, nc):
        self.nc = nc

    def setup(self, ctx):
        pass

    def load(self, sp, f, first, g32_ready):
        pass

    def scalar(self, act, a, out):
        return self.nc.scalar.activation(out, a, ACT.Silu)

    def vector(self, dve, f, n, c, b, act_out, g32, g32_ready):
        self.nc.vector.tensor_tensor(g32, act_out, b, ALU.mult).then_inc(g32_ready, 1)


def ffn(kit, tag, n, w13, w2):
    def norm(ctx):
        h_hi = ctx.enter_context(kit.nc.sbuf_tensor(f"h_hi_{tag}", [P, KT, T], F32R))
        h_lo = ctx.enter_context(kit.nc.sbuf_tensor(f"h_lo_{tag}", [P, KT, T], F32R))
        return Norm(kit, ctx, n, h_hi, h_lo)
    hidden_stage(kit, tag, F_TILES, KT, (kit.dram[w13][0], kit.dram[w13][1]), kit.dram[w2], norm, None,
                 SwiGLU(kit.nc), n)


class Constants:

    def __init__(self, kit, ctx):
        self.squares = ctx.enter_context(kit.nc.sbuf_tensor("squares", [P, 2, P], F32))
        self.ident, self.pair_ones = self.squares[:, 0], self.squares[:, 1]
        self.one_minus_ka = ctx.enter_context(kit.nc.sbuf_tensor("one_minus_ka", [P, CT], F32))


class UnitKeys:

    def __init__(self, kit, ctx, mix, keys, cst):
        self.kit, self.nc, self.mix, self.keys, self.cst = kit, kit.nc, mix, keys, cst
        buf = lambda name: ctx.enter_context(kit.nc.sbuf_tensor(name, [P, T], F32))
        self.raw, self.kk, self.sq = buf("uk_raw"), buf("uk_scaled"), buf("uk_square")
        self.s = {q: kit.sem("uk_" + q) for q in ("loaded", "scaled", "squared", "summed", "rooted", "guarded",
                                                  "inverted", "ready", "stored")}
        self.part = lambda c: slice(c * CH, (c + 1) * CH)

    def load(self, sp, ct, first):
        if not first:
            self.kit.hold(sp, self.s["ready"], ct * NC)
        sp.dma_start(self.raw[:], self.mix[ct + CT]).then_inc(self.s["loaded"], 16)

    def store(self, sp, ct):
        self.kit.hold(sp, self.s["ready"], ct * NC + NC)
        sp.dma_start(self.keys[ct], self.kk[:]).then_inc(self.s["stored"], 16)

    def scale(self, dve, ct, first):
        dve.wait_ge(self.s["loaded"], ct * 16 + 16)
        if not first:
            self.kit.hold(dve, self.s["stored"], ct * 16)
        self.nc.vector.tensor_scalar(self.kk[:], self.raw[:], self.kit.vec[:, bass.ds(ct + PACK["k_k"][0], 1)], None,
                                     ALU.mult).then_inc(self.s["scaled"], 1)

    def square(self, act, ct):
        act.wait_ge(self.s["scaled"], ct + 1)
        self.nc.scalar.activation(self.sq[:], self.kk[:], ACT.Square).then_inc(self.s["squared"], 1)

    def sums(self, pe, ct):
        pe.wait_ge(self.s["squared"], ct + 1)
        for c in range(NC):
            if c == 2:
                pe.wait_ge(self.s["rooted"], ct * NC + 1)
            self.nc.tensor.matmul(self.kit.banks[6 + c % 2][:, 0:CH], self.cst.pair_ones, self.sq[:, self.part(c)],
                                  start=True, stop=True).then_inc(self.s["summed"], 1)

    def roots(self, act, ct):
        for c in range(NC):
            act.wait_ge(self.s["summed"], ct * NC + (c + 1))
            self.nc.scalar.activation(self.raw[:, self.part(c)], self.kit.banks[6 + c % 2][:, 0:CH],
                                      ACT.Sqrt).then_inc(self.s["rooted"], 1)

    def divide(self, dve, ct):
        s, part = self.s, self.part
        for c in range(NC):
            m = ct * NC + (c + 1)
            dve.wait_ge(s["rooted"], m)
            self.nc.vector.tensor_scalar(self.raw[:, part(c)], self.raw[:, part(c)], 1e-12, None,
                                         ALU.max).then_inc(s["guarded"], 1)
            dve.wait_ge(s["guarded"], m)
            self.nc.vector.reciprocal(self.sq[:, part(c)], self.raw[:, part(c)]).then_inc(s["inverted"], 1)
            dve.wait_ge(s["inverted"], m)
            self.nc.vector.tensor_tensor(self.kk[:, part(c)], self.kk[:, part(c)], self.sq[:, part(c)],
                                         ALU.mult).then_inc(s["ready"], 1)


def projection(kit, mix, x_saved, keys, cst):
    nc = kit.nc
    saved = kit.sem("x_saved")
    loaded, w_hi_ready, w_ready = kit.sem("win_loaded"), kit.sem("win_hi_ready"), kit.sem("win_ready")
    proj_done, evicted = kit.sem("proj_done"), kit.sem("proj_evicted")
    pads_ready, tap_done, row_ready = (kit.sem(s) for s in ("pads_ready", "tap_done", "row_ready"))
    stored = [kit.sem(f"row_stored{p}") for p in range(2)]
    with ExitStack() as ctx:
        buf = lambda name, shape, dt=F32: ctx.enter_context(nc.sbuf_tensor(name, shape, dt))
        h_hi, h_lo = buf("h_hi_mix", [P, KT, T], F32R), buf("h_lo_mix", [P, KT, T], F32R)
        norm = Norm(kit, ctx, 1, h_hi, h_lo)
        raw = buf("raw_in", [P, D])
        whi, wlo = buf("whi_in", [P, 2, D], F32R), buf("wlo_in", [P, 2, D], F32R)
        padded = buf("u_padded", [P, 2, T + 4])
        taps = buf("taps", [P, 3])
        row = buf("row_out", [P, 2, T + 4])
        taps_ready, const_loaded, const_ready = (kit.sem(q) for q in ("taps_ready", "const_loaded", "const_ready"))
        unit = UnitKeys(kit, ctx, mix, keys, cst)
        block = ctx.enter_context(nc.Block())
        CONV, LORA_, PLAIN, GATE = range(4)
        nothing = lambda ct: None

        def kind_of(j):
            return CONV if j < J_WD else LORA_ if j < J_F else PLAIN if j < J_GATE else GATE

        def stored_before(rank):
            if isinstance(rank, int):
                return 32 * min(rank, J_WD // 2) + 16 * max(0, rank - J_WD // 2)
            return rank * 16 + 16 * (J_WD // 2)

        def schedule(eng, step, mid, end):
            for j in range(2):
                step(j, j, kind_of(j), 0)
            with eng.Fori(1, J_WD // 2) as i:
                for par in range(2):
                    step(i * 2 + par, par, CONV, i)
            for j in range(J_WD, J_GATE + 2):
                step(j, j % 2, kind_of(j), j // 2)
            first = J_GATE + 2
            def gates(i, keys_beside=True):
                for o in range(2):
                    step(i * 2 + (first + o), (first + o) % 2, GATE, i + (first + o) // 2)
                    if keys_beside:
                        (mid, end)[o](i)
            gates(0)
            with eng.Fori(1, CT) as i:
                gates(i)
            with eng.Fori(CT, (J_END - first) // 2 - 1) as i:
                gates(i, False)
            for j in range(J_END - 2, J_END):
                step(j, j % 2, GATE, j // 2)

        @block.sync
        def _(sp):
            sp.dma_start(raw[:], kit.dram["w_in"][0]).then_inc(loaded, 16)
            sp.dma_start(cst.squares[:], kit.dram["squares"]).then_inc(const_loaded, 16)
            for k in range(KT):
                sp.dma_start(x_saved[k], kit.x[:, k]).then_inc(saved, 16)

            def step(j, par, kind, rank):
                if not (isinstance(j, int) and j == J_END - 1):
                    kit.hold(sp, w_ready, j + 1)
                    sp.dma_start(raw[:], kit.dram["w_in"][j + 1]).then_inc(loaded, 16)
                kit.hold(sp, row_ready, j + 1)
                if kind == CONV:
                    sp.dma_start(mix[j][:, 0:T_CTX], row[:, par, 1:T_CTX + 1]).then_inc(stored[par], 16)
                    sp.dma_start(mix[j][:, T_CTX:T], row[:, par, T_CTX + 3:T + 3]).then_inc(stored[par], 16)
                else:
                    sp.dma_start(mix[j], row[:, par, 0:T]).then_inc(stored[par], 16)

            def mid(ct):
                first = isinstance(ct, int) and ct == 0
                if first:
                    for par in range(2):
                        sp.wait_ge(stored[par], stored_before((J_GATE + 4 - par) // 2))
                else:
                    unit.store(sp, ct - 1)
                unit.load(sp, ct, first)
            schedule(sp, step, mid, nothing)
            unit.store(sp, CT - 1)
            sp.wait_ge(unit.s["stored"], 16 * CT)
            sp.wait_ge(const_loaded, 16)
            for par in range(2):
                sp.wait_ge(stored[par], stored_before((J_END + 1 - par) // 2))
            sp.wait_ge(saved, 16 * KT)

        @block.scalar
        def _(act):
            def high(j, slot, first=False):
                act.wait_ge(loaded, (j + 1) * 16)
                if not first:
                    act.wait_ge(proj_done, (j - 1) * 3)
                nc.scalar.activation(whi[:, slot], raw[:], ACT.Copy).then_inc(w_hi_ready, 1)
            norm.scalar(act, lambda: high(0, 0, True))

            def step(j, par, kind, rank):
                if kind == CONV and not (isinstance(j, int) and j < 2):
                    act.wait_ge(row_ready, j - 1)
                if kind != CONV:
                    act.wait_ge(stored[par], stored_before(rank))
                for c in range(NC):
                    n = j * 3 + c
                    kit.hold(act, proj_done, n + 1)
                    src = kit.banks[3 * par + c]
                    if kind == CONV:
                        for cond, a, b in segments(c):
                            at = c * CH + a + 1 + 2 * cond
                            ins = nc.scalar.activation(padded[:, par, at:at + b - a], src[:, a:b], ACT.Copy)
                    elif kind == LORA_:
                        func = {J_WD: ACT.Tanh, J_AD: ACT.Copy, J_GD: ACT.Sigmoid}[j]
                        ins = nc.scalar.activation(row[:, par, c * CH:(c + 1) * CH], src[:, 0:CH], func)
                    elif kind == PLAIN:
                        ins = nc.scalar.activation(row[:, par, c * CH:(c + 1) * CH], src[:, 0:CH], ACT.Copy)
                    else:
                        g = PACK["gate_b"][0] - J_GATE
                        ins = nc.scalar.activation(row[:, par, c * CH:(c + 1) * CH], src[:, 0:CH], ACT.Sigmoid,
                                                   bias=kit.vec[:, bass.ds(j + g, 1)])
                    ins.then_inc(evicted, 1)
                    if c == 0 and not (isinstance(j, int) and j == J_END - 1):
                        high(j + 1, 1 - par, isinstance(j, int) and j == 0)
            schedule(act, step, lambda ct: unit.square(act, ct), lambda ct: unit.roots(act, ct))

        @block.vector
        def _(dve):
            def low(j, slot):
                dve.wait_ge(w_hi_ready, j + 1)
                nc.vector.tensor_tensor(wlo[:, slot], raw[:], whi[:, slot].bitcast(F32),
                                        ALU.subtract).then_inc(w_ready, 1)
            for par in range(2):
                for a, b in ((0, 1), (T_CTX + 1, T_CTX + 3), (T + 3, T + 4)):
                    nc.vector.memset(padded[:, par, a:b], 0.0).then_inc(pads_ready, 1)
            dve.wait_ge(pads_ready, 6)
            nc.vector.tensor_scalar(cst.one_minus_ka[:], kit.col("k_a", 0, CT), -1.0, 1.0,
                                    ALU.mult, ALU.add).then_inc(const_ready, 1)
            dve.wait_ge(const_ready, 1)
            norm.vector(dve, lambda: low(0, 0))
            conv = PACK["conv"][0]

            def step(j, par, kind, rank):
                if not (isinstance(j, int) and j == J_END - 1):
                    low(j + 1, 1 - par)
                if kind != CONV:
                    dve.wait_ge(evicted, j * 3 + 3)
                    dve.sem_inc(row_ready, 1)
                    return
                for t in range(3):
                    ins = nc.vector.tensor_copy(taps[:, t:t + 1], kit.vec[:, bass.ds(j + (conv + 12 * t), 1)])
                ins.then_inc(taps_ready, 1)
                dve.wait_ge(taps_ready, j + 1)
                dve.wait_ge(evicted, j * 3 + 3)
                if not (isinstance(j, int) and j < 2):
                    dve.wait_ge(stored[par], rank * 32)
                out = row[:, par, 1:T + 3]
                nc.vector.tensor_scalar(out, padded[:, par, 0:T + 2], taps[:, 0:1], None, ALU.mult).then_inc(tap_done, 1)
                for t in (1, 2):
                    dve.wait_ge(tap_done, j * 2 + t)
                    ins = nc.vector.scalar_tensor_tensor(out, padded[:, par, t:T + 2 + t], taps[:, t:t + 1], out,
                                                         ALU.mult, ALU.add)
                    ins.then_inc(tap_done if t == 1 else row_ready, 1)
            schedule(dve, step, lambda ct: unit.scale(dve, ct, isinstance(ct, int) and ct == 0),
                     lambda ct: unit.divide(dve, ct))

        @block.gpsimd
        def _(pool):
            norm.pool(pool)

        @block.tensor
        def _(pe):
            norm.tensor(pe)

            def step(j, par, early=False):
                for c in range(NC):
                    if early and par == 0:
                        pe.wait_ge(norm.h_ready, KT * (c + 1))
                    if c == 0:
                        pe.wait_ge(w_ready, j + 1)
                    if not early:
                        pe.wait_ge(evicted, j * 3 + c - 5)
                    for k in range(KT):
                        cols, toks = slice(k * P, (k + 1) * P), slice(c * CH, (c + 1) * CH)
                        for m, (w, v) in enumerate(((wlo, h_hi), (whi, h_lo), (whi, h_hi))):
                            mm = nc.tensor.matmul(kit.banks[3 * par + c][:, 0:CH], w[:, par, cols], v[:, k, toks],
                                                  start=(k == 0 and m == 0), stop=(k == KT - 1 and m == 2))
                    mm.then_inc(proj_done, 1)
            for j in range(2):
                step(j, j, True)
            pairs = J_END // 2
            keys_from = (J_GATE + 2) // 2
            with pe.Fori(1, keys_from) as i:
                for par in range(2):
                    step(i * 2 + par, par)
            step(2 * keys_from, 0)
            pe.wait_ge(const_loaded, 16)
            with pe.Fori(0, CT) as ct:
                for o in range(2):
                    step(ct * 2 + (2 * keys_from + 1 + o), (1 + o) % 2)
                unit.sums(pe, ct)
            with pe.Fori(keys_from + CT, pairs) as i:
                for par in (1, 2):
                    step(i * 2 + par, par % 2)


def scans(kit, cst, mix, keys, o, kd_sum, states_in, states_out):
    nc = kit.nc
    sem_names = ("lora_in", "lora_done", "lam_ready", "a_ready", "cum_ready", "state_loaded", "state_stored",
                 "pads", "loaded", "v_loaded", "g_ready", "ig_ready", "t_ready", "kka_ready", "kd_ready",
                 "sum_ready", "wide_ready", "turned", "tall_ready", "am_done", "am_ready", "y_done", "y_ready",
                 "wy_done", "wy_ready", "wa_done", "wa_ready", "u_done", "u_ready", "z_done", "z_summed",
                 "z_ready", "o_done", "o_ready", "lora_w_in", "masks_in")
    S = {q: kit.sem("sc_" + q) for q in sem_names}
    G2 = {q: [kit.sem(f"sc_{q}{g}") for g in range(2)]
          for q in ("level_ready", "v_ready", "w_done", "w_ready", "p_done", "p_ready", "v_done")}
    LEVELS = 6
    with ExitStack() as ctx:
        buf = lambda name, shape, dt=F32: ctx.enter_context(nc.sbuf_tensor(name, shape, dt))
        masks = buf("masks", [P, 2, 8, P])
        lora_w = buf("lora_w", [P, 2, W])
        cum, a_all = buf("cum_decay", [P, CT, T]), buf("a_all", [P, CT, T])
        rt, kt, vt, kkt = (buf(f"{n}_tile", [P, CT, P]) for n in ("r", "k", "v", "kk"))
        g_pads, inv_g = buf("g_pad", [P, 2, CT, 2, CK + 1]), buf("inv_g", [P, CT, P])
        t_ka, kd = buf("t_ka", [P, CT, P]), buf("kd", [P, CT, P])
        ars = buf("a_r_wide", [P, 2, CT, 2, P])
        b_wide, k_wide = buf("b_wide", [P, CT, P]), buf("k_wide", [P, CT, P])
        a_tall = buf("a_tall", [P, W])
        k_talls, b_talls, v_talls = (buf(f"{n}_tall", [P, 2, W]) for n in ("k", "b", "v"))
        ams = buf("am", [P, 2 * HEADS * 4 * P])
        level = buf("n_level", [P, 2, 2, 4, P])
        v_inv, w_inv = (buf(n, [P, 2, 4, P]) for n in ("inv_t", "inv"))
        prod = w_inv
        y_tall, wy_tall, u_tall = (buf(n, [P, W]) for n in ("y_tall", "wy_tall", "u_tall"))
        wa = buf("wa_wide", [P, CT, P])
        z, z_sum = buf("z", [P, CT, HD]), buf("z_sum", [P, CT, HD])
        lora, reset, lam = (ams[:, m * T:(m + 1) * T] for m in range(3))
        block = ctx.enter_context(nc.Block())
        bank = kit.banks
        g_pad_of = lambda i: g_pads[:, i % 2]
        ar_of = lambda i: ars[:, i % 2]
        am_of = lambda i: ams[:, i % 2 * (HEADS * 4 * P):(i % 2 + 1) * (HEADS * 4 * P)].rearrange(
            "p (h m t) -> p h m t", h=HEADS, m=4)
        tall_of = lambda i: (a_tall[:], k_talls[:, i % 2], b_talls[:, i % 2], v_talls[:, i % 2])

        class Tile:

            def __init__(self, d, i, par):
                self.d, self.par, self.first = d, par, isinstance(i, int) and i == 0
                self.s = i + d * NTT
                self.tau = i * P if d == 0 or self.first else i * (-P) + NTT * P
                self.before = self.s if self.first else self.s - 1
                self.very_first = self.first and d == 0
                self.slot_is_new = isinstance(self.s, int) and self.s <= 1

        def tile_schedule(eng, head, start, tile, between):
            for d in range(2):
                head(d)
                start(Tile(d, 0, 0))
                tile(Tile(d, 0, 0), Tile(d, 1, 1))
                between(d)
                with eng.Fori(0, (NTT - 3) // 2) as q:
                    tile(Tile(d, q * 2 + 1, 1), Tile(d, q * 2 + 2, 0))
                    tile(Tile(d, q * 2 + 2, 0), Tile(d, q * 2 + 3, 1))
                tile(Tile(d, NTT - 2, 1), Tile(d, NTT - 1, 0))
                tile(Tile(d, NTT - 1, 0), None)

        def cum_step(d, ct, c):
            return (d * CT + ct) * NC + c

        nothing = lambda *_: None
        AM_AT = {(2, 2): (0,), (3, 0): (1,), (3, 2): (2,), (4, 0): (3,), (4, 2): (4,), (5, 0): (5,), (5, 1): (6,),
                 (5, 2): (7,)}

        @block.sync
        def _(sp):
            def head(d):
                if d:
                    sp.wait_ge(S["o_done"], NTT)
                for m in range(2):
                    sp.dma_start(lora[LORA * m:LORA * (m + 1)], mix[J_WD + m][LORA * d:LORA * (d + 1)])\
                        .then_inc(S["lora_in"], 16)
                if d == 0:
                    sp.dma_start(lora_w[:], kit.dram["lora_up"]).then_inc(S["lora_w_in"], 16)
                sp.dma_start(reset, kit.dram["reset"]).then_inc(S["lora_in"], 16)
                if d == 0:
                    sp.dma_start(masks[:], kit.dram["masks"]).then_inc(S["masks_in"], 16)

            def load(n):
                at = bass.ds(n.tau, P)
                if not n.very_first:
                    kit.hold(sp, S["wide_ready"], n.s * 4)
                    kit.hold(sp, S["kd_ready"], n.s)
                for dst, src in ((rt, mix[0:CT]), (kt, mix[CT:2 * CT]), (kkt, keys)):
                    sp.dma_start(dst[:], src[:, :, at].rearrange("c p t -> p c t")).then_inc(S["loaded"], 16)
                if not n.very_first:
                    kit.hold(sp, S["turned"], n.s * 4)
                sp.dma_start(vt[:], mix[2 * CT:3 * CT, :, at].rearrange("c p t -> p c t")).then_inc(S["v_loaded"], 16)

            def tile(t, n):
                if n:
                    load(n)

            def between(d):
                sp.wait_ge(S["z_ready"], (d * NTT + 1) * 2)
                sp.dma_start(states_out[d], z[:]).then_inc(S["state_stored"], 16)
                sp.wait_ge(S["state_stored"], 16 * (d + 1))
                sp.wait_ge(S["o_done"], d * NTT + 1)
                sp.dma_start(z[:], states_in[d]).then_inc(S["state_loaded"], 16)
            tile_schedule(sp, head, load, tile, between)
            sp.wait_ge(S["state_stored"], 32)

        @block.gpsimd
        def _(pool):
            pool.wait_ge(S["masks_in"], 16)

            def head(d):
                pool.wait_ge(S["a_ready"], CT * NC * (d + 1))

            def keys_of(n):
                kit.hold(pool, S["loaded"], (n.s + 1) * 48)
                if not n.very_first:
                    kit.hold(pool, S["turned"], n.s * 4)
                nc.gpsimd.tensor_tensor(b_wide[:], kkt[:], a_all[:, :, bass.ds(n.tau, P)], ALU.mult)\
                    .then_inc(S["kka_ready"], 1)
                if not n.very_first:
                    kit.hold(pool, S["sum_ready"], n.s)
                pool.wait_ge(S["t_ready"], (n.s + 1) * CT)
                nc.gpsimd.tensor_tensor(kd[:], kt[:], t_ka[:], ALU.mult).then_inc(S["kd_ready"], 1)

            def sum_keys(n):
                at = bass.ds(n.tau, P)
                kit.hold(pool, S["kd_ready"], n.s + 1)
                if n.d == 0:
                    nc.gpsimd.tensor_copy(kd_sum[:, :, at], kd[:]).then_inc(S["sum_ready"], 1)
                else:
                    nc.gpsimd.tensor_tensor(kd_sum[:, :, at], kd_sum[:, :, at], kd[:], ALU.add).then_inc(S["sum_ready"], 1)

            def levels_of(t, which):
                for l in which:
                    for g in range(2):
                        if l == 0:
                            pool.wait_ge(S["am_ready"], t.s * 8 + (4 * g + 4))
                            if not t.very_first:
                                pool.wait_ge(G2["p_done"][g], t.s * 5 - 1)
                        if l == 1 and not t.very_first:
                            pool.wait_ge(G2["p_done"][g], t.s * 5)
                        if l == 2:
                            pool.wait_ge(G2["v_ready"][g], t.s * 6 + 1)
                        if l >= 3:
                            pool.wait_ge(G2["p_done"][g], t.s * 5 + (l - 2))
                        nc.gpsimd.tensor_tensor(level[:, g, l % 2], am_of(t.par)[:, 4 * g:4 * g + 4, 0],
                                                masks[:, t.d, 2 + l:3 + l].broadcast_to([P, 4, P]),
                                                ALU.mult).then_inc(G2["level_ready"][g], 1)

            def start(n):
                keys_of(n)
                sum_keys(n)
                levels_of(n, (0, 1))

            def tile(t, n):
                if n:
                    keys_of(n)
                levels_of(t, (2,))
                if n:
                    sum_keys(n)
                levels_of(t, (3, 4, 5))
                if n:
                    levels_of(n, (0, 1))
            tile_schedule(pool, head, start, tile, nothing)

        @block.scalar
        def _(act):
            copy = lambda out, src: nc.scalar.activation(out, src, ACT.Copy)

            def head(d):
                for ct in range(CT):
                    for c in range(NC):
                        n = cum_step(d, ct, c)
                        part = slice(c * CH, (c + 1) * CH)
                        act.wait_ge(S["lora_done"], 2 * n + 1)
                        if c == 0 and d * CT + ct:
                            act.wait_ge(S["cum_ready"], d * CT + ct)
                        nc.scalar.activation(lam[:, part], bank[n % 4][:, 0:CH], ACT.Sigmoid,
                                             bias=kit.col("w0", d * CT + ct)).then_inc(S["lam_ready"], 1)
                        act.wait_ge(S["lora_done"], 2 * n + 2)
                        nc.scalar.activation(a_all[:, ct, part], bank[4 + n % 4][:, 0:CH], ACT.Sigmoid,
                                             bias=kit.col("a0", d * CT + ct)).then_inc(S["a_ready"], 1)
                act.wait_ge(S["cum_ready"], CT * (d + 1))
                act.wait_ge(S["a_ready"], CT * NC * (d + 1))
                act.wait_ge(S["pads"], 2 * d + 2)

            def decays_of(n):
                at, g_pad = bass.ds(n.tau, P), g_pad_of(n.par)
                body = slice(1, CK + 1) if n.d == 0 else slice(0, CK)
                if not n.slot_is_new:
                    kit.hold(act, S["z_ready"], n.before * 2)
                nc.scalar.activation(g_pad[:, :, :, body], cum[:, :, at].rearrange("p c (k t) -> p c k t", k=2),
                                     ACT.Exp, scale=-DECAY_SCALE).then_inc(S["g_ready"], 1)

            def rates_of(n):
                at = bass.ds(n.tau, P)
                if not n.very_first:
                    kit.hold(act, S["wide_ready"], n.s * 4)
                    kit.hold(act, S["kd_ready"], n.s)
                nc.scalar.activation(inv_g[:], cum[:, :, at], ACT.Exp, scale=DECAY_SCALE).then_inc(S["ig_ready"], 1)
                for ct in range(CT):
                    nc.scalar.activation(t_ka[:, ct], a_all[:, ct, at], ACT.Identity, scale=kit.col("k_a", ct),
                                         bias=cst.one_minus_ka[:, ct:ct + 1]).then_inc(S["t_ready"], 1)

            def tall_copies(n):
                for m, dst in enumerate(tall_of(n.par)):
                    act.wait_ge(S["turned"], n.s * 4 + (m + 1))
                    copy(dst, bank[m][:]).then_inc(S["tall_ready"], 1)

            def start(n):
                decays_of(n)
                rates_of(n)
                tall_copies(n)

            def tile(t, n):
                if n:
                    decays_of(n)
                for l in range(1, LEVELS):
                    for g in range(2):
                        act.wait_ge(G2["w_done"][g], t.s * 5 + l)
                        copy(w_inv[:, g], bank[2 * g][:]).then_inc(G2["w_ready"][g], 1)
                    if n and l == 1:
                        rates_of(n)
                    for g in range(2):
                        act.wait_ge(G2["p_done"][g], t.s * 5 + l)
                        copy(prod[:, g], bank[2 * g][:]).then_inc(G2["p_ready"][g], 1)
                    if l == 1:
                        act.wait_ge(S["y_done"], t.s + 1)
                        copy(y_tall[:], bank[4][:]).then_inc(S["y_ready"], 1)
                act.wait_ge(S["wy_done"], t.s + 1)
                copy(wy_tall[:], bank[5][:]).then_inc(S["wy_ready"], 1)
                act.wait_ge(S["wa_done"], t.s + 1)
                copy(wa[:], bank[6][:]).then_inc(S["wa_ready"], 1)
                if n:
                    tall_copies(n)
            tile_schedule(act, head, start, tile, nothing)

        @block.vector
        def _(dve):

            def head(d):
                dve.wait_ge(S["lora_in"], 48 * (d + 1))
                for ct in range(CT):
                    dve.wait_ge(S["lam_ready"], cum_step(d, ct, NC))
                    way = slice(None, None, 1 if d == 0 else -1)
                    nc.vector.tensor_tensor_scan(cum[:, ct, way], reset, lam[:, way], 0.0,
                                                 ALU.mult, ALU.add).then_inc(S["cum_ready"], 1)
                edge = 0 if d == 0 else CK
                nc.vector.memset(g_pads[:, :, :, :, edge:edge + 1], 1.0).then_inc(S["pads"], 1)
                nc.vector.memset(z[:], 0.0).then_inc(S["pads"], 1)
                dve.wait_ge(S["pads"], 2 * d + 2)
                dve.wait_ge(S["masks_in"], 16)

            by_chunk = lambda v: v.rearrange("p c (k t) -> p c k t", k=2)

            def wide_a_r(n):
                before, upto = (slice(0, CK), slice(1, CK + 1)) if n.d == 0 else (slice(1, CK + 1), slice(0, CK))
                ar, g_pad = ar_of(n.par), g_pad_of(n.par)
                dve.wait_ge(S["loaded"], (n.s + 1) * 48)
                dve.wait_ge(S["g_ready"], n.s + 1)
                if not n.slot_is_new:
                    dve.wait_ge(S["o_done"], n.before)
                nc.vector.tensor_tensor(by_chunk(ar[:, :, 0]), by_chunk(kkt[:]), g_pad[:, :, :, before],
                                        ALU.mult).then_inc(S["wide_ready"], 1)
                nc.vector.tensor_tensor(by_chunk(ar[:, :, 1]), by_chunk(rt[:]), g_pad[:, :, :, upto],
                                        ALU.mult).then_inc(S["wide_ready"], 1)

            def wide_b_k(n):
                dve.wait_ge(S["ig_ready"], n.s + 1)
                dve.wait_ge(S["kka_ready"], n.s + 1)
                if not n.very_first:
                    dve.wait_ge(S["turned"], n.s * 4)
                nc.vector.scalar_tensor_tensor(b_wide[:], b_wide[:], -1.0, inv_g[:], ALU.mult, ALU.mult)\
                    .then_inc(S["wide_ready"], 1)
                dve.wait_ge(S["kd_ready"], n.s + 1)
                nc.vector.tensor_tensor(k_wide[:], kd[:], inv_g[:], ALU.mult).then_inc(S["wide_ready"], 1)

            def mask_am(n, heads):
                rep = masks[:, n.d, 0:2].rearrange("p (q m) t -> p q m t", q=1).broadcast_to([P, 2, 2, P])
                for h in heads:
                    dve.wait_ge(S["am_done"], n.s * 8 + (h + 1))
                    nc.vector.tensor_tensor(am_of(n.par)[:, h].rearrange("p (q m) t -> p q m t", q=2),
                                            bank[5 + h % 2][:].rearrange("p (q m t) -> p q m t", q=2, m=2),
                                            rep, ALU.mult).then_inc(S["am_ready"], 1)

            def first_inverse(n, groups=(0, 1)):
                for g in groups:
                    dve.wait_ge(G2["level_ready"][g], n.s * 6 + 1)
                    if not n.very_first:
                        dve.wait_ge(S["wa_done"], n.s)
                    nc.vector.tensor_tensor(v_inv[:, g], level[:, g, 0],
                                            cst.squares[:, 0:1].broadcast_to([P, 4, P]), ALU.add)\
                        .then_inc(G2["v_ready"][g], 1)

            def start(n):
                wide_a_r(n)
                wide_b_k(n)
                mask_am(n, range(HEADS))
                first_inverse(n)

            def tile(t, n):
                s, g_pad = t.s, g_pad_of(t.par)
                last = slice(CK, CK + 1) if t.d == 0 else slice(0, 1)
                if n:
                    wide_a_r(n)
                def masks_at(l, place):
                    if n:
                        mask_am(n, AM_AT.get((l, place), ()))
                for l in range(1, LEVELS):
                    masks_at(l, 0)
                    masks_at(l, 1)
                    for g in range(2):
                        dve.wait_ge(G2["v_done"][g], s * 5 + l)
                        nc.vector.tensor_tensor(v_inv[:, g], bank[2 * g + 1][:].rearrange("p (h t) -> p h t", h=4),
                                                v_inv[:, g], ALU.add).then_inc(G2["v_ready"][g], 1)
                    if n and l == 1:
                        wide_b_k(n)
                    masks_at(l, 2)
                for k, c in enumerate((0, 1) if t.d == 0 else (1, 0)):
                    m = s * 2 + k
                    rows = slice(CK * c, CK * c + CK)
                    by_head = lambda v: v[rows].rearrange("p (c e i) -> p c e i", e=2, i=HD)
                    dve.wait_ge(S["u_done"], m + 1)
                    if k == 0:
                        dve.wait_ge(S["wy_ready"], s + 1)
                    for e in range(2):
                        nc.vector.tensor_tensor(by_head(u_tall[:])[:, :, e],
                                                bank[4 + e][rows, 0:CT * HD].rearrange("p (c i) -> p c i", c=CT),
                                                by_head(wy_tall[:])[:, :, e], ALU.add).then_inc(S["u_ready"], 1)
                    if n and k:
                        first_inverse(n, (1,))
                    dve.wait_ge(S["z_done"], m + 1)
                    nc.vector.tensor_tensor(z_sum[:], bank[6][:, 0:CT * HD].rearrange("p (c i) -> p c i", c=CT), z[:],
                                            ALU.add).then_inc(S["z_summed"], 1)
                    dve.wait_ge(S["z_summed"], m + 1)
                    nc.vector.tensor_tensor(z[:], z_sum[:], g_pad[:, :, c, last].broadcast_to([P, CT, HD]),
                                            ALU.mult).then_inc(S["z_ready"], 1)
                    if n and k == 0:
                        first_inverse(n, (0,))
                kit.hold(dve, S["o_done"], s + 1)
                src, dst = bank[7][:].rearrange("p (c t) -> p c t", c=CT), o[:, :, bass.ds(t.tau, P)]
                if t.d == 0:
                    nc.vector.tensor_copy(dst, src).then_inc(S["o_ready"], 1)
                else:
                    nc.vector.tensor_tensor(dst, src, dst, ALU.add).then_inc(S["o_ready"], 1)
            tile_schedule(dve, head, start, tile, nothing)

        @block.tensor
        def _(pe):
            pe.wait_ge(S["lora_w_in"], 16)
            mm = nc.tensor.matmul
            hold = lambda q, v: kit.hold(pe, S[q], v)

            def head(d):
                if d:
                    pe.wait_ge(S["o_ready"], NTT)
                pe.wait_ge(S["lora_in"], 48 * (d + 1))
                for ct in range(CT):
                    for c in range(NC):
                        n = cum_step(d, ct, c)
                        part = slice(c * CH, (c + 1) * CH)
                        for m, ready in ((0, "lam_ready"), (1, "a_ready")):
                            if n >= 4:
                                pe.wait_ge(S[ready], n - 3)
                            rows = slice(LORA * m, LORA * (m + 1))
                            mm(bank[4 * m + n % 4][:, 0:CH], lora_w[rows, d, ct * P:(ct + 1) * P],
                               lora[rows, part], start=True, stop=True).then_inc(S["lora_done"], 1)
                pe.wait_ge(S["a_ready"], CT * NC * (d + 1))
                pe.wait_ge(S["lam_ready"], CT * NC * (d + 1))
                pe.wait_ge(S["pads"], 2 * d + 2)

            def am_products(n, heads):
                for h in heads:
                    ct, e = divmod(h, 2)
                    half = slice(64 * e, 64 * e + 64)
                    if h == 0:
                        hold("wide_ready", n.s * 4 + 4)
                    if h >= 2:
                        hold("am_ready", n.s * 8 + (h - 1))
                    both = ar_of(n.par)[half, ct].rearrange("p m t -> p (m t)")
                    mm(bank[5 + h % 2][:, 0:2 * P], b_wide[half, ct], both, start=True, stop=True)
                    mm(bank[5 + h % 2][:, 2 * P:4 * P], k_wide[half, ct], both, start=True, stop=True)\
                        .then_inc(S["am_done"], 1)

            def turn(n, which):
                ar = ar_of(n.par)
                sources = (lambda ct: ar[:, ct, 0], lambda ct: k_wide[:, ct], lambda ct: b_wide[:, ct],
                           lambda ct: vt[:, ct])
                for m in which:
                    if m == 3:
                        hold("v_loaded", (n.s + 1) * 16)
                    for ct in range(CT):
                        ins = nc.tensor.transpose(bank[m][:, ct * P:(ct + 1) * P], sources[m](ct), cst.ident)
                    ins.then_inc(S["turned"], 1)

            def start(n):
                am_products(n, range(HEADS))
                turn(n, range(4))

            def tile(t, n):
                s, am, ar = t.s, am_of(t.par), ar_of(t.par)
                _, k_tall, b_tall, v_tall = tall_of(t.par)
                pairs = [divmod(h, 2) + (h,) for h in range(HEADS)]

                def between_products(l, place):
                    if l == 1 and place != 1:
                        for h in range(2 * place, 2 * place + 4):
                            ins = mm(bank[4][:, h * HD:(h + 1) * HD], am[:, h, 2], v_tall[:, h * HD:(h + 1) * HD],
                                     start=True, stop=True)
                        if place:
                            ins.then_inc(S["y_done"], 1)
                    if (l, place) == (2, 0):
                        if not t.very_first:
                            hold("o_ready", s)
                        for ct, e, h in pairs:
                            mm(bank[7][64 * e:64 * e + 64, ct * P:(ct + 1) * P], v_tall[:, h * HD:(h + 1) * HD],
                               am[:, h, 3], start=(ct == 0), stop=False, skip_group_check=True)
                    if n:
                        am_products(n, AM_AT.get((l, place), ()))
                hold("tall_ready", s * 4 + 4)
                if not t.very_first:
                    hold("z_ready", s * 2)
                for l in range(1, LEVELS):
                    for g in range(2):
                        kit.hold(pe, G2["v_ready"][g], s * 6 + l)
                        for q in range(4):
                            ins = nc.tensor.transpose(bank[2 * g][:, q * P:(q + 1) * P], v_inv[:, g, q], cst.ident)
                        ins.then_inc(G2["w_done"][g], 1)
                    between_products(l, 0)
                    for g in range(2):
                        kit.hold(pe, G2["level_ready"][g], s * 6 + (l + 1))
                        kit.hold(pe, G2["w_ready"][g], s * 5 + l)
                        for q in range(4):
                            ins = mm(bank[2 * g][:, q * P:(q + 1) * P], level[:, g, l % 2, q], w_inv[:, g, q],
                                     start=True, stop=True)
                        ins.then_inc(G2["p_done"][g], 1)
                    between_products(l, 1)
                    for g in range(2):
                        kit.hold(pe, G2["p_ready"][g], s * 5 + l)
                        for q in range(4):
                            ins = mm(bank[2 * g + 1][:, q * P:(q + 1) * P], prod[:, g, q], v_inv[:, g, q],
                                     start=True, stop=True)
                        ins.then_inc(G2["v_done"][g], 1)
                    between_products(l, 2)
                hold("y_ready", s + 1)
                if n:
                    hold("am_ready", n.s * 8 + 7)
                for g in range(2):
                    kit.hold(pe, G2["v_ready"][g], s * 6 + 6)
                for h in range(HEADS):
                    ins = mm(bank[5][:, h * HD:(h + 1) * HD], v_inv[:, h // 4, h % 4], y_tall[:, h * HD:(h + 1) * HD],
                             start=True, stop=True)
                ins.then_inc(S["wy_done"], 1)
                if n:
                    hold("am_ready", n.s * 8 + 8)
                for ct, e, h in pairs:
                    ins = mm(bank[6][64 * e:64 * e + 64, ct * P:(ct + 1) * P], a_tall[:, h * HD:(h + 1) * HD],
                             v_inv[:, h // 4, h % 4], start=True, stop=True)
                ins.then_inc(S["wa_done"], 1)
                if n:
                    turn(n, (0, 1))
                hold("wy_ready", s + 1)
                hold("wa_ready", s + 1)
                if not t.first:
                    hold("state_loaded", 16 * (t.d + 1))
                for k, c in enumerate((0, 1) if t.d == 0 else (1, 0)):
                    m = s * 2 + k
                    rows = slice(CK * c, CK * c + CK)
                    if k:
                        if n:
                            turn(n, (2, 3))
                        hold("z_ready", m)
                    for ct, e, h in pairs:
                        half = slice(64 * e, 64 * e + 64)
                        ins = mm(bank[4 + e][rows, ct * HD:(ct + 1) * HD], wa[half, ct, rows], z[half, ct],
                                 start=True, stop=True)
                    ins.then_inc(S["u_done"], 1)
                    for ct, e, h in pairs:
                        half = slice(64 * e, 64 * e + 64)
                        mm(bank[7][half, ct * P + CK * c:ct * P + CK * c + CK], z[half, ct], ar[half, ct, 1, rows],
                           start=False, stop=False, skip_group_check=True)
                    for ct, e, h in pairs:
                        mm(bank[6][64 * e:64 * e + 64, ct * HD:(ct + 1) * HD], k_tall[rows, h * HD:(h + 1) * HD],
                           v_tall[rows, h * HD:(h + 1) * HD], start=(ct == 0), stop=False, skip_group_check=True)
                    hold("u_ready", (m + 1) * 2)
                    for ct, e, h in pairs:
                        ins = mm(bank[6][64 * e:64 * e + 64, ct * HD:(ct + 1) * HD], b_tall[rows, h * HD:(h + 1) * HD],
                                 u_tall[rows, h * HD:(h + 1) * HD], start=False, stop=True, skip_group_check=True)
                    ins.then_inc(S["z_done"], 1)
                for ct, e, h in pairs:
                    ins = mm(bank[7][64 * e:64 * e + 64, ct * P:(ct + 1) * P], u_tall[:, h * HD:(h + 1) * HD], am[:, h, 1],
                             start=False, stop=True, skip_group_check=True)
                ins.then_inc(S["o_done"], 1)
            tile_schedule(pe, head, start, tile, nothing)


def head_norm(kit, cst, mix, o, kd_sum, o_hi, o_lo, fourier_inputs):
    nc = kit.nc
    s = {q: kit.sem("hn_" + q) for q in (
        "loaded", "mean_done", "centered", "rk_ready", "squared", "var_done", "rooted", "inverted", "scaled",
        "affine", "bonus_done", "bonus_v", "with_bonus", "gate_done", "gated", "hi_ready", "lo_ready",
        "f_in")}
    r_loaded, v_loaded = ([kit.sem(f"hn_{q}_loaded{ct}") for ct in range(CT)] for q in "rv")
    with ExitStack() as ctx:
        buf = lambda name, shape, dt=F32: ctx.enter_context(nc.sbuf_tensor(name, shape, dt))
        r, v = buf("hn_r", [P, CT, T]), buf("hn_v", [P, CT, T])
        gd, g_up = buf("hn_gd", [P, T]), buf("hn_g_up", [P, W])
        block = ctx.enter_context(nc.Block())
        steps = CT * NC
        ct_of, part = (lambda m: m // NC), (lambda m: slice(m % NC * CH, m % NC * CH + CH))
        at = lambda a, m: a[:, ct_of(m), part(m)]
        bank = lambda m, q: kit.banks[4 * (m % 2) + q][:, 0:CH]

        def skewed(stages):
            for t in range(steps + max(lag for lag, _ in stages)):
                for lag, piece in stages:
                    if 0 <= t - lag < steps:
                        piece(t - lag)

        @block.sync
        def _(sp):
            for ct in range(CT):
                sp.dma_start(r[:, ct], mix[ct]).then_inc(r_loaded[ct], 16)
                if ct == 0:
                    sp.dma_start(g_up[:], kit.dram["g_up"]).then_inc(s["loaded"], 16)
                    sp.dma_start(gd[:], mix[J_GD]).then_inc(s["loaded"], 16)
                sp.dma_start(v[:, ct], mix[2 * CT + ct]).then_inc(v_loaded[ct], 16)
            f, cs, dft_ctx = fourier_inputs
            sp.dma_start(cs[:], kit.dram["dft_features"]).then_inc(s["f_in"], 16)
            sp.dma_start(dft_ctx[:], kit.dram["dft_context"]).then_inc(s["f_in"], 16)
            sp.dma_start(f[:], mix[J_F:J_GATE].rearrange("c p t -> p c t")).then_inc(s["f_in"], 16)
            sp.wait_ge(s["f_in"], 48)

        @block.tensor
        def _(pe):
            def sums(m):
                if m >= 2:
                    pe.wait_ge(s["centered"], m - 1)
                nc.tensor.matmul(bank(m, 0), cst.pair_ones, at(o, m), start=True, stop=True).then_inc(s["mean_done"], 1)

            def gate(m):
                if m >= 2:
                    pe.wait_ge(s["gated"], m - 1)
                elif m == 0:
                    pe.wait_ge(s["loaded"], 32)
                nc.tensor.matmul(bank(m, 3), g_up[:, ct_of(m) * P:(ct_of(m) + 1) * P], gd[:, part(m)],
                                 start=True, stop=True).then_inc(s["gate_done"], 1)

            def bonus(m):
                pe.wait_ge(s["rk_ready"], m + 1)
                if m >= 2:
                    pe.wait_ge(s["bonus_v"], m - 1)
                nc.tensor.matmul(bank(m, 2), cst.pair_ones, at(kd_sum, m), start=True, stop=True)\
                    .then_inc(s["bonus_done"], 1)

            def variance(m):
                pe.wait_ge(s["squared"], m + 1)
                if m >= 2:
                    pe.wait_ge(s["rooted"], m - 1)
                nc.tensor.matmul(bank(m, 1), cst.pair_ones, at(r, m), start=True, stop=True).then_inc(s["var_done"], 1)
            skewed([(0, sums), (0, bonus), (0, variance), (1, gate)])

        @block.scalar
        def _(act):
            def square(m):
                act.wait_ge(s["centered"], m + 1)
                act.wait_ge(s["rk_ready"], m + 1)
                nc.scalar.activation(at(r, m), at(o, m), ACT.Square).then_inc(s["squared"], 1)

            def root(m):
                act.wait_ge(s["var_done"], m + 1)
                nc.scalar.activation(at(r, m), bank(m, 1), ACT.Sqrt, scale=1.0 / HD, bias=kit.eps[:, 1:2])\
                    .then_inc(s["rooted"], 1)

            def affine(m):
                act.wait_ge(s["scaled"], m + 1)
                nc.scalar.activation(at(r, m), at(o, m), ACT.Identity, scale=kit.col("lnx_w", ct_of(m)),
                                     bias=kit.col("lnx_b", ct_of(m))).then_inc(s["affine"], 1)

            def high(m):
                act.wait_ge(s["gated"], m + 1)
                nc.scalar.activation(at(o_hi, m), at(o, m), ACT.Copy).then_inc(s["hi_ready"], 1)
            skewed([(0, square), (0, root), (1, affine), (2, high)])

        @block.vector
        def _(dve):
            def center(m):
                dve.wait_ge(s["mean_done"], m + 1)
                nc.vector.scalar_tensor_tensor(at(o, m), bank(m, 0), -1.0 / HD, at(o, m), ALU.mult, ALU.add)\
                    .then_inc(s["centered"], 1)
                dve.wait_ge(r_loaded[ct_of(m)], 16)
                nc.vector.scalar_tensor_tensor(at(kd_sum, m), at(r, m), kit.col("r_k", ct_of(m)), at(kd_sum, m),
                                               ALU.mult, ALU.mult).then_inc(s["rk_ready"], 1)

            def normed(m):
                dve.wait_ge(s["rooted"], m + 1)
                nc.vector.reciprocal(at(kd_sum, m), at(r, m)).then_inc(s["inverted"], 1)
                dve.wait_ge(s["inverted"], m + 1)
                nc.vector.tensor_tensor(at(o, m), at(o, m), at(kd_sum, m), ALU.mult).then_inc(s["scaled"], 1)

            def bonus(m):
                dve.wait_ge(s["bonus_done"], m + 1)
                dve.wait_ge(v_loaded[ct_of(m)], 16)
                nc.vector.tensor_tensor(at(v, m), bank(m, 2), at(v, m), ALU.mult).then_inc(s["bonus_v"], 1)

            def gated(m):
                dve.wait_ge(s["with_bonus"], m + 1)
                dve.wait_ge(s["gate_done"], m + 1)
                nc.vector.tensor_tensor(at(o, m), bank(m, 3), at(v, m), ALU.mult).then_inc(s["gated"], 1)
            skewed([(0, center), (1, bonus), (1, normed), (2, gated)])
            dve.wait_ge(s["lo_ready"], steps)

        @block.gpsimd
        def _(pool):
            def with_bonus(m):
                pool.wait_ge(s["affine"], m + 1)
                pool.wait_ge(s["bonus_v"], m + 1)
                nc.gpsimd.tensor_tensor(at(v, m), at(v, m), at(r, m), ALU.add).then_inc(s["with_bonus"], 1)

            def low(m):
                pool.wait_ge(s["hi_ready"], m + 1)
                nc.gpsimd.tensor_tensor(at(o_lo, m), at(o, m), at(o_hi, m).bitcast(F32), ALU.subtract)\
                    .then_inc(s["lo_ready"], 1)
            skewed([(0, with_bonus), (1, low)])


def fourier_buffers(kit, ctx):
    return [ctx.enter_context(kit.nc.sbuf_tensor(name, shape, F32)) for name, shape in (
        ("fo_f", [P, FG, T]), ("fo_cs", [P, 2 * FD]), ("fo_dft_ctx", [P, 2, T_CTX]))]


def fourier(kit, inputs, f_hi, f_lo):
    nc = kit.nc
    s = {q: kit.sem("fo_" + q) for q in (
        "g_done", "g_ready", "ctx_done", "ctx_hi", "ctx_lo", "g_hi_ready", "g_lo_ready",
        "dft_hi_ready", "dft_ready", "unit_done", "hi_ready", "lo_ready")}
    dft_loaded = [kit.sem(f"fo_dft_loaded{p}") for p in range(2)]
    LT = NTT - 1
    with ExitStack() as ctx:
        buf = lambda name, shape, dt=F32: ctx.enter_context(nc.sbuf_tensor(name, shape, dt))
        f, cs, dft_ctx = inputs
        g = buf("fo_g", [P, NTT, 2, FG, FD])
        raw = buf("fo_raw", [P, 2, T_LAT])
        dft_hi, dft_lo = buf("fo_dft_hi", [P, 2, T_LAT], F32R), buf("fo_dft_lo", [P, 2, T_LAT], F32R)
        g_hi, g_lo = buf("fo_g_hi", [P, 2, FG, FD], F32R), buf("fo_g_lo", [P, 2, FG, FD], F32R)
        block = ctx.enter_context(nc.Block())
        bank = kit.banks

        @block.sync
        def _(sp):
            def load(tt, first=False):
                for p in range(2):
                    if not first:
                        kit.hold(sp, s["dft_ready"], tt * 2 + (p - 1))
                    sp.dma_start(raw[:, p], kit.dram["dft_latents"][tt, p]).then_inc(dft_loaded[p], 16)
            load(0, True)
            with sp.Fori(1, LT) as tt:
                load(tt)

        @block.tensor
        def _(pe):
            for m in range(2 * NTT):
                tt, pair = divmod(m, 2)
                if m >= 8:
                    pe.wait_ge(s["g_ready"], m - 7)
                for q in range(2):
                    ins = nc.tensor.matmul(bank[m % 8][:, q * 2 * FD:(q + 1) * 2 * FD],
                                           f[:, 2 * pair + q, tt * P:(tt + 1) * P], cs[:], start=True, stop=True)
                ins.then_inc(s["g_done"], 1)
            pe.wait_ge(s["g_ready"], 2 * NTT)
            for q in range(FG):
                for p in range(2):
                    ins = nc.tensor.matmul(bank[0][:, q * P:(q + 1) * P], g[:, 0, p, q], dft_ctx[:, p],
                                           start=(p == 0), stop=(p == 1))
            ins.then_inc(s["ctx_done"], 1)
            pe.wait_ge(s["ctx_lo"], 1)

            def units(tt, early=False, late=False):
                for p in range(2):
                    pe.wait_ge(s["g_lo_ready"], tt * 2 + (p + 1))
                    pe.wait_ge(s["dft_ready"], tt * 2 + (p + 1))
                    for q in range(FG):
                        for half in range(2):
                            cols = slice(half * 512, half * 512 + 512)
                            for m, (w, v) in enumerate(((g_lo, dft_hi), (g_hi, dft_lo), (g_hi, dft_hi))):
                                ins = nc.tensor.matmul(bank[2 * q + half][:], w[:, p, q], v[:, p, cols],
                                                       start=(early and p == 0 and m == 0),
                                                       stop=(late and p == 1 and m == 2), skip_group_check=True)
                    ins.then_inc(s["unit_done"], 1)
            units(0, early=True)
            with pe.Fori(1, LT - 1) as tt:
                units(tt)
            units(LT - 1, late=True)

        @block.scalar
        def _(act):
            for m in range(2 * NTT):
                tt, pair = divmod(m, 2)
                act.wait_ge(s["g_done"], m + 1)
                for q in range(2):
                    ins = nc.scalar.activation(g[:, tt, :, 2 * pair + q], bank[m % 8][:, q * 2 * FD:(q + 1) * 2 * FD]
                                               .rearrange("p (a t) -> p a t", a=2), ACT.Copy)
                ins.then_inc(s["g_ready"], 1)
            act.wait_ge(s["ctx_done"], 1)
            nc.scalar.activation(f_hi[:, :, 0:T_CTX], bank[0][:].rearrange("p (g t) -> p g t", g=FG), ACT.Copy)\
                .then_inc(s["ctx_hi"], 1)
            act.wait_ge(s["g_ready"], 2 * NTT)

            def split(tt, first=False):
                for p in range(2):
                    if not first:
                        kit.hold(act, s["unit_done"], tt * 2 + (p - 1))
                    tile = g[:, bass.ds(tt + 1, 1), p]
                    nc.scalar.activation(g_hi[:, p:p + 1], tile, ACT.Copy).then_inc(s["g_hi_ready"], 1)
                    act.wait_ge(dft_loaded[p], (tt + 1) * 16)
                    nc.scalar.activation(dft_hi[:, p], raw[:, p], ACT.Copy).then_inc(s["dft_hi_ready"], 1)
            split(0, True)
            with act.Fori(1, LT) as tt:
                split(tt)
            act.wait_ge(s["unit_done"], 2 * LT)
            for q in range(FG):
                for half in range(2):
                    cols = slice(T_CTX + half * 512, T_CTX + half * 512 + 512)
                    nc.scalar.activation(f_hi[:, q, cols], bank[2 * q + half][:], ACT.Copy).then_inc(s["hi_ready"], 1)

        @block.vector
        def _(dve):
            dve.wait_ge(s["ctx_hi"], 1)
            nc.vector.tensor_tensor(f_lo[:, :, 0:T_CTX], bank[0][:].rearrange("p (g t) -> p g t", g=FG),
                                    f_hi[:, :, 0:T_CTX].bitcast(F32), ALU.subtract).then_inc(s["ctx_lo"], 1)

            def split(tt):
                for p in range(2):
                    dve.wait_ge(s["g_hi_ready"], tt * 2 + (p + 1))
                    nc.vector.tensor_tensor(g_lo[:, p:p + 1], g[:, bass.ds(tt + 1, 1), p], g_hi[:, p:p + 1].bitcast(F32),
                                            ALU.subtract).then_inc(s["g_lo_ready"], 1)
                    dve.wait_ge(s["dft_hi_ready"], tt * 2 + (p + 1))
                    nc.vector.tensor_tensor(dft_lo[:, p], raw[:, p], dft_hi[:, p].bitcast(F32),
                                            ALU.subtract).then_inc(s["dft_ready"], 1)
            split(0)
            with dve.Fori(1, LT) as tt:
                split(tt)
            for m in range(2 * FG):
                q, half = divmod(m, 2)
                cols = slice(T_CTX + half * 512, T_CTX + half * 512 + 512)
                dve.wait_ge(s["hi_ready"], m + 1)
                nc.vector.tensor_tensor(f_lo[:, q, cols], bank[m][:], f_hi[:, q, cols].bitcast(F32),
                                        ALU.subtract).then_inc(s["lo_ready"], 1)
            dve.wait_ge(s["lo_ready"], 2 * FG)


class Merge:

    on_pool = True

    def __init__(self, kit, mix):
        self.kit, self.nc, self.mix = kit, kit.nc, mix
        self.loaded, self.left, self.right = kit.sem("gates_loaded"), kit.sem("gated_a"), kit.sem("gated_b")

    def setup(self, ctx):
        self.gates = ctx.enter_context(self.nc.sbuf_tensor("gates", [P, 2, T], F32))
        self.parts = ctx.enter_context(self.nc.sbuf_tensor("gated_parts", [P, 2, CH], F32))

    def load(self, sp, f, first, g32_ready):
        if not first:
            self.kit.hold(sp, g32_ready, f * 3)
        for b in range(2):
            sp.dma_start(self.gates[:, b], self.mix[f + (J_GATE + KT * b)]).then_inc(self.loaded, 16)

    def scalar(self, act, a, out):
        return self.nc.scalar.activation(out, a, ACT.Copy)

    def vector(self, dve, f, n, c, b, act_out, g32, g32_ready):
        if c == 0:
            dve.wait_ge(self.loaded, (f + 1) * 32)
        if not (isinstance(n, int) and n == 0):
            dve.wait_ge(g32_ready, n)
        self.nc.vector.tensor_tensor(self.parts[:, 1], b, self.gates[:, 1, c * CH:(c + 1) * CH],
                                     ALU.mult).then_inc(self.right, 1)

    def pool(self, pool, f, n, c, act_out, g32, g32_ready):
        if c == 0:
            pool.wait_ge(self.loaded, (f + 1) * 32)
        if not (isinstance(n, int) and n == 0):
            pool.wait_ge(g32_ready, n)
        self.nc.gpsimd.tensor_tensor(self.parts[:, 0], act_out, self.gates[:, 0, c * CH:(c + 1) * CH],
                                     ALU.mult).then_inc(self.left, 1)
        pool.wait_ge(self.left, n + 1)
        pool.wait_ge(self.right, n + 1)
        self.nc.gpsimd.tensor_tensor(g32, self.parts[:, 0], self.parts[:, 1], ALU.add).then_inc(g32_ready, 1)


def merge(kit, mix, halves, x_saved):
    def load_x(sp, loaded):
        for k in range(KT):
            sp.dma_start(kit.x[:, k], x_saved[k]).then_inc(loaded, 16)
    hidden_stage(kit, "merge", KT, CT, (kit.dram["w_rwkv"], kit.dram["w_fourier"]), kit.dram["w_out"],
                 None, halves, Merge(kit, mix), 1, load_x)


def final_norm(kit, out):
    nc = kit.nc
    s = {q: kit.sem("fn_" + q) for q in ("squared", "summed", "rooted", "inverted", "scaled", "stored")}
    with ExitStack() as ctx:
        buf = lambda name, shape: ctx.enter_context(nc.sbuf_tensor(name, shape, F32))
        sq, inv, y = buf("fn_square", [P, 2, CH]), buf("fn_inv", [P, 2, NC, CH]), buf("fn_y", [P, KT, T])
        block = ctx.enter_context(nc.Block())
        at = lambda a, k, c: a[:, k, c * CH:(c + 1) * CH]

        @block.scalar
        def _(act):
            for m in range(NC * KT):
                c, k = divmod(m, KT)
                if m >= 2:
                    act.wait_ge(s["summed"], m - 1)
                nc.scalar.activation(sq[:, m % 2], at(kit.x, k, c), ACT.Square).then_inc(s["squared"], 1)
                if k == KT - 1:
                    act.wait_ge(s["summed"], m + 1)
                    nc.scalar.activation(inv[:, 0, c], kit.banks[c][:, 0:CH], ACT.Sqrt, scale=1.0 / D,
                                         bias=kit.eps[:, 0:1]).then_inc(s["rooted"], 1)

        @block.tensor
        def _(pe):
            for m in range(NC * KT):
                c, k = divmod(m, KT)
                pe.wait_ge(s["squared"], m + 1)
                nc.tensor.matmul(kit.banks[c][:, 0:CH], kit.ones[:], sq[:, m % 2], start=(k == 0),
                                 stop=(k == KT - 1)).then_inc(s["summed"], 1)

        @block.vector
        def _(dve):
            for c in range(NC):
                dve.wait_ge(s["rooted"], c + 1)
                nc.vector.reciprocal(inv[:, 1, c], inv[:, 0, c]).then_inc(s["inverted"], 1)
                dve.wait_ge(s["inverted"], c + 1)
                for k in range(KT):
                    nc.vector.scalar_tensor_tensor(at(y, k, c), at(kit.x, k, c), kit.col("final_norm", k), inv[:, 1, c],
                                                   ALU.mult, ALU.mult).then_inc(s["scaled"], 1)

        @block.sync
        def _(sp):
            for m in range(NC * KT):
                c, k = divmod(m, KT)
                sp.wait_ge(s["scaled"], m + 1)
                sp.dma_start(out[k][:, c * CH:(c + 1) * CH], at(y, k, c)).then_inc(s["stored"], 16)
            sp.wait_ge(s["stored"], 16 * NC * KT)


def program(nc, dram, y_out, states_out):
    scratch = lambda name, shape, dt=F32: nc.dram_tensor(name, shape, dt).ap()
    mix, keys = scratch("mix", (J_END, P, T)), scratch("keys", (CT, P, T))
    x_saved = scratch("x_saved", (KT, P, T))
    with ExitStack() as ctx:
        kit = Kit(nc, ctx, dram)
        with kit.stage():
            modulation(kit)
        with kit.stage():
            ffn(kit, "ffn1", 0, "ffn1_w13", "ffn1_w2")
        with ExitStack() as mixer:
            cst = Constants(kit, mixer)
            with kit.stage():
                projection(kit, mix, x_saved, keys, cst)
            o, kd_sum = kit.x[:, 0:CT], kit.x[:, CT:KT]
            with kit.stage():
                scans(kit, cst, mix, keys, o, kd_sum, dram["states"], states_out)
            halves = [[mixer.enter_context(nc.sbuf_tensor(f"{branch}_{q}", [P, CT, T], F32R)) for q in ("hi", "lo")]
                      for branch in ("rwkv", "fourier")]
            with ExitStack() as ctx_fourier:
                fourier_inputs = fourier_buffers(kit, ctx_fourier)
                with kit.stage():
                    head_norm(kit, cst, mix, o, kd_sum, *halves[0], fourier_inputs)
                with kit.stage():
                    fourier(kit, fourier_inputs, *halves[1])
            with kit.stage():
                merge(kit, mix, halves, x_saved)
        with kit.stage():
            ffn(kit, "ffn2", 2, "ffn2_w13", "ffn2_w2")
        with kit.stage():
            final_norm(kit, y_out)


def mask_array():
    s, t = np.arange(P)[:, None], np.arange(P)[None, :]
    out = np.zeros((P, 2, 8, P), np.float32)
    for d in range(2):
        strict = (s // CK == t // CK) & ((s < t) if d == 0 else (s > t))
        out[:, d, 0], out[:, d, 1] = strict, strict | (s == t)
        for l in range(6):
            m = 1 << l
            out[:, d, 2 + l] = strict & (s // (2 * m) == t // (2 * m)) & (s // m != t // m)
    return out


def reset_array():
    return np.broadcast_to((np.arange(T) % CK != 0).astype(np.float32), (P, T))


def dft_arrays():
    def parts(angle, n, sign):
        return np.stack([np.cos(angle), sign * np.sin(angle)], 1).astype(np.float64) / np.sqrt(n)
    j = np.arange(FD)
    features = parts(2 * np.pi * (np.outer(j, j) % FD) / FD, FD, 1).reshape(FD, 2 * FD)
    t = np.arange(T_CTX)
    context = parts(2 * np.pi * (np.outer(t, t) % T_CTX) / T_CTX, T_CTX, -1)
    wide, rows = 64, T_LAT // 64
    r, c = np.divmod(np.arange(T_LAT), wide)
    turns = (np.outer(r, r) % rows) / rows + (np.outer(c, c) % wide) / wide
    latents = parts(2 * np.pi * turns, T_LAT, -1).reshape(T_LAT // P, P, 2, T_LAT).transpose(0, 2, 1, 3)
    return [a.astype(np.float32) for a in (features, context, latents)]


def up_tiles(w, n):
    k = w.shape[0] // P
    return w.reshape(k, P, n, P).transpose(2, 1, 0, 3).reshape(n, P, k * P)


def kernel(x_prompt, x_sample, state_rwkv_fwd, state_rwkv_bwd, c, c_ctx, ada_w, ada_b, norm_w, ffn1_w13, ffn1_w2,
           ffn2_w13, ffn2_w2, w_in, gate_b, conv_rkv, w0, w_up, a0, a_up, g_up, k_k, k_a, r_k, lnx_w, lnx_b,
           w_o_rwkv, w_fourier, w_out, final_norm):
    import concourse.bacc as bacc
    from concourse.bass_utils import run_bass_kernel_spmd

    a = np.asarray
    vectors = dict(ada_b=ada_b, norm_w=norm_w, final_norm=final_norm, gate_b=gate_b, conv=conv_rkv, w0=w0, a0=a0,
                   k_k=k_k, k_a=k_a, r_k=r_k, lnx_w=lnx_w, lnx_b=lnx_b)
    rows = [a(vectors[n]).reshape(-1, P) for n in PACK if n != "c"] + [a(c_ctx).reshape(-1, P), a(c).reshape(-1, P)]
    features, context, latents = dft_arrays()
    pair_ones = np.kron(np.eye(2, dtype=np.float32), np.ones((HD, HD), np.float32))

    def w13(w):
        w = a(w)[0]
        return np.stack([up_tiles(w[:, :F_TILES * P], F_TILES), up_tiles(w[:, F_TILES * P:], F_TILES)])

    def states(s):
        return a(s).reshape(CT, 2, HD, HD).transpose(1, 3, 0, 2).reshape(P, CT, HD)
    arrays = {
        "vec": np.concatenate(rows, 0).T,
        "xT": np.concatenate([a(x_prompt)[0], a(x_sample)[0]], 0).T.reshape(KT, P, T),
        "ada_w": a(ada_w)[0].reshape(4, 2, P, 9, D).transpose(3, 0, 2, 1, 4),
        "select": np.equal(np.arange(P)[:, None] % 32, np.arange(2)).astype(np.float32),
        "ffn1_w13": w13(ffn1_w13), "ffn1_w2": a(ffn1_w2)[0].reshape(F_TILES, P, D),
        "ffn2_w13": w13(ffn2_w13), "ffn2_w2": a(ffn2_w2)[0].reshape(F_TILES, P, D),
        "w_in": up_tiles(a(w_in)[0], J_END),
        "lora_up": np.concatenate([a(w_up)[0], a(a_up)[0]], 1).transpose(1, 0, 2),
        "g_up": a(g_up)[0], "states": np.stack([states(state_rwkv_fwd), states(state_rwkv_bwd)]),
        "w_rwkv": up_tiles(a(w_o_rwkv)[0], KT), "w_fourier": up_tiles(a(w_fourier)[0], KT),
        "w_out": a(w_out)[0].reshape(KT, P, D),
        "masks": mask_array(), "reset": reset_array(), "squares": np.stack([np.eye(P, dtype=np.float32), pair_ones], 1),
        "dft_features": features, "dft_context": context, "dft_latents": latents,
    }
    arrays = {n: np.ascontiguousarray(v) for n, v in arrays.items()}
    nc = bacc.Bacc("TRN2", target_bir_lowering=False, num_devices=1)
    dram = {n: nc.dram_tensor("in_" + n, v.shape, F32, kind="ExternalInput").ap() for n, v in arrays.items()}
    y_out = nc.dram_tensor("out_y", (KT, P, T), F32, kind="ExternalOutput").ap()
    s_out = nc.dram_tensor("out_states", (2, P, CT, HD), F32, kind="ExternalOutput").ap()
    program(nc, dram, y_out, s_out)
    got = run_bass_kernel_spmd(nc, [{"in_" + n: v for n, v in arrays.items()}], core_ids=[0]).results[0]
    y = got["out_y"].reshape(D, T).T
    s = got["out_states"].reshape(2, 2, HD, CT, HD).transpose(0, 3, 1, 4, 2).reshape(2, 1, 1, HEADS, HD, HD)
    return (np.ascontiguousarray(y[None, :T_CTX]), np.ascontiguousarray(y[None, T_CTX:]),
            np.ascontiguousarray(s[0]), np.ascontiguousarray(s[1]))
```
